# Optimizing a Trainium2 kernel written in Bass

```python
import math
import jax
import jax.numpy as jnp
from jax import lax
import numpy as np

D_MODEL = 1024
BATCH = 1
SEQ = 512
DEPTH = 2

GRID_W = 64
CTX_LEN = 256
NORM_EPS = 1e-6

SSM_HEADS = 16
SSM_HEAD_DIM = 64
SSM_INNER = SSM_HEADS * SSM_HEAD_DIM
SSM_STATE = 128
SSM_GROUPS = 2
SSM_GN = SSM_GROUPS * SSM_STATE
SSM_XBC = SSM_INNER + 2 * SSM_GN
SSM_PROJ = SSM_INNER + SSM_XBC + 2 * SSM_HEADS
SSM_CONV_W = 5
SSD_CHUNK = 128
DT_MIN = 0.001
DT_MAX = 0.1

NA_HEADS = 16
NA_HEAD_DIM = 64
NA_INNER = NA_HEADS * NA_HEAD_DIM
NA_ROWS = 8
NA_COLS = 16

AB_PROJ = SSM_PROJ + 3 * NA_INNER
AB_OUT = SSM_INNER + NA_INNER

GQA_HEADS = 16
GQA_KV_HEADS = 4
GQA_HEAD_DIM = 64
GQA_Q = GQA_HEADS * GQA_HEAD_DIM
GQA_KV = GQA_KV_HEADS * GQA_HEAD_DIM
GQA_PROJ = GQA_Q + 2 * GQA_KV
Q_BLOCK = 128
ROPE_THETA = 10000.0

N_EXPERTS = 32
N_GROUPS = 8
EXPERTS_PER_GROUP = N_EXPERTS // N_GROUPS
TOP_K = 2
D_EXPERT = 512
MOE_BLOCK = 128

kernel_name = "hybrid_ssd_natten_gqa_moe_prefix_dit"

def _rmsnorm(x, g):
    xf = x.astype(jnp.float32)
    y = xf * lax.rsqrt(jnp.mean(xf * xf, axis=-1, keepdims=True) + NORM_EPS)
    return (y * g.astype(jnp.float32)).astype(x.dtype)

def _attend(q, k, v):
    s = jnp.einsum('bqkgd,bskd->bkgqs', q, k).astype(jnp.float32) * (q.shape[-1] ** -0.5)
    p = jax.nn.softmax(s, axis=-1).astype(v.dtype)
    return jnp.einsum('bkgqs,bskd->bqkgd', p, v)

def _axial_rope_tables(n_tokens):
    t = jnp.arange(n_tokens)
    row = (t // GRID_W).astype(jnp.float32)
    col = (t % GRID_W).astype(jnp.float32)
    n_freq = GQA_HEAD_DIM // 4
    inv = ROPE_THETA ** (-jnp.arange(n_freq, dtype=jnp.float32) / n_freq)
    ang = jnp.concatenate([row[:, None] * inv, col[:, None] * inv], axis=-1)
    return jnp.cos(ang), jnp.sin(ang)

def _apply_rope(x, cos, sin):
    half = x.shape[-1] // 2
    shape = (1, x.shape[1]) + (1,) * (x.ndim - 3) + (half,)
    cs = cos.reshape(shape).astype(x.dtype)
    sn = sin.reshape(shape).astype(x.dtype)
    x1, x2 = x[..., :half], x[..., half:]
    return jnp.concatenate([x1 * cs - x2 * sn, x1 * sn + x2 * cs], axis=-1)

def _dwconv_centred(u, w, bias):
    ch = u.shape[-1]
    y = lax.conv_general_dilated(u, w[:, None, :].astype(u.dtype), window_strides=(1,),
                                 padding=[(SSM_CONV_W // 2, SSM_CONV_W // 2)],
                                 dimension_numbers=('NWC', 'WIO', 'NWC'), feature_group_count=ch)
    return y + bias.astype(u.dtype)

def _ssd_scan(x, dt, a, bm, cm, init_state):
    f32 = jnp.float32
    b, l, h, p = x.shape
    g, n = bm.shape[-2], bm.shape[-1]
    j = h // g
    L = SSD_CHUNK
    nc = l // L
    xd = (x.astype(f32) * dt[..., None]).reshape(b, nc, L, g, j, p)
    a_dt = jnp.transpose((dt * a).reshape(b, nc, L, g, j), (0, 3, 4, 1, 2))
    bc = bm.astype(f32).reshape(b, nc, L, g, n)
    cc = cm.astype(f32).reshape(b, nc, L, g, n)
    a_cum = jnp.cumsum(a_dt, axis=-1)
    tri = jnp.tril(jnp.ones((L, L), bool))
    decay = jnp.exp(jnp.where(tri, a_cum[..., :, None] - a_cum[..., None, :], -jnp.inf))
    cb = jnp.einsum('bclgn,bcsgn->bgcls', cc, bc)
    y_diag = jnp.einsum('bgjcls,bcsgjp->bclgjp', cb[:, :, None] * decay, xd)
    decay_states = jnp.exp(a_cum[..., -1:] - a_cum)
    states = jnp.einsum('bclgn,bgjcl,bclgjp->bcgjpn', bc, decay_states, xd)
    states = jnp.concatenate([init_state.astype(f32).reshape(b, 1, g, j, p, n), states], axis=1)
    chunk_cum = jnp.cumsum(jnp.pad(a_cum[..., -1], ((0, 0), (0, 0), (0, 0), (1, 0))), axis=-1)
    tri_c = jnp.tril(jnp.ones((nc + 1, nc + 1), bool))
    chunk_decay = jnp.exp(jnp.where(tri_c, chunk_cum[..., :, None] - chunk_cum[..., None, :], -jnp.inf))
    states = jnp.einsum('bgjzc,bcgjpn->bzgjpn', chunk_decay, states)
    y_off = jnp.einsum('bclgn,bcgjpn,bgjcl->bclgjp', cc, states[:, :-1], jnp.exp(a_cum))
    y = (y_diag + y_off).reshape(b, l, h, p)
    return y, states[:, -1].reshape(b, h, p, n)

def _ssd_branch(u, conv_w, conv_b, a_log, dt_bias, d_skip, norm_g, init_f, init_b):
    f32 = jnp.float32
    b, l, _ = u.shape
    z = u[..., :SSM_INNER]
    xbc = jax.nn.silu(_dwconv_centred(u[..., SSM_INNER:SSM_INNER + SSM_XBC], conv_w, conv_b))
    dt_raw = u[..., SSM_INNER + SSM_XBC:].astype(f32)
    xs = xbc[..., :SSM_INNER].reshape(b, l, SSM_HEADS, SSM_HEAD_DIM)
    bm = xbc[..., SSM_INNER:SSM_INNER + SSM_GN].reshape(b, l, SSM_GROUPS, SSM_STATE)
    cm = xbc[..., SSM_INNER + SSM_GN:].reshape(b, l, SSM_GROUPS, SSM_STATE)
    a = -jnp.exp(a_log.astype(f32))
    dtb = dt_bias.astype(f32)
    dt_f = jax.nn.softplus(dt_raw[..., :SSM_HEADS] + dtb[0])
    dt_b = jax.nn.softplus(dt_raw[..., SSM_HEADS:] + dtb[1])
    y_f, s_f = _ssd_scan(xs, dt_f, a[0], bm, cm, init_f)
    flip = lambda t: jnp.flip(t, axis=1)
    y_b, s_b = _ssd_scan(flip(xs), flip(dt_b), a[1], flip(bm), flip(cm), init_b)
    y = y_f + flip(y_b) + xs.astype(f32) * d_skip.astype(f32)[:, None]
    y = y.reshape(b, l, SSM_INNER) * jax.nn.silu(z.astype(f32))
    return _rmsnorm(y, norm_g).astype(u.dtype), s_f, s_b

def _neighbourhood_attention(q, k, v, k_ctx, v_ctx, rpb):
    b, n, h, d = q.shape
    rows = n // GRID_W
    wr = min(NA_ROWS, rows)
    nk = wr * GRID_W
    scale = d ** -0.5
    qg = jnp.moveaxis(q.reshape(b, rows, GRID_W, h, d), 1, 0)
    kg = k.reshape(b, rows, GRID_W, h, d)
    vg = v.reshape(b, rows, GRID_W, h, d)
    qcol = jnp.arange(GRID_W)
    cstart = jnp.clip(qcol - NA_COLS // 2, 0, GRID_W - NA_COLS)
    kcol = jnp.arange(GRID_W)
    col_ok = (kcol[None, :] >= cstart[:, None]) & (kcol[None, :] < cstart[:, None] + NA_COLS)
    col_ok = jnp.broadcast_to(col_ok[:, None, :], (GRID_W, wr, GRID_W)).reshape(GRID_W, nk)
    col_idx = jnp.clip(kcol[None, :] - qcol[:, None] + NA_COLS - 1, 0, 2 * NA_COLS - 2)

    def row_block(args):
        r, q_row = args
        rs = jnp.clip(r - wr // 2, 0, rows - wr)
        k_blk = lax.dynamic_slice_in_dim(kg, rs, wr, axis=1).reshape(b, nk, h, d)
        v_blk = lax.dynamic_slice_in_dim(vg, rs, wr, axis=1).reshape(b, nk, h, d)
        row_idx = rs + jnp.arange(wr) - r + NA_ROWS - 1
        bias = rpb[:, row_idx[:, None, None], col_idx[None, :, :]]
        bias = jnp.transpose(bias, (0, 2, 1, 3)).reshape(h, GRID_W, nk).astype(jnp.float32)
        s_lat = jnp.einsum('bqhd,bkhd->bhqk', q_row, k_blk).astype(jnp.float32) * scale + bias
        s_lat = jnp.where(col_ok, s_lat, -jnp.inf)
        s_ctx = jnp.einsum('bqhd,bchd->bhqc', q_row, k_ctx).astype(jnp.float32) * scale
        p = jax.nn.softmax(jnp.concatenate([s_lat, s_ctx], axis=-1), axis=-1).astype(v.dtype)
        return (jnp.einsum('bhqk,bkhd->bqhd', p[..., :nk], v_blk)
                + jnp.einsum('bhqc,bchd->bqhd', p[..., nk:], v_ctx))

    out = lax.map(row_block, (jnp.arange(rows), qg))
    return jnp.moveaxis(out, 0, 1).reshape(b, n, h, d)

def _mixer_ssd_na(xn, cn, w_in, w_out, conv_w, conv_b, a_log, dt_bias, d_skip, ssm_norm_g, rpb, need_ctx):
    b, n, _ = xn.shape
    lc = cn.shape[1]
    pl = xn @ w_in
    pc = cn @ w_in
    o1, o2 = SSM_PROJ + NA_INNER, SSM_PROJ + 2 * NA_INNER
    zeros = jnp.zeros((b, SSM_HEADS, SSM_HEAD_DIM, SSM_STATE), jnp.float32)
    y_c_ssd, s_f, s_b = _ssd_branch(pc[..., :SSM_PROJ], conv_w, conv_b, a_log, dt_bias, d_skip, ssm_norm_g, zeros, zeros)
    kc = pc[..., SSM_PROJ:o1].reshape(b, lc, NA_HEADS, NA_HEAD_DIM) if False else pc[..., o1:o2].reshape(b, lc, NA_HEADS, NA_HEAD_DIM)
    vc = pc[..., o2:].reshape(b, lc, NA_HEADS, NA_HEAD_DIM)
    y_ssd, _, _ = _ssd_branch(pl[..., :SSM_PROJ], conv_w, conv_b, a_log, dt_bias, d_skip, ssm_norm_g, s_f, s_b)
    q = pl[..., SSM_PROJ:o1].reshape(b, n, NA_HEADS, NA_HEAD_DIM)
    k = pl[..., o1:o2].reshape(b, n, NA_HEADS, NA_HEAD_DIM)
    v = pl[..., o2:].reshape(b, n, NA_HEADS, NA_HEAD_DIM)
    o_na = _neighbourhood_attention(q, k, v, kc, vc, rpb).reshape(b, n, NA_INNER)
    y = jnp.concatenate([y_ssd, o_na], axis=-1) @ w_out
    yc = None
    if need_ctx:
        qc = pc[..., SSM_PROJ:o1].reshape(b, lc, NA_HEADS, 1, NA_HEAD_DIM)
        o_c = _attend(qc, kc, vc).reshape(b, lc, NA_INNER)
        yc = jnp.concatenate([y_c_ssd, o_c], axis=-1) @ w_out
    return y, yc

def _mixer_gqa(xn, cn, w_in, w_out, q_g, k_g, cos, sin, need_ctx):
    b, n, _ = xn.shape
    lc = cn.shape[1]
    g = GQA_HEADS // GQA_KV_HEADS
    p = xn @ w_in
    q = _rmsnorm(p[..., :GQA_Q].reshape(b, n, GQA_KV_HEADS, g, GQA_HEAD_DIM), q_g)
    k = _rmsnorm(p[..., GQA_Q:GQA_Q + GQA_KV].reshape(b, n, GQA_KV_HEADS, GQA_HEAD_DIM), k_g)
    v = p[..., GQA_Q + GQA_KV:].reshape(b, n, GQA_KV_HEADS, GQA_HEAD_DIM)
    q = _apply_rope(q, cos, sin)
    k = _apply_rope(k, cos, sin)
    pkv = cn @ w_in[:, GQA_Q:]
    kc = _rmsnorm(pkv[..., :GQA_KV].reshape(b, lc, GQA_KV_HEADS, GQA_HEAD_DIM), k_g)
    vc = pkv[..., GQA_KV:].reshape(b, lc, GQA_KV_HEADS, GQA_HEAD_DIM)
    k_all = jnp.concatenate([k, kc], axis=1)
    v_all = jnp.concatenate([v, vc], axis=1)
    nb = n // Q_BLOCK
    qb = jnp.moveaxis(q.reshape(b, nb, Q_BLOCK, GQA_KV_HEADS, g, GQA_HEAD_DIM), 1, 0)
    o = lax.map(lambda qq: _attend(qq, k_all, v_all), qb)
    y = jnp.moveaxis(o, 0, 1).reshape(b, n, GQA_Q) @ w_out
    yc = None
    if need_ctx:
        qc = _rmsnorm((cn @ w_in[:, :GQA_Q]).reshape(b, lc, GQA_KV_HEADS, g, GQA_HEAD_DIM), q_g)
        yc = _attend(qc, kc, vc).reshape(b, lc, GQA_Q) @ w_out
    return y, yc

def _moe(xf, router_w, router_bias, w_gate, w_up, w_down):
    t, d = xf.shape
    s = jax.nn.sigmoid(jnp.dot(xf.astype(jnp.float32), router_w.astype(jnp.float32)))
    sb = (s + router_bias.astype(jnp.float32)).reshape(t, N_GROUPS, EXPERTS_PER_GROUP)
    grp = jnp.argmax(lax.top_k(sb, 2)[0].sum(-1), axis=-1)
    in_grp = jnp.take_along_axis(sb, grp[:, None, None], axis=1)[:, 0]
    _, loc = lax.top_k(in_grp, TOP_K)
    eidx = grp[:, None] * EXPERTS_PER_GROUP + loc
    wts = jnp.take_along_axis(s, eidx, axis=1)
    wts = wts / jnp.sum(wts, axis=-1, keepdims=True)
    m = t * TOP_K
    flat_e = eidx.reshape(-1)
    order = jnp.argsort(flat_e)
    e_sorted = flat_e[order]
    tok = order // TOP_K
    counts = jnp.bincount(flat_e, length=N_EXPERTS)
    padded = (counts + MOE_BLOCK - 1) // MOE_BLOCK * MOE_BLOCK
    pad_end = jnp.cumsum(padded)
    pad_start = pad_end - padded
    seg_start = jnp.cumsum(counts) - counts
    dest = pad_start[e_sorted] + jnp.arange(m) - seg_start[e_sorted]
    nb = -(-m // MOE_BLOCK) + N_EXPERTS
    slot_tok = jnp.full((nb * MOE_BLOCK,), t, jnp.int32).at[dest].set(tok.astype(jnp.int32))
    blk_e = jnp.minimum(jnp.searchsorted(pad_end, jnp.arange(nb) * MOE_BLOCK, side='right'), N_EXPERTS - 1)
    xpad = jnp.concatenate([xf, jnp.zeros((1, d), xf.dtype)], axis=0)
    xb = xpad[slot_tok].reshape(nb, MOE_BLOCK, d)

    def expert_block(args):
        xblk, e = args
        hid = jax.nn.silu(xblk @ w_gate[e]) * (xblk @ w_up[e])
        return hid @ w_down[e]

    yb = lax.map(expert_block, (xb, blk_e)).reshape(-1, d)
    y_sorted = yb[dest] * wts.reshape(-1)[order][:, None].astype(xf.dtype)
    return jnp.zeros_like(xf).at[tok].add(y_sorted)

def setup_inputs(seed: int = 0) -> dict:
    key = jax.random.key(seed)
    keys = jax.random.split(key, 32)
    counter = [0]
    f32 = jnp.float32

    def nk():
        kk = keys[counter[0]]
        counter[0] += 1
        return kk

    def nrm(shape, scale):
        return jax.random.normal(nk(), shape, f32) * scale

    n_ab = (DEPTH + 1) // 2
    n_c = DEPTH // 2
    x = nrm((BATCH, SEQ, D_MODEL), 1.0)
    c = nrm((BATCH, D_MODEL), 1.0)
    ctx = nrm((BATCH, CTX_LEN, D_MODEL), 1.0)
    c_ctx = nrm((D_MODEL,), 1.0)
    w_mod = nrm((DEPTH, D_MODEL, 6 * D_MODEL), 0.5 * D_MODEL ** -0.5)
    b_mod = nrm((DEPTH, 6 * D_MODEL), 0.01)
    norm1_g = 1.0 + nrm((DEPTH, D_MODEL), 0.01)
    norm2_g = 1.0 + nrm((DEPTH, D_MODEL), 0.01)
    final_g = 1.0 + nrm((D_MODEL,), 0.01)
    ab_w_in = nrm((n_ab, D_MODEL, AB_PROJ), D_MODEL ** -0.5)
    ab_w_out = nrm((n_ab, AB_OUT, D_MODEL), AB_OUT ** -0.5)
    ssm_conv_w = nrm((n_ab, SSM_CONV_W, SSM_XBC), SSM_CONV_W ** -0.5)
    ssm_conv_b = nrm((n_ab, SSM_XBC), 0.01)
    ssm_A_log = jnp.log(jax.random.uniform(nk(), (n_ab, 2, SSM_HEADS), f32, 1.0, 16.0))
    dt = jnp.exp(jax.random.uniform(nk(), (n_ab, 2, SSM_HEADS), f32)
                 * (math.log(DT_MAX) - math.log(DT_MIN)) + math.log(DT_MIN))
    ssm_dt_bias = dt + jnp.log(-jnp.expm1(-dt))
    ssm_D = 1.0 + nrm((n_ab, SSM_HEADS), 0.01)
    ssm_norm_g = 1.0 + nrm((n_ab, SSM_INNER), 0.01)
    na_rpb = nrm((n_ab, NA_HEADS, 2 * NA_ROWS - 1, 2 * NA_COLS - 1), 0.1)
    gqa_w_in = nrm((n_c, D_MODEL, GQA_PROJ), D_MODEL ** -0.5)
    gqa_w_out = nrm((n_c, GQA_Q, D_MODEL), GQA_Q ** -0.5)
    gqa_q_norm = 1.0 + nrm((n_c, GQA_HEAD_DIM), 0.01)
    gqa_k_norm = 1.0 + nrm((n_c, GQA_HEAD_DIM), 0.01)
    router_w = nrm((D_MODEL, N_EXPERTS), D_MODEL ** -0.5)
    router_bias = nrm((N_EXPERTS,), 0.01)
    moe_w_gate = nrm((DEPTH, N_EXPERTS, D_MODEL, D_EXPERT), D_MODEL ** -0.5)
    moe_w_up = nrm((DEPTH, N_EXPERTS, D_MODEL, D_EXPERT), D_MODEL ** -0.5)
    moe_w_down = nrm((DEPTH, N_EXPERTS, D_EXPERT, D_MODEL), D_EXPERT ** -0.5)
    return {"x": x, "c": c, "ctx": ctx, "c_ctx": c_ctx, "w_mod": w_mod, "b_mod": b_mod,
            "norm1_g": norm1_g, "norm2_g": norm2_g, "final_g": final_g,
            "ab_w_in": ab_w_in, "ab_w_out": ab_w_out, "ssm_conv_w": ssm_conv_w, "ssm_conv_b": ssm_conv_b,
            "ssm_A_log": ssm_A_log, "ssm_dt_bias": ssm_dt_bias, "ssm_D": ssm_D, "ssm_norm_g": ssm_norm_g,
            "na_rpb": na_rpb, "gqa_w_in": gqa_w_in, "gqa_w_out": gqa_w_out,
            "gqa_q_norm": gqa_q_norm, "gqa_k_norm": gqa_k_norm,
            "router_w": router_w, "router_bias": router_bias,
            "moe_w_gate": moe_w_gate, "moe_w_up": moe_w_up, "moe_w_down": moe_w_down}

def reference(x, c, ctx, c_ctx, w_mod, b_mod, norm1_g, norm2_g, final_g,
              ab_w_in, ab_w_out, ssm_conv_w, ssm_conv_b, ssm_A_log, ssm_dt_bias, ssm_D, ssm_norm_g,
              na_rpb, gqa_w_in, gqa_w_out, gqa_q_norm, gqa_k_norm,
              router_w, router_bias, moe_w_gate, moe_w_up, moe_w_down):
    b, n, _ = x.shape
    cos, sin = _axial_rope_tables(n)
    h = x
    hc = ctx
    for i in range(DEPTH):
        need_ctx = i < DEPTH - 1
        m = (jax.nn.silu(c) @ w_mod[i] + b_mod[i]).reshape(b, 6, D_MODEL)
        mc = (jax.nn.silu(c_ctx) @ w_mod[i] + b_mod[i]).reshape(6, D_MODEL)
        xn = _rmsnorm(h, norm1_g[i]) * (1 + m[:, 1, None]) + m[:, 0, None]
        cn = _rmsnorm(hc, norm1_g[i]) * (1 + mc[1]) + mc[0]
        j = i // 2
        if i % 2 == 0:
            y, yc = _mixer_ssd_na(xn, cn, ab_w_in[j], ab_w_out[j], ssm_conv_w[j], ssm_conv_b[j],
                                  ssm_A_log[j], ssm_dt_bias[j], ssm_D[j], ssm_norm_g[j], na_rpb[j], need_ctx)
        else:
            y, yc = _mixer_gqa(xn, cn, gqa_w_in[j], gqa_w_out[j], gqa_q_norm[j], gqa_k_norm[j],
                               cos, sin, need_ctx)
        h = h + m[:, 2, None] * y
        if need_ctx:
            hc = hc + mc[2] * yc
        xn2 = _rmsnorm(h, norm2_g[i]) * (1 + m[:, 4, None]) + m[:, 3, None]
        if need_ctx:
            cn2 = _rmsnorm(hc, norm2_g[i]) * (1 + mc[4]) + mc[3]
            toks = jnp.concatenate([xn2.reshape(-1, D_MODEL), cn2.reshape(-1, D_MODEL)], axis=0)
            f = _moe(toks, router_w, router_bias, moe_w_gate[i], moe_w_up[i], moe_w_down[i])
            h = h + m[:, 5, None] * f[:b * n].reshape(b, n, D_MODEL)
            hc = hc + mc[5] * f[b * n:].reshape(hc.shape)
        else:
            f = _moe(xn2.reshape(-1, D_MODEL), router_w, router_bias, moe_w_gate[i], moe_w_up[i], moe_w_down[i])
            h = h + m[:, 5, None] * f.reshape(b, n, D_MODEL)
    return _rmsnorm(h, final_g)


_drawn_inputs = setup_inputs


def setup_inputs(seed=0):
    import zlib

    import numpy as np

    out = dict(_drawn_inputs(seed))
    spreads = {}
    factors = {'final_g': 36.341,
     'ssm_conv_b': 3.362,
     'ssm_D': 24.9,
     'ssm_norm_g': 3.792,
     'na_rpb': 10.35,
     'gqa_q_norm': 21.794,
     'gqa_k_norm': 8.0}
    for name, (base, spread) in spreads.items():
        noise = np.random.default_rng([zlib.crc32(name.encode()), seed]).standard_normal(out[name].shape)
        drawn = base * np.exp(spread * noise) if base else spread * noise
        out[name] = jnp.asarray(drawn.astype(out[name].dtype))
    for name, factor in factors.items():
        out[name] = (out[name] * factor).astype(out[name].dtype)
    return out
```

```python
from contextlib import ExitStack, contextmanager

import concourse.bass as bass
from concourse import mybir

F32 = mybir.dt.float32
BF16 = mybir.dt.bfloat16
I32 = mybir.dt.int32
ALU = mybir.AluOpType
ACT = mybir.ActivationFunctionType
AX = mybir.AxisListType

P = 128
D = 1024
KD = D // P
N_LAT, N_CTX = 512, 256
LT, CT = N_LAT // P, N_CTX // P
NT = LT + CT
TOK = N_LAT + N_CTX
EPS = 1e-6
HEADS, HD = 16, 64
XBC = 1536
O_Z, O_XBC, O_DT, O_Q, O_K, O_V = 0, 1024, 2560, 2592, 3616, 4640
GRID = 64
NEG = -1.0e30
NE, NG, EPG, DE = 32, 8, 4, 512
CAP = TOK
BLK = 128
MOD = 6 * D

C_IDENT, C_ONES, C_TRIF, C_TRIB, C_TRIS, C_NEGF, C_NEGB = [i * P for i in range(7)]
C_NAMASK = 7 * P
C_TOKID = C_NAMASK + GRID
C_IOTA = C_TOKID + NT
C_EPS = C_IOTA + NE
C_COS = C_EPS + 1
C_SIN = C_COS + LT * HD // 2
C_END = C_SIN + LT * HD // 2


def latent_col(t):
    return t * P if t < LT else N_LAT + 4 + (t - LT) * P


CONV_W = N_LAT + 4 + N_CTX
RAW_W = CONV_W + 4


class Chain:

    def __init__(self, eng, sem):
        self.eng, self.sem, self.n = eng, sem, 0

    def __call__(self, ins):
        ins.then_inc(self.sem, 1)
        self.n += 1
        self.eng.wait_ge(self.sem, self.n)


class Kernel:
    def __init__(self, nc, ctx, io):
        self.nc, self.ctx, self.io = nc, ctx, io
        self.n_sems, self.stage_sems, self.old_sems = 0, [], []
        self.passed = nc.alloc_semaphore("loop_wait_passed")
        self.arena = ctx.enter_context(nc.sbuf_tensor("arena", [P, 52700], F32))
        self.ps = ctx.enter_context(nc.psum_tensor("ps", [P, 8, 512], F32))
        at = 0

        def region(n):
            nonlocal at
            ap = self.arena[:, at:at + n]
            at += n
            return ap

        self.h = region(NT * D).rearrange("p (t d) -> p t d", t=NT)
        self.big = region(40032)
        self.xt_r = self.big[:, 0:6144]
        self.rw = self.big[:, 6144:27744]
        self.r2 = self.big[:, 27744:33888]
        self.r3 = self.big[:, 33888:40032]
        self.const = region(C_END)
        self.negb = region(TOK)
        self.identb = region(P // 2)
        self.misc = region(52700 - at)
        c = self.const
        self.ident = c[:, C_IDENT:C_IDENT + P]
        self.ones = c[:, C_ONES:C_ONES + P]
        self.eps = c[:, C_EPS:C_EPS + 1]
        self.xT = self.xt_r.rearrange("p (k t) -> p k t", k=KD)
        dram = nc.dram_tensor
        self.mods = dram("mods", (2, 2 * MOD), F32).ap()
        self.rpb_flat = dram("rpb_flat", (1, HEADS * 15 * 31 + 128), F32).ap()
        self.rows = dram("rows", (TOK, D), F32).ap()
        self.slots = dram("slots", (NE * CAP, 2), I32).ap()
        self.pairs = dram("pairs", (2 * TOK, D), F32).ap()

    def sem(self, name):
        self.n_sems += 1
        s = self.nc.alloc_semaphore(f"{name}_{self.n_sems}")
        self.stage_sems.append(s)
        return s

    @contextmanager
    def stage(self):
        if self.old_sems:
            self.nc.clear_and_free_semaphores(self.old_sems)
        self.old_sems, self.stage_sems = self.stage_sems, []
        with self.nc.Block() as block:
            yield block

    def mod_row(self, cond, layer, i):
        o = layer * MOD + i * D
        return self.mods[cond:cond + 1, o:o + D].to_broadcast([P, D])


def load_stage(k):
    nc, io = k.nc, k.io
    loaded, const_in, flat_out, zeroed = k.sem("stream_in"), k.sem("const_in"), k.sem("rpb_flat_out"), k.sem("pad_zeroed")
    zero_out = k.sem("pad_out")
    n = HEADS * 15 * 31
    pad = k.misc[0:1, 0:64]
    with k.stage() as block:

        @block.sync
        def _(sp):
            sp.dma_start(k.const[:, :], io["const"]).then_inc(const_in, 16)
            sp.dma_start(k.h[:, 0:LT, :], io["x"][0].rearrange("(t p) d -> p t d", p=P)).then_inc(loaded, 16)
            sp.dma_start(k.h[:, LT:NT, :], io["ctx"][0].rearrange("(t p) d -> p t d", p=P)).then_inc(loaded, 16)
            sp.dma_start(k.rpb_flat[:, 64:64 + n],
                         io["na_rpb"].rearrange("a h r c -> a (h r c)")).then_inc(flat_out, 16)
            sp.wait_ge(zeroed, 1)
            sp.dma_start(k.rpb_flat[:, 0:64], pad).then_inc(zero_out, 16)
            sp.dma_start(k.rpb_flat[:, 64 + n:128 + n], pad).then_inc(zero_out, 16)
            sp.wait_ge(zero_out, 32)
            sp.wait_ge(flat_out, 16)
            sp.wait_ge(loaded, 32)

        @block.vector
        def _(dve):
            dve.memset(pad, 0.0).then_inc(zeroed, 1)
            dve.wait_ge(const_in, 16)
            dve.tensor_copy(k.identb.bitcast(BF16), k.ident)
            negb = k.negb.bitcast(BF16).rearrange("p (g t l) -> p g t l", g=2, t=NT)
            for g, col in enumerate((C_NEGF, C_NEGB)):
                for t in range(NT):
                    dve.tensor_copy(negb[:, g, t, :], k.const[:, col:col + P])


def modulation_stage(k):
    nc, io = k.nc, k.io
    cond_in, cond_T, cond_ready = k.sem("cond_in"), k.sem("cond_T"), k.sem("cond_ready")
    bias_in, prod_done, added, stored = k.sem("bmod_in"), k.sem("mod_prod"), k.sem("mod_added"), k.sem("mods_out")
    SLOTS, CH = 4, 512
    w_in = [k.sem(f"wmod_in{s}") for s in range(SLOTS)]
    n_chunks = 2 * MOD // CH
    c_rows = k.misc[0:16, 0:P]
    c_cols = k.misc[:, P:P + 16]
    wring = k.rw[:, 0:SLOTS * KD * CH].rearrange("p (s k n) -> p s k n", s=SLOTS, k=KD)
    row = k.big[0:2, 27744:27744 + 2 * MOD]
    with k.stage() as block:

        @block.sync
        def _(sp):
            sp.dma_start(c_rows[0:8, :], io["c"].rearrange("a (k p) -> (a k) p", p=P)).then_inc(cond_in, 16)
            sp.dma_start(c_rows[8:16, :], io["c_ctx"].rearrange("(k p) -> k p", p=P)).then_inc(cond_in, 16)
            for cond in range(2):
                sp.dma_start(row[cond:cond + 1, :],
                             io["b_mod"].rearrange("(a l) n -> a (l n)", a=1)).then_inc(bias_in, 16)
            for j in range(n_chunks):
                layer, c0 = divmod(j * CH, MOD)
                if j >= SLOTS:
                    sp.wait_ge(prod_done, j - SLOTS + 1)
                sp.dma_start(wring[:, j % SLOTS],
                             io["w_mod"][layer, :, c0:c0 + CH].rearrange("(k p) n -> p k n", p=P))\
                    .then_inc(w_in[j % SLOTS], 16)
            sp.wait_ge(added, n_chunks)
            sp.dma_start(k.mods, row).then_inc(stored, 16)
            sp.wait_ge(stored, 16)

        @block.scalar
        def _(act):
            act.wait_ge(cond_T, 1)
            act.activation(c_cols, k.ps[:, 7, 0:16], ACT.Silu).then_inc(cond_ready, 1)

        @block.tensor
        def _(pe):
            pe.wait_ge(cond_in, 32)
            pe.transpose(k.ps[:, 7, 0:16], c_rows, k.ident[0:16, 0:16]).then_inc(cond_T, 1)
            pe.wait_ge(cond_ready, 1)
            for j in range(n_chunks):
                pe.wait_ge(w_in[j % SLOTS], 16 * (j // SLOTS + 1))
                if j >= 4:
                    pe.wait_ge(added, j - 3)
                for kk in range(KD):
                    mm = pe.matmul(k.ps[0:2, j % 4, :], c_cols[:, kk:16:8], wring[:, j % SLOTS, kk, :],
                                   start=(kk == 0), stop=(kk == KD - 1))
                mm.then_inc(prod_done, 1)

        @block.vector
        def _(dve):
            dve.wait_ge(bias_in, 32)
            for j in range(n_chunks):
                dve.wait_ge(prod_done, j + 1)
                part = row[:, j * CH:(j + 1) * CH]
                dve.tensor_tensor(part, k.ps[0:2, j % 4, :], part, ALU.add).then_inc(added, 1)


def norm_stage(k, src, tiles, g_row, mod, xT, scratch, rows_out=None, out=None):
    nc = k.nc
    T = len(tiles)
    g_in, mod_in = k.sem("gain_in"), k.sem("mod_in")
    squared, root, rooted = k.sem("squared"), k.sem("root"), k.sem("rstd")
    rows_ready, gain_ready, chain = k.sem("rows_ready"), k.sem("gain_ready"), k.sem("norm_chain")
    turned, copied = k.sem("turned"), k.sem("turned_copied")
    stored = [k.sem(f"rows_stored{s}") for s in range(2)]
    nr = 2 if mod else 1
    gains = scratch[:, 0:nr * D].rearrange("p (c d) -> p c d", c=nr)
    shifts = scratch[:, 2 * D:4 * D].rearrange("p (c d) -> p c d", c=2)
    g = scratch[:, 4 * D:5 * D] if mod else gains[:, 0, :]
    xn = scratch[:, 5 * D:7 * D].rearrange("p (s d) -> p s d", s=2)
    junk = scratch[:, 7 * D:8 * D]
    stat = k.misc[:, 0:3 * NT].rearrange("p (a t) -> p a t", a=3)
    dst = rows_out if rows_out is not None else out
    with k.stage() as block:

        @block.sync
        def _(sp):
            sp.dma_start(g, g_row.to_broadcast([P, D])).then_inc(g_in, 16)
            if mod:
                for cond in range(2):
                    sp.dma_start(gains[:, cond, :], k.mod_row(cond, mod[0], mod[1])).then_inc(mod_in, 16)
                    sp.dma_start(shifts[:, cond, :], k.mod_row(cond, mod[0], mod[2])).then_inc(mod_in, 16)
            if dst is not None:
                for i, t in enumerate(tiles):
                    sp.wait_ge(rows_ready, i + 1)
                    sp.dma_start(dst[t * P:(t + 1) * P, :], xn[:, i % 2, :]).then_inc(stored[i % 2], 16)
                for s in range(2):
                    sp.wait_ge(stored[s], 16 * (T // 2))

        @block.scalar
        def _(act):
            link = Chain(act, squared)
            for i, t in enumerate(tiles):
                link(act.activation(junk, src(t), ACT.Square, accum_out=stat[:, 0, i:i + 1]))
            act.activation(stat[:, 1, 0:T], stat[:, 0, 0:T], ACT.Sqrt, bias=k.eps, scale=1.0 / D).then_inc(root, 1)
            if xT is not None:
                for i, t in enumerate(tiles):
                    act.wait_ge(turned, i + 1)
                    act.activation(xT[:, :, t * P:(t + 1) * P],
                                   k.ps[:, 2 * (i % 2):2 * (i % 2) + 2, :].rearrange("p a (b c) -> p (a b) c", c=P),
                                   ACT.Copy).then_inc(copied, 1)

        @block.vector
        def _(dve):
            link = Chain(dve, chain)
            dve.wait_ge(g_in, 16)
            if mod:
                dve.wait_ge(mod_in, 64)
                for cond in range(2):
                    dve.scalar_tensor_tensor(out=gains[:, cond, :], in0=gains[:, cond, :], scalar=1.0, in1=g,
                                             op0=ALU.add, op1=ALU.mult).then_inc(gain_ready, 1)
            dve.wait_ge(root, 1)
            dve.reciprocal(stat[:, 2, 0:T], stat[:, 1, 0:T]).then_inc(rooted, 1)
            dve.wait_ge(rooted, 1)
            if mod:
                dve.wait_ge(gain_ready, 2)
            for i, t in enumerate(tiles):
                cond = (0 if t < LT else 1) if mod else 0
                if i >= 2:
                    if xT is not None:
                        dve.wait_ge(turned, i - 1)
                    if dst is not None:
                        dve.wait_ge(stored[i % 2], 16 * (i // 2))
                last = dve.scalar_tensor_tensor(out=xn[:, i % 2, :], in0=src(t), scalar=stat[:, 2, i:i + 1],
                                                in1=gains[:, cond, :], op0=ALU.mult, op1=ALU.mult)
                if mod:
                    link(last)
                    last = dve.tensor_tensor(xn[:, i % 2, :], xn[:, i % 2, :], shifts[:, cond, :], ALU.add)
                last.then_inc(rows_ready, 1)

        if xT is not None:
            @block.tensor
            def _(pe):
                for i in range(T):
                    pe.wait_ge(rows_ready, i + 1)
                    if i >= 2:
                        pe.wait_ge(copied, i - 1)
                    for kk in range(KD):
                        tr = pe.transpose(k.ps[:, 2 * (i % 2) + kk // 4, (kk % 4) * P:(kk % 4 + 1) * P],
                                          xn[:, i % 2, kk * P:(kk + 1) * P], k.ident)
                    tr.then_inc(turned, 1)


def product_stage(k, name, chunks, ring, jobs, evacuate, extra=None):
    nc = k.nc
    R = len(ring)
    w_in = [k.sem(f"{name}_w_in{s}") for s in range(R)]
    prod = k.sem(f"{name}_prod")
    taken = {"v": k.sem(f"{name}_taken_v"), "s": k.sem(f"{name}_taken_s")}
    chain = k.sem(f"{name}_chain")
    extra_in = k.sem(f"{name}_extra_in")
    last_use = [max(j for j, job in enumerate(jobs) if c in job[0]) for c in range(len(chunks))]
    order = [sum(1 for job in jobs[:j + 1] if job[3] == jobs[j][3]) for j in range(len(jobs))]

    def slot(c):
        kk, n = chunks[c].shape[1], chunks[c].shape[2]
        return ring[c % R][:, 0:kk * n].rearrange("p (k n) -> p k n", k=kk)

    with k.stage() as block:

        @block.sync
        def _(sp):
            n_extra = extra(sp, extra_in) if extra else 0
            for c, src in enumerate(chunks):
                if c >= R:
                    sp.wait_ge(prod, max(last_use[:c - R + 1]) + 1)
                sp.dma_start(slot(c), src).then_inc(w_in[c % R], 16)

        @block.tensor
        def _(pe):
            for j, (used, shape, operands, _) in enumerate(jobs):
                for c in used:
                    pe.wait_ge(w_in[c % R], 16 * (c // R + 1))
                for i in range(j - 8, j - 7):
                    if i >= 0:
                        pe.wait_ge(taken[jobs[i][3]], order[i])
                pairs = operands([slot(c) for c in used])
                for i, (lhsT, rhs) in enumerate(pairs):
                    mm = pe.matmul(k.ps[0:shape[0], j % 8, 0:shape[1]], lhsT, rhs,
                                   start=(i == 0), stop=(i == len(pairs) - 1))
                mm.then_inc(prod, 1)

        def take(which, eng):
            link = Chain(eng, chain)
            for j, job in enumerate(jobs):
                if job[3] == which:
                    eng.wait_ge(prod, j + 1)
                    evacuate(which, eng, j, k.ps[0:job[1][0], j % 8, 0:job[1][1]], link)\
                        .then_inc(taken[which], 1)

        @block.scalar
        def _(act):
            take("s", act)

        @block.vector
        def _(dve):
            if extra:
                dve.wait_ge(extra_in, extra.count)
            take("v", dve)


def copy_out(which, eng, dst, src, scale=None):
    if which == "s":
        return eng.activation(dst, src, ACT.Copy, scale=1.0 if scale is None else scale)
    if scale is None:
        return eng.tensor_copy(dst, src)
    return eng.tensor_scalar(dst, src, scale, None, ALU.mult)


def weight_chunk(w, col, n):
    return w[:, col:col + n].rearrange("(k p) n -> p k n", p=P)


def channel_major_jobs(k, chunk, n_tiles, jobs, dsts, dst_of):
    for ct in range(n_tiles):
        for part, (a, b) in enumerate(((0, N_LAT), (N_LAT, TOK))):
            def operands(w, ct=ct, a=a, b=b):
                return [(w[0][:, kk, ct * P:(ct + 1) * P], k.xT[:, kk, a:b]) for kk in range(KD)]
            jobs.append(([chunk], [P, b - a], operands, "vs"[len(jobs) % 2]))
            dsts.append(dst_of(ct, part, a, b))


def token_major_jobs(k, chunk, n, tiles, jobs, dsts, dst_of, engine=None):
    for t in tiles:
        def operands(w, t=t):
            return [(k.xT[:, kk, t * P:(t + 1) * P], w[0][:, kk, 0:n]) for kk in range(KD)]
        jobs.append(([chunk], [P, n], operands, engine or "vs"[len(jobs) % 2]))
        dsts.append(dst_of(t))


def ssd_views(k):
    v = {}
    v["raw"] = k.rw[:, 0:12 * RAW_W].rearrange("p (c n) -> p c n", c=12)
    rest = k.rw[:, 12 * RAW_W:]
    v["ring"] = [rest[:, s * 4096:(s + 1) * 4096] for s in range(3)]
    at = 0

    def part(n):
        nonlocal at
        at += n
        return rest[:, at - n:at]

    v["conv"] = part(2 * CONV_W).rearrange("p (s n) -> p s n", s=2)
    v["btok"] = part(NT * 256).rearrange("p (t n) -> p t n", t=NT)
    v["sel"] = part(16 * P)
    cb_at = at
    v["cb"] = part(2 * TOK).rearrange("p (g n) -> p g n", g=2)
    v["decay"] = part(4 * TOK).rearrange("p (s d n) -> p s d n", s=2, d=2)
    v["xd"] = part(4 * NT * HD).rearrange("p (s d t n) -> p s d t n", s=2, d=2, t=NT)
    sc = rest[:, cb_at:cb_at + 6 * D]
    v["state"] = sc[:, 0:2 * D].rearrange("p (d n) -> p d n", d=2)
    v["xw"] = sc[:, 2 * D:4 * D].rearrange("p (d n) -> p d n", d=2)
    v["yo"] = sc[:, 4 * D:6 * D].rearrange("p (d n) -> p d n", d=2)
    v["xs"] = k.r2.rearrange("p (t n) -> p t n", t=NT)
    v["y"] = k.r3.rearrange("p (t n) -> p t n", t=NT)
    m = k.misc
    at2 = 32

    def small(n):
        nonlocal at2
        at2 += n
        return m[:, at2 - n:at2]

    v["par"] = small(72)
    v["par_rows"] = small(P)[0:72, :]
    v["bc"] = small(80)
    for nm in ("dt", "adt", "nac", "eac", "etot", "wst", "u0", "u1"):
        v[nm] = small(NT * 32).rearrange("p (t n) -> p t n", t=NT)
    v["rowf"] = small(TOK)[0:16, :]
    v["rowb"] = small(TOK)[0:16, :]
    return v


def ssd_project_stage(k, v):
    w = k.io["ab_w_in"][0]
    chunks = [weight_chunk(w, O_XBC + i * 512, 512) for i in range(3)] + [weight_chunk(w, O_DT, 32)]
    jobs, dsts = [], []
    for c in range(3):
        channel_major_jobs(k, c, 4, jobs, dsts,
                           lambda ct, part, a, b, c=c: v["raw"][:, 4 * c + ct, 2 + a + 4 * part:2 + b + 4 * part])
    token_major_jobs(k, 3, 32, range(NT), jobs, dsts, lambda t: v["dt"][:, t, :])
    product_stage(k, "xbc", chunks, v["ring"], jobs,
                  lambda which, eng, j, ps, link: copy_out(which, eng, dsts[j], ps))


def conv_stage(k, v):
    nc, io = k.nc, k.io
    par_in, par_T, par_ok = k.sem("conv_par_in"), k.sem("conv_par_T"), k.sem("conv_par_ready")
    bc_in, sel_in = k.sem("ssd_bc_in"), k.sem("sel_in")
    padded, conved, silued, chain = k.sem("pads_zeroed"), k.sem("conved"), k.sem("silued"), k.sem("conv_chain")
    turned, copied = k.sem("xs_turned"), k.sem("xs_copied")
    aexp, dtv, dte, adt_ok = k.sem("a_exp"), k.sem("dt_abs"), k.sem("dt_exp"), k.sem("adt_ready")
    cum, cum_rows, cum_T, cum_ok, ctot = (k.sem("cum_rows"), k.sem("cum_rows_copied"), k.sem("cum_T"),
                                          k.sem("cum_copied"), k.sem("cum_tot"))
    exps, coef = k.sem("decay_exps"), k.sem("coef")
    raw, conv = v["raw"], v["conv"]
    cw = v["par"][:, 0:60].rearrange("p (w c) -> p w c", w=5)
    cb = v["par"][:, 60:72]
    a_b, dtb_b = v["bc"][:, 0:32], v["bc"][:, 32:64]

    def cols(t):
        return slice(latent_col(t), latent_col(t) + P)

    with k.stage() as block:

        @block.sync
        def _(sp):
            sp.dma_start(v["par_rows"][0:60, :],
                         io["ssm_conv_w"][0].rearrange("w (c p) -> (w c) p", p=P)).then_inc(par_in, 16)
            sp.dma_start(v["par_rows"][60:72, :],
                         io["ssm_conv_b"][0].rearrange("(c p) -> c p", p=P)).then_inc(par_in, 16)
            sp.dma_start(a_b, io["ssm_A_log"].rearrange("a d h -> a (d h)").to_broadcast([P, 32])).then_inc(bc_in, 16)
            sp.dma_start(dtb_b, io["ssm_dt_bias"].rearrange("a d h -> a (d h)").to_broadcast([P, 32]))\
                .then_inc(bc_in, 16)
            sp.dma_start(v["bc"][:, 64:80], io["ssm_D"].to_broadcast([P, 16])).then_inc(bc_in, 16)
            sp.dma_start(v["sel"][0:16, :], io["sel"]).then_inc(sel_in, 16)
            sp.wait_ge(sel_in, 16)

        @block.gpsimd
        def _(pool):
            for c0 in (0, 2 + N_LAT, RAW_W - 2):
                pad = pool.memset(raw[:, :, c0:c0 + (4 if c0 == 2 + N_LAT else 2)], 0.0)
                pad.then_inc(padded, 1)

        @block.vector
        def _(dve):
            link = Chain(dve, chain)
            dve.wait_ge(bc_in, 48)
            bias = dtb_b.unsqueeze(1).to_broadcast([P, NT, 32])
            link(dve.tensor_tensor(v["dt"], v["dt"], bias, ALU.add))
            link(dve.tensor_scalar(v["u0"], v["dt"], -1.0, None, ALU.mult))
            dve.tensor_tensor(v["u0"], v["u0"], v["dt"], ALU.min).then_inc(dtv, 1)
            dve.wait_ge(par_T, 1)
            dve.tensor_copy(v["par"], k.ps[:, 7, 0:72]).then_inc(par_ok, 1)
            dve.wait_ge(par_ok, 1)
            dve.wait_ge(padded, 3)
            dve.wait_ge(dte, 1)
            link(dve.tensor_scalar(v["u1"], v["u0"], 2.0, None, ALU.add))
            link(dve.reciprocal(v["u1"], v["u1"]))
            link(dve.tensor_tensor(v["u0"], v["u0"], v["u1"], ALU.mult))
            link(dve.tensor_tensor(v["u1"], v["u0"], v["u0"], ALU.mult))
            acc = v["adt"]
            link(dve.tensor_scalar(acc, v["u1"], 2.0 / 17, 2.0 / 15, ALU.mult, ALU.add))
            for n in (13, 11, 9, 7, 5, 3, 1):
                link(dve.tensor_tensor(acc, acc, v["u1"], ALU.mult))
                link(dve.tensor_scalar(acc, acc, 2.0 / n, None, ALU.add))
            link(dve.tensor_tensor(acc, acc, v["u0"], ALU.mult))
            link(dve.tensor_scalar(v["dt"], v["dt"], 0.0, None, ALU.max))
            link(dve.tensor_tensor(v["dt"], v["dt"], acc, ALU.add))
            dve.wait_ge(aexp, 1)
            link(dve.tensor_scalar(a_b, a_b, -1.0, None, ALU.mult))
            dve.tensor_tensor(v["adt"], v["dt"], a_b.unsqueeze(1).to_broadcast([P, NT, 32]), ALU.mult)\
                .then_inc(adt_ok, 1)
            for c in range(12):
                if c >= 2:
                    dve.wait_ge(silued, c - 1)
                link(dve.tensor_scalar(conv[:, c % 2, :], raw[:, c, 0:CONV_W], cw[:, 0, c:c + 1], cb[:, c:c + 1],
                                       ALU.mult, ALU.add))
                for w in range(1, 5):
                    last = dve.scalar_tensor_tensor(out=conv[:, c % 2, :], in0=raw[:, c, w:w + CONV_W],
                                                    scalar=cw[:, w, c:c + 1], in1=conv[:, c % 2, :],
                                                    op0=ALU.mult, op1=ALU.add)
                    if w < 4:
                        link(last)
                last.then_inc(conved, 1)
                if c == 2:
                    dve.wait_ge(cum, 4)
                    dve.tensor_copy(v["rowf"][:, 0:512], k.ps[0:16, 4, :])
                    dve.tensor_copy(v["rowf"][:, 512:TOK], k.ps[0:16, 5, 0:256])
                    dve.tensor_copy(v["rowb"][:, 0:512], k.ps[0:16, 6, :])
                    dve.tensor_copy(v["rowb"][:, 512:TOK], k.ps[0:16, 7, 0:256]).then_inc(cum_rows, 1)
                if c == 4:
                    dve.wait_ge(cum_T, 1)
                    dve.wait_ge(ctot, 1)
                    cum_ps = k.ps[:, 4, 0:NT * 32].rearrange("p (t n) -> p t n", t=NT)
                    tot_ps = k.ps[:, 5, 0:NT * 32].rearrange("p (t n) -> p t n", t=NT)
                    link(dve.tensor_scalar(v["nac"], cum_ps, -1.0, None, ALU.mult))
                    link(dve.tensor_tensor(v["wst"], tot_ps, v["nac"], ALU.add))
                    dve.tensor_copy(v["etot"], tot_ps).then_inc(cum_ok, 1)
            dve.wait_ge(exps, 3)
            link(dve.tensor_tensor(v["wst"], v["wst"], v["dt"], ALU.mult))
            for i in range(NT):
                dve.wait_ge(turned, i + 1)
                src = k.ps[:, 2 * (i % 2):2 * (i % 2) + 2, :].rearrange("p a n -> p (a n)")
                dve.tensor_copy(v["xs"][:, i, :], src).then_inc(copied, 1)
            dve.wait_ge(turned, NT + 1)
            dve.tensor_copy(v["btok"], k.ps[:, 4:7, :].rearrange("p a (b n) -> p (a b) n", n=256)).then_inc(copied, 1)

        @block.scalar
        def _(act):
            act.wait_ge(bc_in, 48)
            act.activation(a_b, a_b, ACT.Exp).then_inc(aexp, 1)
            act.wait_ge(dtv, 1)
            act.activation(v["u0"], v["u0"], ACT.Exp).then_inc(dte, 1)
            for c in range(12):
                act.wait_ge(conved, c + 1)
                act.activation(raw[:, c, 0:CONV_W], conv[:, c % 2, :], ACT.Silu).then_inc(silued, 1)
            act.wait_ge(cum_ok, 1)
            act.activation(v["eac"], v["nac"], ACT.Exp, scale=-1.0).then_inc(exps, 1)
            act.activation(v["etot"], v["etot"], ACT.Exp).then_inc(exps, 1)
            act.activation(v["wst"], v["wst"], ACT.Exp).then_inc(exps, 1)

        @block.tensor
        def _(pe):
            pe.wait_ge(par_in, 32)
            pe.transpose(k.ps[:, 7, 0:72], v["par_rows"], k.ident[0:72, 0:72]).then_inc(par_T, 1)
            pe.wait_ge(par_ok, 1)
            pe.wait_ge(adt_ok, 1)
            tri = [k.const[:, C_TRIF:C_TRIF + P], k.const[:, C_TRIB:C_TRIB + P]]
            for d in range(2):
                for half, (t0, t1) in enumerate(((0, LT), (LT, NT))):
                    for t in range(t0, t1):
                        mm = pe.matmul(k.ps[0:16, 4 + 2 * d + half, (t - t0) * P:(t - t0 + 1) * P],
                                       v["adt"][:, t, 16 * d:16 * d + 16], tri[d], start=True, stop=True)
                    mm.then_inc(cum, 1)
            pe.wait_ge(cum_rows, 1)
            for t in range(NT):
                for d, row in enumerate((v["rowf"], v["rowb"])):
                    tr = pe.transpose(k.ps[:, 4, t * 32 + 16 * d:t * 32 + 16 * d + 16], row[:, t * P:(t + 1) * P],
                                      k.ident[0:16, 0:16])
            tr.then_inc(cum_T, 1)
            pe.matmul(k.ps[:, 5, 0:NT * 32], k.ones, v["adt"].rearrange("p t n -> p (t n)"),
                      start=True, stop=True).then_inc(ctot, 1)
            pe.wait_ge(silued, 12)
            for t in range(NT):
                if t >= 2:
                    pe.wait_ge(copied, t - 1)
                for c in range(8):
                    tr = pe.transpose(k.ps[:, 2 * (t % 2) + c // 4, (c % 4) * P:(c % 4 + 1) * P],
                                      raw[:, c, cols(t)], k.ident)
                tr.then_inc(turned, 1)
            pe.wait_ge(cum_ok, 1)
            for t in range(NT):
                for g in range(2):
                    tr = pe.transpose(k.ps[:, 4 + t // 2, (t % 2) * 256 + g * P:(t % 2) * 256 + (g + 1) * P],
                                      raw[:, 8 + g, cols(t)], k.ident)
            tr.then_inc(turned, 1)


def ssd_diagonal_stage(k, v):
    nc = k.nc
    cb_done, cb_ok = k.sem("cb_prod"), k.sem("cb_copied")
    bcast, decayed, scaled, xd_ok = k.sem("cum_bcast"), k.sem("decayed"), k.sem("decay_x_cb"), k.sem("xd_ready")
    yprod, y_ok, chain = k.sem("ydiag_prod"), k.sem("ydiag_taken"), k.sem("ydiag_chain")
    raw = v["raw"]
    rows = (v["rowf"], v["rowb"])
    negb = k.negb.bitcast(BF16).rearrange("p (g n) -> p g n", g=2)
    xs4 = v["xs"].rearrange("p t (h n) -> p t h n", n=HD)
    y4 = v["y"].rearrange("p t (h n) -> p t h n", n=HD)
    NU = 2 * HEADS

    def cum_ps(u):
        return k.ps[:, 2 * (u % 2):2 * (u % 2) + 2, :].rearrange("p a n -> p (a n)")[:, 0:TOK]

    with k.stage() as block:

        @block.tensor
        def _(pe):
            for g in range(2):
                for t in range(NT):
                    c = slice(latent_col(t), latent_col(t) + P)
                    mm = pe.matmul(k.ps[:, 2 * g + t // LT, (t % LT) * P:(t % LT + 1) * P], raw[:, 8 + g, c],
                                   raw[:, 10 + g, c], start=True, stop=True)
                mm.then_inc(cb_done, 1)
            pe.wait_ge(cb_ok, 2)

            def broadcast(u):
                h, d = divmod(u, 2)
                if u >= 2:
                    pe.wait_ge(decayed, u - 1)
                for bank, (a, b) in enumerate(((0, 512), (512, TOK))):
                    out = k.ps[:, 2 * (u % 2) + bank, 0:b - a]
                    pe.matmul(out, v["sel"][0:16, h * P:(h + 1) * P], rows[d][:, a:b], start=True, stop=False)
                    mm = pe.matmul(out, k.identb.bitcast(BF16), negb[:, d, a:b], start=False, stop=True)
                mm.then_inc(bcast, 1)

            broadcast(0)
            broadcast(1)
            for h in range(HEADS):
                if h + 1 < HEADS:
                    broadcast(2 * h + 2)
                    broadcast(2 * h + 3)
                pe.wait_ge(scaled, 2 * h + 2)
                pe.wait_ge(xd_ok, 2 * h + 2)
                if h >= 2:
                    pe.wait_ge(y_ok, h - 1)
                for t in range(NT):
                    for d in range(2):
                        mm = pe.matmul(k.ps[:, 4 + h % 2, t * HD:(t + 1) * HD],
                                       v["decay"][:, h % 2, d, t * P:(t + 1) * P], v["xd"][:, h % 2, d, t, :],
                                       start=(d == 0), stop=(d == 1))
                mm.then_inc(yprod, 1)

        @block.scalar
        def _(act):
            for u in range(NU):
                h, d = divmod(u, 2)
                act.wait_ge(bcast, u + 1)
                if h >= 2:
                    act.wait_ge(yprod, h - 1)
                for t in range(NT):
                    e = act.activation(v["decay"][:, h % 2, d, t * P:(t + 1) * P], cum_ps(u)[:, t * P:(t + 1) * P],
                                       ACT.Exp, bias=v["nac"][:, t, 16 * d + h:16 * d + h + 1])
                e.then_inc(decayed, 1)

        @block.vector
        def _(dve):
            for g in range(2):
                dve.wait_ge(cb_done, g + 1)
                dve.tensor_copy(v["cb"][:, g, :], k.ps[:, 2 * g:2 * g + 2, :].rearrange("p a n -> p (a n)")[:, 0:TOK])\
                    .then_inc(cb_ok, 1)
            dve.wait_ge(cb_ok, 2)

            def take(h):
                dve.wait_ge(yprod, h + 1)
                dve.scalar_tensor_tensor(out=y4[:, :, h, :], in0=xs4[:, :, h, :], scalar=v["bc"][:, 64 + h:65 + h],
                                         in1=k.ps[:, 4 + h % 2, 0:NT * HD].rearrange("p (t n) -> p t n", t=NT),
                                         op0=ALU.mult, op1=ALU.add).then_inc(y_ok, 1)

            for h in range(HEADS):
                for d in range(2):
                    if h >= 2:
                        dve.wait_ge(yprod, h - 1)
                    dt_b = v["dt"][:, :, 16 * d + h:16 * d + h + 1].to_broadcast([P, NT, HD])
                    dve.tensor_tensor(v["xd"][:, h % 2, d, :, :], xs4[:, :, h, :], dt_b, ALU.mult).then_inc(xd_ok, 1)
                    dve.wait_ge(decayed, 2 * h + d + 1)
                    m = v["decay"][:, h % 2, d, :]
                    dve.tensor_tensor(m, m, v["cb"][:, h // 8, :], ALU.mult).then_inc(scaled, 1)
                if h >= 1:
                    take(h - 1)
            take(HEADS - 1)


def ssd_states_stage(k, v):
    nc = k.nc
    weighted, off_prod, st_prod = k.sem("x_weighted"), k.sem("yoff_prod"), k.sem("state_prod")
    state_ok, y_ok, chain = k.sem("state_ready"), k.sem("yoff_taken"), k.sem("state_chain")
    raw, S, xw, yo = v["raw"], v["state"], v["xw"], v["yo"]
    order = [[LT, LT + 1] + list(range(LT)), [LT + 1, LT] + list(range(LT))[::-1]]
    steps = [(i, d) for i in range(NT) for d in range(2)]

    def heads(ap):
        return ap.rearrange("p (h n) -> p h n", n=HD)

    def per_head(coef, t, d):
        return coef[:, t, 16 * d:16 * d + 16].unsqueeze(2).to_broadcast([P, HEADS, HD])

    def off_ps(d):
        return k.ps[:, 4 * d:4 * d + 2, :].rearrange("p a n -> p (a n)")

    def st_ps(d):
        return k.ps[:, 4 * d + 2:4 * d + 4, :].rearrange("p a n -> p (a n)")

    with k.stage() as block:

        @block.tensor
        def _(pe):
            for n, (i, d) in enumerate(steps):
                t = order[d][i]
                c = slice(latent_col(t), latent_col(t) + P)
                if i > 0:
                    pe.wait_ge(state_ok, n - 1)
                    for g in range(2):
                        mm = pe.matmul(k.ps[:, 4 * d + g, :], raw[:, 10 + g, c], S[:, d, g * 512:(g + 1) * 512],
                                       start=True, stop=True)
                    mm.then_inc(off_prod, 1)
                if i < NT - 1:
                    pe.wait_ge(weighted, n + 1)
                    for g in range(2):
                        mm = pe.matmul(k.ps[:, 4 * d + 2 + g, :], v["btok"][:, t, g * P:(g + 1) * P],
                                       xw[:, d, g * 512:(g + 1) * 512], start=True, stop=True)
                    mm.then_inc(st_prod, 1)

        @block.gpsimd
        def _(pool):
            for n, (i, d) in enumerate(steps):
                t = order[d][i]
                if i < NT - 1:
                    if i > 0:
                        pool.wait_ge(st_prod, n - 1)
                    pool.tensor_tensor(heads(xw[:, d, :]), heads(v["xs"][:, t, :]), per_head(v["wst"], t, d),
                                       ALU.mult).then_inc(weighted, 1)

        @block.vector
        def _(dve):
            link = Chain(dve, chain)
            for n, (i, d) in enumerate(steps):
                t = order[d][i]
                if i > 0:
                    dve.wait_ge(off_prod, n - 1)
                    link(dve.tensor_tensor(heads(yo[:, d, :]), heads(off_ps(d)), per_head(v["eac"], t, d), ALU.mult))
                    link(dve.tensor_tensor(v["y"][:, t, :], v["y"][:, t, :], yo[:, d, :], ALU.add))
                if i < NT - 1:
                    dve.wait_ge(st_prod, n + 1)
                    if i == 0:
                        dve.tensor_copy(S[:, d, :], st_ps(d)).then_inc(state_ok, 1)
                    else:
                        link(dve.tensor_tensor(heads(S[:, d, :]), heads(S[:, d, :]), per_head(v["etot"], t, d),
                                               ALU.mult))
                        dve.tensor_tensor(S[:, d, :], S[:, d, :], st_ps(d), ALU.add).then_inc(state_ok, 1)


def gate_stage(k, v):
    w = k.io["ab_w_in"][0]
    chunks = [weight_chunk(w, O_Z + i * 512, 512) for i in range(2)]
    jobs, dsts = [], []
    for c in range(2):
        token_major_jobs(k, c, 512, range(NT), jobs, dsts, lambda t, c=c: (t, c), engine="s")
    z = k.rw[:, 0:6144].rearrange("p (t n) -> p t n", t=NT)
    product_stage(k, "z", chunks, v["ring"], jobs,
                  lambda which, eng, j, ps, link: eng.activation(
                      z[:, dsts[j][0], dsts[j][1] * 512:(dsts[j][1] + 1) * 512], ps, ACT.Silu))
    nc = k.nc
    with k.stage() as block:

        @block.vector
        def _(dve):
            for t in range(0, NT, 2):
                dve.tensor_tensor(v["y"][:, t, :], v["y"][:, t, :], z[:, t, :], ALU.mult)

        @block.gpsimd
        def _(pool):
            for t in range(1, NT, 2):
                pool.tensor_tensor(v["y"][:, t, :], v["y"][:, t, :], z[:, t, :], ALU.mult)


def na_project_stage(k, n):
    w = k.io["ab_w_in"][0]
    chunks = [weight_chunk(w, o + i * 512, 512) for o in (O_Q, O_K, O_V) for i in range(2)]
    jobs, dsts = [], []
    for c in range(4):
        dst = n["qT"] if c < 2 else n["kT"]
        channel_major_jobs(k, c, 4, jobs, dsts,
                           lambda ct, part, a, b, c=c, dst=dst: (dst[:, 4 * (c % 2) + ct, a:b], c < 2, c < 2 and part == 0))
    for c in range(4, 6):
        token_major_jobs(k, c, 512, range(NT), jobs, dsts,
                         lambda t, c=c: (n["v"][:, t, (c - 4) * 512:(c - 3) * 512], False, False))

    def evacuate(which, eng, j, ps, link):
        dst, is_q, latent_q = dsts[j]
        if latent_q:
            dst, ps = backwards(dst), ps.rearrange("p (u t) -> p u t", t=P)
        return copy_out(which, eng, dst, ps, HD ** -0.5 if is_q else None)

    product_stage(k, "naqkv", chunks, n["ring"], jobs, evacuate)


def backwards(ap):
    (ps, pn), (step, n) = ap.ap
    return bass.AP(ap.tensor, ap.offset + (P - 1) * step, [[ps, pn], [P * step, n // P], [-step, P]])


def attention_stage(k, name, qT, kT, vv, oT, n_ctx_units, bias, pt, pt_ctx):
    nc = k.nc
    U = LT + n_ctx_units
    N = HEADS * U
    s_done, mx_done, exp_done, p_ok = k.sem(f"{name}_scores"), k.sem(f"{name}_max"), k.sem(f"{name}_exp"), k.sem(f"{name}_probs")
    turned, pt_ok = k.sem(f"{name}_probs_T"), k.sem(f"{name}_probs_T_copied")
    pv_done, o_ok, chain = k.sem(f"{name}_pv"), k.sem(f"{name}_o_taken"), k.sem(f"{name}_chain")
    chain_act = k.sem(f"{name}_chain_act")
    prob = k.misc[:, 0:3 * TOK].rearrange("p (s n) -> p s n", s=3)
    st = k.misc[:, 3 * TOK:3 * TOK + 18].rearrange("p (s a) -> p s a", s=3)
    bias_in = [k.sem(f"{name}_bias_in{s}") for s in range(2)]
    bias_ok = k.sem(f"{name}_bias_masked")
    groups = []
    for h in range(HEADS):
        groups.append((h, False, h * U + LT - 1))
        if n_ctx_units:
            groups.append((h, True, h * U + U - 1))

    def is_lat(n):
        return n % U < LT

    def scores_ps(n):
        pair = k.ps[:, 2 * (n % 2):2 * (n % 2) + 2, :].rearrange("p a n -> p (a n)")
        return pair[:, 0:TOK] if is_lat(n) else pair[:, N_LAT:TOK]

    def prob_of(n):
        return prob[:, n % 3, 0:TOK] if is_lat(n) else prob[:, n % 3, N_LAT:TOK]

    with k.stage() as block:

        if bias is not None:
            @block.sync
            def _(sp):
                for h in range(HEADS):
                    if h >= 2:
                        sp.wait_ge(mx_done, (h - 2) * U + LT)
                    for r in range(2):
                        base = k.rpb_flat[0:1, 64 + h * 15 * 31 + 31 * (1 - r) + 15 - (GRID - 1):]
                        src = bass.AP(base.tensor, base.offset, [[1, GRID], [31, 14], [1, GRID]])
                        sp.dma_start(bias["tile"][(1 - r) * GRID:(2 - r) * GRID, h % 2, :, :], src)\
                            .then_inc(bias_in[h % 2], 16)

        @block.tensor
        def _(pe):
            def scores(n):
                h, u = divmod(n, U)
                if n >= 2:
                    pe.wait_ge(exp_done, n - 1)
                if is_lat(n):
                    pe.matmul(k.ps[:, 2 * (n % 2), :], qT(h, u), kT(h, 0, N_LAT), start=True, stop=True)
                pe.matmul(k.ps[:, 2 * (n % 2) + 1, 0:N_CTX], qT(h, u), kT(h, N_LAT, TOK), start=True, stop=True)\
                    .then_inc(s_done, 1)

            def turn(n):
                pe.wait_ge(p_ok, n + 1)
                if n >= 1:
                    pe.wait_ge(pt_ok, n)
                keys = NT if is_lat(n) else CT
                for kt in range(keys):
                    tr = pe.transpose(k.ps[:, 4 + kt // 4, (kt % 4) * P:(kt % 4 + 1) * P],
                                      prob_of(n)[:, kt * P:(kt + 1) * P], k.ident)
                tr.then_inc(turned, 1)

            def values(i):
                h, is_ctx, last = groups[i]
                pe.wait_ge(pt_ok, last + 1)
                if i >= 2:
                    pe.wait_ge(o_ok, i - 1)
                keys = CT if is_ctx else NT
                for kt in range(keys):
                    src = pt_ctx[:, h % 2, kt, :] if is_ctx else pt[:, h % 2, kt, :]
                    mm = pe.matmul(k.ps[:, 6 + i % 2, 0:src.shape[1]], vv(h, kt + (LT if is_ctx else 0)), src,
                                   start=(kt == 0), stop=(kt == keys - 1))
                mm.then_inc(pv_done, 1)

            i = 0
            for n in range(N + 4):
                if n < N:
                    scores(n)
                while i < len(groups) and groups[i][2] <= n - 3:
                    values(i)
                    i += 1
                if 2 <= n < N + 2:
                    turn(n - 2)

        @block.scalar
        def _(act):
            for n in range(N + 2):
                if n < N:
                    act.wait_ge(mx_done, n + 1)
                    s = st[:, n % 3, :]
                    if is_lat(n) and bias is not None:
                        act.activation(prob_of(n)[:, 0:N_LAT], prob_of(n)[:, 0:N_LAT], ACT.Exp, bias=s[:, 1:2],
                                       accum_out=s[:, 2:3]).then_inc(chain_act, 1)
                        act.activation(prob_of(n)[:, N_LAT:TOK], scores_ps(n)[:, N_LAT:TOK], ACT.Exp, bias=s[:, 1:2],
                                       accum_out=s[:, 3:4]).then_inc(exp_done, 1)
                    else:
                        act.activation(prob_of(n), scores_ps(n), ACT.Exp, bias=s[:, 1:2],
                                       accum_out=s[:, 2:3]).then_inc(exp_done, 1)
                if n >= 2:
                    m = n - 2
                    h, u = divmod(m, U)
                    act.wait_ge(turned, m + 1)
                    if h >= 2:
                        per = len(groups) // HEADS
                        act.wait_ge(pv_done, per * (h - 2) + (1 if u < LT else per))
                    if is_lat(m):
                        dst = pt[:, h % 2, :, u * P:(u + 1) * P]
                        src = k.ps[:, 4:6, :].rearrange("p a (b n) -> p (a b) n", n=P)[:, 0:NT, :]
                    else:
                        dst = pt_ctx[:, h % 2, :, (u - LT) * P:(u - LT + 1) * P]
                        src = k.ps[:, 4, 0:CT * P].rearrange("p (b n) -> p b n", n=P)
                    act.activation(dst, src, ACT.Copy).then_inc(pt_ok, 1)

        @block.vector
        def _(dve):
            link = Chain(dve, chain)

            def maximum(n):
                h, u = divmod(n, U)
                s = st[:, n % 3, :]
                if u == 0 and bias is not None:
                    dve.wait_ge(bias_in[h % 2], 32 * (h // 2 + 1))
                    tile = bias["tile"][:, h % 2, :, :]
                    mask = bias["mask"].unsqueeze(1).to_broadcast([P, 14, GRID])
                    dve.tensor_tensor(tile, tile, mask, ALU.add).then_inc(bias_ok, 1)
                    dve.wait_ge(bias_ok, h + 1)
                dve.wait_ge(s_done, n + 1)
                if n >= 3:
                    dve.wait_ge(turned, n - 2)
                if is_lat(n) and bias is not None:
                    link(dve.tensor_reduce(s[:, 0:1], scores_ps(n)[:, N_LAT:TOK], AX.X, ALU.max))
                    b = bias["tile"][:, h % 2, 6 - 2 * u:14 - 2 * u, :].rearrange("p r c -> p (r c)")
                    link(dve.tensor_tensor_reduce(prob_of(n)[:, 0:N_LAT], scores_ps(n)[:, 0:N_LAT], b, 1.0,
                                                  s[:, 0:1], ALU.add, ALU.max, s[:, 4:5]))
                    dve.tensor_scalar(s[:, 1:2], s[:, 4:5], -1.0, None, ALU.mult).then_inc(mx_done, 1)
                else:
                    dve.tensor_reduce(s[:, 1:2], scores_ps(n), AX.X, ALU.max, negate=True).then_inc(mx_done, 1)

            def normalise(n):
                s = st[:, n % 3, :]
                dve.wait_ge(exp_done, n + 1)
                if is_lat(n) and bias is not None:
                    dve.wait_ge(chain_act, (n // U) * LT + n % U + 1)
                    link(dve.tensor_tensor(s[:, 2:3], s[:, 2:3], s[:, 3:4], ALU.add))
                link(dve.reciprocal(s[:, 5:6], s[:, 2:3]))
                dve.tensor_scalar(prob_of(n), prob_of(n), s[:, 5:6], None, ALU.mult).then_inc(p_ok, 1)

            def take(i):
                h, is_ctx, _ = groups[i]
                a, b = (N_LAT, N_LAT + N_CTX) if is_ctx else (0, N_LAT)
                r = (h % 2) * HD
                dve.wait_ge(pv_done, i + 1)
                src = k.ps[r:r + HD, 6 + i % 2, 0:b - a]
                if bias is not None and not is_ctx:
                    src = backwards(src)
                dve.tensor_copy(oT[r:r + HD, h // 2, a:b].rearrange("p (u t) -> p u t", t=P),
                                src if len(src.shape) == 3 else src.rearrange("p (u t) -> p u t", t=P)).then_inc(o_ok, 1)

            i = 0
            for n in range(N + 5):
                if n < N:
                    maximum(n)
                if 1 <= n <= N:
                    normalise(n - 1)
                while i < len(groups) and groups[i][2] <= n - 4:
                    take(i)
                    i += 1


def output_stage(k, name, w, lhs_tiles, tiles, layer, ring, scratch):
    n_half = w.shape[0] // (KD * P)
    conds = 2 if len(tiles) > LT else 1
    chunks = [w[a * D:(a + 1) * D, n * 512:(n + 1) * 512].rearrange("(k p) n -> p k n", p=P)
              for n in range(2) for a in range(n_half)]
    gate = scratch[:, 0:2 * D].rearrange("p (c d) -> p c d", c=2)
    tmp = scratch[:, 2 * D:2 * D + 1024].rearrange("p (s n) -> p s n", s=2)
    jobs, where = [], []
    for n in range(2):
        for t in tiles:
            def operands(ws, t=t):
                return [(lhs_tiles(a * KD + kk, t), ws[a][:, kk, :]) for a in range(n_half) for kk in range(KD)]
            jobs.append(([n * n_half + a for a in range(n_half)], [P, 512], operands, "v"))
            where.append((t, n))

    def load_gates(sp, sem):
        for cond in range(conds):
            sp.dma_start(gate[:, cond, :], k.mod_row(cond, layer, 2)).then_inc(sem, 16)
    load_gates.count = 16 * conds

    def evacuate(which, eng, j, ps, link):
        t, n = where[j]
        cols = slice(n * 512, (n + 1) * 512)
        link(eng.tensor_tensor(tmp[:, j % 2, :], ps, gate[:, 0 if t < LT else 1, cols], ALU.mult))
        return eng.tensor_tensor(k.h[:, t, cols], k.h[:, t, cols], tmp[:, j % 2, :], ALU.add)

    product_stage(k, name, chunks, ring, jobs, evacuate, load_gates)


def router_stage(k, T, r):
    nc, io = k.nc, k.io
    rw_in, rb_in = k.sem("router_w_in"), k.sem("router_b_in")
    logit, sig, chain = k.sem("logits"), k.sem("sigmoid"), k.sem("route_chain")
    mask_ok, ranked, dest_ok = k.sem("choice_mask"), k.sem("ranks"), k.sem("slots_known")
    fill_ok, filled, put, idx_in = k.sem("fill_made"), k.sem("table_filled"), k.sem("slots_put"), k.sem("slots_in")
    at = 0

    def part(*shape):
        nonlocal at
        n = 1
        for x in shape:
            n *= x
        at += n
        ap = k.rw[:, at - n:at]
        if len(shape) == 2:
            return ap.rearrange("p (a b) -> p a b", a=shape[0])
        if len(shape) == 3:
            return ap.rearrange("p (a b c) -> p a b c", a=shape[0], b=shape[1])
        return ap

    rw = part(KD, NE)
    rb = part(NE)
    s, sb, prod = part(T, NE), part(T, NE), part(T, NE)
    hi1, hi2, lo1, lo2, gs, gval = [part(T, NG) for _ in range(6)]
    gbest, vmin_g, best, vm1, vm2, wsum = [part(T) for _ in range(6)]
    s_in, b_in, oh1, oh2, val, pr4 = [part(T, EPG) for _ in range(6)]
    e_of = [part(T), part(T)]
    OH = [part(T, NE), part(T, NE)]
    M = part(T, NE)
    rank = [part(T), part(T)]
    dest = part(T, 2).bitcast(I32)
    entry = part(T, 2, 2).bitcast(I32)
    fill = part(NE * CAP // P, 2).bitcast(I32)
    cmax = part(1)
    iota = k.const[:, C_IOTA:C_IOTA + NE]
    tokid = k.const[:, C_TOKID:C_TOKID + T]

    def b2(ap, n):
        return ap.unsqueeze(2).to_broadcast([P, ap.shape[1], n])

    with k.stage() as block:

        @block.sync
        def _(sp):
            sp.dma_start(rw, io["router_w"].rearrange("(k p) e -> p k e", p=P)).then_inc(rw_in, 16)
            sp.dma_start(rb, io["router_bias"].rearrange("(a e) -> a e", a=1).to_broadcast([P, NE])).then_inc(rb_in, 16)
            sp.wait_ge(fill_ok, 2)
            sp.dma_start(k.slots.rearrange("(p n) w -> p n w", p=P), fill).then_inc(filled, 16)
            sp.wait_ge(put, 2 * T * 16)
            sp.dma_start(r["idxs"], k.slots.rearrange("(e c) w -> c e w", c=CAP)[0:P]).then_inc(idx_in, 16)
            sp.wait_ge(idx_in, 16)

        @block.gpsimd
        def _(pool):
            pool.memset(fill[:, :, 0:1], 0).then_inc(fill_ok, 1)
            pool.memset(fill[:, :, 1:2], 4 * TOK).then_inc(fill_ok, 1)
            pool.wait_ge(dest_ok, 2)
            pool.wait_ge(filled, 16)
            for t in range(T):
                for c in range(2):
                    pool.indirect_dma_start(
                        out=k.slots, out_offset=bass.IndirectOffsetOnAxis(ap=dest[:, t, c:c + 1], axis=0),
                        in_=entry[:, t, c, :], in_offset=None).then_inc(put, 16)

        @block.tensor
        def _(pe):
            pe.wait_ge(rw_in, 16)
            for t in range(T):
                for kk in range(KD):
                    mm = pe.matmul(k.ps[:, 7, t * NE:(t + 1) * NE], k.xT[:, kk, t * P:(t + 1) * P], rw[:, kk, :],
                                   start=(kk == 0), stop=(kk == KD - 1))
            mm.then_inc(logit, 1)
            pe.wait_ge(mask_ok, 1)
            for t in range(T):
                for u in range(t + 1):
                    stat = k.const[:, C_TRIS:C_TRIS + P] if u == t else k.ones
                    pe.matmul(k.ps[:, 6, t * NE:(t + 1) * NE], stat, M[:, u, :], start=(u == 0), stop=(u == t))
            for u in range(T):
                mm = pe.matmul(k.ps[:, 5, 0:NE], k.ones, M[:, u, :], start=(u == 0), stop=(u == T - 1))
            mm.then_inc(ranked, 1)

        @block.scalar
        def _(act):
            act.wait_ge(logit, 1)
            act.activation(s, k.ps[:, 7, 0:T * NE].rearrange("p (t e) -> p t e", t=T), ACT.Sigmoid).then_inc(sig, 1)

        @block.vector
        def _(dve):
            link = Chain(dve, chain)
            tt, ts = dve.tensor_tensor, dve.tensor_scalar
            dve.wait_ge(rb_in, 16)
            dve.wait_ge(sig, 1)
            link(tt(sb, s, rb.unsqueeze(1).to_broadcast([P, T, NE]), ALU.add))
            four = sb.rearrange("p t (g j) -> p t g j", j=EPG)
            link(tt(hi1, four[:, :, :, 0], four[:, :, :, 1], ALU.max))
            link(tt(lo1, four[:, :, :, 0], four[:, :, :, 1], ALU.min))
            link(tt(hi2, four[:, :, :, 2], four[:, :, :, 3], ALU.max))
            link(tt(lo2, four[:, :, :, 2], four[:, :, :, 3], ALU.min))
            link(tt(gs, hi1, hi2, ALU.max))
            link(tt(hi1, hi1, hi2, ALU.min))
            link(tt(lo1, lo1, lo2, ALU.max))
            link(tt(hi1, hi1, lo1, ALU.max))
            link(tt(gs, gs, hi1, ALU.add))

            def first_best(values, n, top, val_, vmin, onehot):
                link(dve.tensor_reduce(top, values, AX.X, ALU.max))
                link(tt(val_, values, b2(top, n), ALU.is_equal))
                link(ts(val_, val_, -99.0, None, ALU.mult))
                link(tt(val_, val_, iota[:, 0:n].unsqueeze(1).to_broadcast([P, T, n]), ALU.add))
                link(dve.tensor_reduce(vmin, val_, AX.X, ALU.min))
                link(tt(onehot, val_, b2(vmin, n), ALU.is_equal))

            first_best(gs, NG, gbest, gval, vmin_g, hi2)
            for dst, src in ((b_in, sb), (s_in, s)):
                link(tt(prod.rearrange("p t (g j) -> p t g j", j=EPG), src.rearrange("p t (g j) -> p t g j", j=EPG),
                        hi2.unsqueeze(3).to_broadcast([P, T, NG, EPG]), ALU.mult))
                link(dve.tensor_reduce(dst, prod.rearrange("p t (g j) -> p t j g", j=EPG), AX.X, ALU.add))
            first_best(b_in, EPG, best, val, vm1, oh1)
            link(ts(pr4, oh1, NEG, None, ALU.mult))
            link(tt(b_in, b_in, pr4, ALU.add))
            first_best(b_in, EPG, best, val, vm2, oh2)
            for c, (oh, vm) in enumerate(((oh1, vm1), (oh2, vm2))):
                link(tt(pr4, oh, s_in, ALU.mult))
                link(dve.tensor_reduce(r["wts"][:, c, 0:T], pr4, AX.X, ALU.add))
                link(ts(e_of[c], vmin_g, float(EPG), 99.0 * (EPG + 1), ALU.mult, ALU.add))
                link(tt(e_of[c], e_of[c], vm, ALU.add))
                link(tt(OH[c], b2(e_of[c], NE), iota.unsqueeze(1).to_broadcast([P, T, NE]), ALU.is_equal))
            dve.tensor_tensor(M, OH[0], OH[1], ALU.add).then_inc(mask_ok, 1)
            link(tt(wsum, r["wts"][:, 0, 0:T], r["wts"][:, 1, 0:T], ALU.add))
            link(dve.reciprocal(wsum, wsum))
            for c in range(2):
                link(tt(r["wts"][:, c, 0:T], r["wts"][:, c, 0:T], wsum, ALU.mult))
                link(dve.tensor_copy(entry[:, :, c, 0], tokid))
                link(ts(entry[:, :, c, 1], tokid, float(c * T * P), None, ALU.add))
            dve.wait_ge(ranked, 1)
            for c in range(2):
                link(tt(prod, OH[c], k.ps[:, 6, 0:T * NE].rearrange("p (t e) -> p t e", t=T), ALU.mult))
                link(dve.tensor_reduce(rank[c], prod, AX.X, ALU.add))
                link(ts(e_of[c], e_of[c], float(CAP), None, ALU.mult))
                dve.tensor_tensor(dest[:, :, c], e_of[c], rank[c], ALU.add).then_inc(dest_ok, 1)
            link(dve.tensor_reduce(cmax, k.ps[:, 5, 0:NE], AX.X, ALU.max))
            link(ts(r["more"], cmax, float(BLK) + 0.5, None, ALU.is_gt))


def moe_views(k):
    r = {}
    at = 0

    def part(n):
        nonlocal at
        at += n
        return k.big[:, at - n:at]

    r["wg"] = [part(KD * DE).rearrange("p (k n) -> p k n", k=KD) for _ in range(2)]
    r["wu"] = [part(KD * DE).rearrange("p (k n) -> p k n", k=KD) for _ in range(2)]
    r["wd"] = [part(DE * D // P).rearrange("p (k n) -> p k n", k=DE // P) for _ in range(2)]
    r["xb"] = [part(D) for _ in range(2)]
    r["xT"] = [part(D).rearrange("p (k t) -> p k t", k=KD) for _ in range(2)]
    r["sg"] = [part(DE) for _ in range(2)]
    r["hid"] = [part(DE) for _ in range(2)]
    r["hT"] = [part(DE).rearrange("p (k t) -> p k t", k=DE // P) for _ in range(2)]
    r["yo"] = [part(D) for _ in range(2)]
    r["gate"] = part(2 * D).rearrange("p (c d) -> p c d", c=2)
    m = k.misc
    r["idx"] = [m[:, 2 * s:2 * s + 2].bitcast(I32) for s in range(2)]
    r["more"] = m[:, 4:5].bitcast(I32)
    r["wts"] = m[:, 8:8 + 2 * NT].rearrange("p (c t) -> p c t", c=2)
    r["idxs"] = m[:, 32:32 + 2 * NE].bitcast(I32).rearrange("p (e w) -> p e w", w=2)
    return r


def expert_loop(eng):
    for e in (0, 1):
        yield 0, e, e
    with eng.Fori(1, NE // 2 - 1) as i:
        yield i, 0, 2 * i
        yield i, 1, 2 * i + 1
    for e in (NE - 2, NE - 1):
        yield NE // 2 - 1, e % 2, e


def wait_from(eng, sem, n):
    if not isinstance(n, int) or n > 0:
        eng.wait_ge(sem, n)


def wait_alone(k, eng, sem, n):
    eng.wait_ge(sem, n)
    if not isinstance(n, int):
        eng.sem_inc(k.passed, 1)


def gather_rows(k, pool, dst, idx):
    return pool.indirect_dma_start(out=dst, out_offset=None, in_=k.rows,
                                   in_offset=bass.IndirectOffsetOnAxis(ap=idx[:, 0:1], axis=0),
                                   bounds_check=TOK - 1, oob_is_err=False)


def scatter_rows(k, pool, T, src, idx):
    return pool.indirect_dma_start(out=k.pairs, out_offset=bass.IndirectOffsetOnAxis(ap=idx[:, 1:2], axis=0),
                                   in_=src, in_offset=None, bounds_check=2 * T * P - 1, oob_is_err=False)


def experts_stage(k, layer, T, r):
    nc, io = k.nc, k.io
    wg_in, wu_in, wd_in = [[k.sem(f"{n}_in{s}") for s in range(2)] for n in ("w_gate", "w_up", "w_down")]
    x_in, y_out = [[k.sem(f"{n}{s}") for s in range(2)] for n in ("rows_in", "pair_rows_out")]
    g_done, u_done, d_done = k.sem("gate_prod"), k.sem("up_prod"), k.sem("down_prod")
    x_turned, xT_ok, silu_ok, hid_ok = k.sem("rows_T"), k.sem("rows_T_copied"), k.sem("gate_silu"), k.sem("hidden")
    h_turned, hT_ok, y_ok, idx_ok = k.sem("hidden_T"), k.sem("hidden_T_copied"), k.sem("y_copied"), k.sem("idx_staged")

    with k.stage() as block:

        @block.sync
        def _(sp):
            for i, s, e in expert_loop(sp):
                for dst, src, sem, freed in ((r["wg"][s], io["moe_w_gate"], wg_in[s], g_done),
                                             (r["wu"][s], io["moe_w_up"], wu_in[s], u_done),
                                             (r["wd"][s], io["moe_w_down"], wd_in[s], d_done)):
                    wait_from(sp, freed, e - 1)
                    w = src[layer, bass.ds(e, 1)] if not isinstance(e, int) else src[layer, e:e + 1]
                    sp.dma_start(dst, w.rearrange("a (k p) n -> p (a k) n", p=P)).then_inc(sem, 16)

        @block.gpsimd
        def _(pool):
            def fetch(i, s, e):
                wait_from(pool, y_out[s], 16 * i)
                at = r["idxs"][:, e, :] if isinstance(e, int) else r["idxs"][:, bass.ds(e, 1), :].rearrange("p a w -> p (a w)")
                pool.tensor_copy(r["idx"][s], at).then_inc(idx_ok, 1)
                wait_from(pool, x_turned, e - 1)
                wait_alone(k, pool, idx_ok, e + 1)
                gather_rows(k, pool, r["xb"][s], r["idx"][s]).then_inc(x_in[s], 16)

            fetch(0, 0, 0)
            fetch(0, 1, 1)
            for i, s, e in expert_loop(pool):
                wait_alone(k, pool, y_ok, e + 1)
                scatter_rows(k, pool, T, r["yo"][s], r["idx"][s]).then_inc(y_out[s], 16)
                if not isinstance(e, int) or e + 2 < NE:
                    fetch(i + 1, s, e + 2)
            for s in range(2):
                pool.wait_ge(y_out[s], 16 * (NE // 2))

        @block.tensor
        def _(pe):
            def turn_rows(count, s):
                pe.wait_ge(x_in[s], count)
                for kk in range(KD):
                    tr = pe.transpose(k.ps[:, 4 + kk // 4, (kk % 4) * P:(kk % 4 + 1) * P],
                                      r["xb"][s][:, kk * P:(kk + 1) * P], k.ident)
                tr.then_inc(x_turned, 1)

            turn_rows(16, 0)
            for i, s, e in expert_loop(pe):
                for w, w_in, bank, done in ((r["wg"][s], wg_in[s], 0, g_done), (r["wu"][s], wu_in[s], 1, u_done)):
                    pe.wait_ge(w_in, 16 * (i + 1))
                    if bank == 0:
                        pe.wait_ge(xT_ok, e + 1)
                    for kk in range(KD):
                        mm = pe.matmul(k.ps[:, bank, :], r["xT"][s][:, kk, :], w[:, kk, :],
                                       start=(kk == 0), stop=(kk == KD - 1))
                    mm.then_inc(done, 1)
                if not isinstance(e, int) or e + 1 < NE:
                    turn_rows(16 * (i + 1 + s), 1 - s)
                pe.wait_ge(hid_ok, e + 1)
                for kk in range(DE // P):
                    tr = pe.transpose(k.ps[:, 6, kk * P:(kk + 1) * P], r["hid"][s][:, kk * P:(kk + 1) * P], k.ident)
                tr.then_inc(h_turned, 1)
                pe.wait_ge(wd_in[s], 16 * (i + 1))
                wait_from(pe, y_ok, e)
                pe.wait_ge(hT_ok, e + 1)
                for n in range(2):
                    for kk in range(DE // P):
                        mm = pe.matmul(k.ps[:, 2 + n, :], r["hT"][s][:, kk, :],
                                       r["wd"][s][:, kk, n * 512:(n + 1) * 512],
                                       start=(kk == 0), stop=(kk == DE // P - 1))
                mm.then_inc(d_done, 1)

        @block.scalar
        def _(act):
            def copy_rows_T(count, s):
                act.wait_ge(x_turned, count)
                act.activation(r["xT"][s], k.ps[:, 4:6, :].rearrange("p a (b t) -> p (a b) t", t=P), ACT.Copy)\
                    .then_inc(xT_ok, 1)

            copy_rows_T(1, 0)
            for i, s, e in expert_loop(act):
                act.wait_ge(g_done, e + 1)
                act.activation(r["sg"][s], k.ps[:, 0, :], ACT.Silu).then_inc(silu_ok, 1)
                if not isinstance(e, int) or e + 1 < NE:
                    copy_rows_T(e + 2, 1 - s)
                act.wait_ge(h_turned, e + 1)
                act.activation(r["hT"][s], k.ps[:, 6, :].rearrange("p (b t) -> p b t", t=P), ACT.Copy)\
                    .then_inc(hT_ok, 1)

        @block.vector
        def _(dve):
            for i, s, e in expert_loop(dve):
                dve.wait_ge(silu_ok, e + 1)
                dve.wait_ge(u_done, e + 1)
                dve.tensor_tensor(r["hid"][s], r["sg"][s], k.ps[:, 1, :], ALU.mult).then_inc(hid_ok, 1)
                dve.wait_ge(d_done, e + 1)
                wait_from(dve, y_out[s], 16 * i)
                dve.tensor_copy(r["yo"][s], k.ps[:, 2:4, :].rearrange("p a n -> p (a n)")).then_inc(y_ok, 1)


def more_blocks_stage(k, layer, T, r):
    nc, io = k.nc, k.io
    w_in, idx_in, x_in, y_out = k.sem("more_w_in"), k.sem("more_idx_in"), k.sem("more_rows_in"), k.sem("more_pairs_out")
    gu_done, d_done, x_turned, xT_ok = k.sem("more_gu"), k.sem("more_down"), k.sem("more_rows_T"), k.sem("more_rows_T_copied")
    silu_ok, hid_ok, h_turned, hT_ok, y_ok = (k.sem("more_silu"), k.sem("more_hidden"), k.sem("more_hidden_T"),
                                              k.sem("more_hidden_T_copied"), k.sem("more_y"))
    J = T * P // BLK - 1
    wg, wu, wd = r["wg"][0], r["wu"][0], r["wd"][0]
    xb, xT, sg, hid, hT, yo, idx = [r[n][0] for n in ("xb", "xT", "sg", "hid", "hT", "yo", "idx")]

    def blocks(eng):
        with eng.Fori(0, NE) as e:
            with eng.Fori(0, J) as j:
                yield e * J + j + 1

    with k.stage() as block:

        @block.sync
        def _(sp):
            more = sp.value_load(r["more"][0:1, 0:1], min_val=0, max_val=1)
            with sp.If(more > 0):
                with sp.Fori(0, NE) as e:
                    for dst, src in ((wg, io["moe_w_gate"]), (wu, io["moe_w_up"]), (wd, io["moe_w_down"])):
                        sp.dma_start(dst, src[layer, bass.ds(e, 1)].rearrange("a (k p) n -> p (a k) n", p=P))\
                            .then_inc(w_in, 16)
                    with sp.Fori(0, J) as j:
                        n = e * J + j + 1
                        sp.dma_start(idx, k.slots[bass.ds(e * CAP + j * BLK + BLK, P), :]).then_inc(idx_in, 16)
                        wait_alone(k, sp, y_out, 16 * n)

        @block.gpsimd
        def _(pool):
            more = pool.value_load(r["more"][0:1, 0:1], min_val=0, max_val=1)
            with pool.If(more > 0):
                for n in blocks(pool):
                    wait_alone(k, pool, idx_in, 16 * n)
                    gather_rows(k, pool, xb, idx).then_inc(x_in, 16)
                    wait_alone(k, pool, y_ok, n)
                    scatter_rows(k, pool, T, yo, idx).then_inc(y_out, 16)
                    wait_alone(k, pool, y_out, 16 * n)

        @block.tensor
        def _(pe):
            more = pe.value_load(r["more"][0:1, 0:1], min_val=0, max_val=1)
            with pe.If(more > 0):
                with pe.Fori(0, NE) as e:
                    wait_alone(k, pe, w_in, 48 * e + 48)
                    with pe.Fori(0, J) as j:
                        n = e * J + j + 1
                        pe.wait_ge(x_in, 16 * n)
                        for kk in range(KD):
                            tr = pe.transpose(k.ps[:, 4 + kk // 4, (kk % 4) * P:(kk % 4 + 1) * P],
                                              xb[:, kk * P:(kk + 1) * P], k.ident)
                        tr.then_inc(x_turned, 1)
                        pe.wait_ge(xT_ok, n)
                        for bank, w in ((0, wg), (1, wu)):
                            for kk in range(KD):
                                mm = pe.matmul(k.ps[:, bank, :], xT[:, kk, :], w[:, kk, :],
                                               start=(kk == 0), stop=(kk == KD - 1))
                        mm.then_inc(gu_done, 1)
                        pe.wait_ge(hid_ok, n)
                        for kk in range(DE // P):
                            tr = pe.transpose(k.ps[:, 6, kk * P:(kk + 1) * P], hid[:, kk * P:(kk + 1) * P], k.ident)
                        tr.then_inc(h_turned, 1)
                        pe.wait_ge(hT_ok, n)
                        for half in range(2):
                            for kk in range(DE // P):
                                mm = pe.matmul(k.ps[:, 2 + half, :], hT[:, kk, :],
                                               wd[:, kk, half * 512:(half + 1) * 512],
                                               start=(kk == 0), stop=(kk == DE // P - 1))
                        mm.then_inc(d_done, 1)
                        wait_alone(k, pe, y_ok, n)

        @block.scalar
        def _(act):
            more = act.value_load(r["more"][0:1, 0:1], min_val=0, max_val=1)
            with act.If(more > 0):
                for n in blocks(act):
                    act.wait_ge(x_turned, n)
                    act.activation(xT, k.ps[:, 4:6, :].rearrange("p a (b t) -> p (a b) t", t=P), ACT.Copy)\
                        .then_inc(xT_ok, 1)
                    act.wait_ge(gu_done, n)
                    act.activation(sg, k.ps[:, 0, :], ACT.Silu).then_inc(silu_ok, 1)
                    act.wait_ge(h_turned, n)
                    act.activation(hT, k.ps[:, 6, :].rearrange("p (b t) -> p b t", t=P), ACT.Copy).then_inc(hT_ok, 1)

        @block.vector
        def _(dve):
            more = dve.value_load(r["more"][0:1, 0:1], min_val=0, max_val=1)
            with dve.If(more > 0):
                for n in blocks(dve):
                    dve.wait_ge(silu_ok, n)
                    dve.tensor_tensor(hid, sg, k.ps[:, 1, :], ALU.mult).then_inc(hid_ok, 1)
                    dve.wait_ge(d_done, n)
                    dve.tensor_copy(yo, k.ps[:, 2:4, :].rearrange("p a n -> p (a n)")).then_inc(y_ok, 1)


def combine_stage(k, layer, T, r):
    nc = k.nc
    gate_in, chain, done = k.sem("moe_gate_in"), k.sem("combine_chain"), k.sem("combined")
    y_in = [k.sem(f"pairs_in{s}") for s in range(2)]
    buf = k.big[:, 0:4 * D].rearrange("p (s c d) -> p s c d", s=2, c=2)
    conds = 2 if T > LT else 1
    with k.stage() as block:

        @block.sync
        def _(sp):
            for cond in range(conds):
                sp.dma_start(r["gate"][:, cond, :], k.mod_row(cond, layer, 5)).then_inc(gate_in, 16)
            for t in range(T):
                if t >= 2:
                    sp.wait_ge(done, t - 1)
                for c in range(2):
                    sp.dma_start(buf[:, t % 2, c, :], k.pairs[(c * T + t) * P:(c * T + t + 1) * P, :])\
                        .then_inc(y_in[t % 2], 16)

        @block.vector
        def _(dve):
            link = Chain(dve, chain)
            dve.wait_ge(gate_in, 16 * conds)
            for t in range(T):
                a, b = buf[:, t % 2, 0, :], buf[:, t % 2, 1, :]
                dve.wait_ge(y_in[t % 2], 32 * (t // 2 + 1))
                link(dve.tensor_scalar(a, a, r["wts"][:, 0, t:t + 1], None, ALU.mult))
                link(dve.scalar_tensor_tensor(out=a, in0=b, scalar=r["wts"][:, 1, t:t + 1], in1=a,
                                              op0=ALU.mult, op1=ALU.add))
                link(dve.tensor_tensor(a, a, r["gate"][:, 0 if t < LT else 1, :], ALU.mult))
                dve.tensor_tensor(k.h[:, t, :], k.h[:, t, :], a, ALU.add).then_inc(done, 1)


def moe(k, layer, T, xT_scratch):
    r = moe_views(k)
    norm_stage(k, lambda t: k.h[:, t, :], range(T), k.io["norm2_g"][layer:layer + 1, :], (layer, 4, 3), k.xT,
               k.rw[:, 0:8 * D], rows_out=k.rows)
    router_stage(k, T, r)
    experts_stage(k, layer, T, r)
    more_blocks_stage(k, layer, T, r)
    combine_stage(k, layer, T, r)


def gqa_project_stage(k, g):
    w = k.io["gqa_w_in"][0]
    chunks = [weight_chunk(w, i * 512, 512) for i in range(3)]
    jobs, dsts = [], []
    for c in range(2):
        token_major_jobs(k, c, 512, range(LT), jobs, dsts, lambda t, c=c: g["q"][:, t, c * 512:(c + 1) * 512])
    token_major_jobs(k, 2, 512, range(NT), jobs, dsts, lambda t: g["kv"][:, t, :])
    product_stage(k, "gqkv", chunks, g["ring"], jobs,
                  lambda which, eng, j, ps, link: copy_out(which, eng, dsts[j], ps))


def gqa_rope_stage(k, g):
    nc, io = k.nc, k.io
    KV = 4
    H2 = HD // 2
    g_in, tab, chain, sq, root = k.sem("qk_gain_in"), k.sem("rope_tables"), k.sem("rope_chain"), k.sem("qk_squared"), k.sem("qk_root")
    q_ok, k_ok, v_ok, turned, copied = k.sem("q_roped"), k.sem("k_roped"), k.sem("v_doubled"), k.sem("qk_T"), k.sem("qk_T_copied")
    q, kv = g["q"], g["kv"]
    qh = q.rearrange("p t (h n) -> p t h n", n=HD)
    kh = kv[:, :, 0:KV * HD].rearrange("p t (h n) -> p t h n", n=HD)
    gains = g["small"][:, 0:2 * HD].rearrange("p (a n) -> p a n", a=2)
    tables = g["small"][:, 128:128 + 8 * LT * H2].rearrange("p (a b t n) -> p a b t n", a=2, b=4, t=LT)
    at = 128 + 8 * LT * H2
    sq_q = g["small"][:, at:at + LT * HEADS].rearrange("p (t h) -> p t h", t=LT)
    sq_k = g["small"][:, at + 64:at + 64 + NT * KV].rearrange("p (t h) -> p t h", t=NT)
    tmp = g["tmp"]
    cos = k.const[:, C_COS:C_COS + LT * H2].rearrange("p (t n) -> p t n", t=LT)
    sin = k.const[:, C_SIN:C_SIN + LT * H2].rearrange("p (t n) -> p t n", t=LT)
    sq_buf = tmp[:, 0:LT * D].rearrange("p (t n) -> p t n", t=LT)
    sqk_buf = tmp[:, LT * D:LT * D + NT * KV * HD].rearrange("p (t n) -> p t n", t=NT)

    with k.stage() as block:

        @block.sync
        def _(sp):
            sp.dma_start(gains[:, 0, :], io["gqa_q_norm"].to_broadcast([P, HD])).then_inc(g_in, 16)
            sp.dma_start(gains[:, 1, :], io["gqa_k_norm"].to_broadcast([P, HD])).then_inc(g_in, 16)

        @block.scalar
        def _(act):
            act.activation(sq_buf, q, ACT.Square).then_inc(sq, 1)
            act.activation(sqk_buf, kv[:, :, 0:KV * HD], ACT.Square).then_inc(sq, 1)
            act.wait_ge(root, 2)
            act.activation(sq_q, sq_q, ACT.Sqrt, bias=k.eps, scale=1.0 / HD).then_inc(root, 1)
            act.activation(sq_k, sq_k, ACT.Sqrt, bias=k.eps, scale=1.0 / HD).then_inc(root, 1)
            for i in range(LT + NT):
                act.wait_ge(turned, i + 1)
                if i < NT:
                    act.activation(g["kT"][:, :, i * P:(i + 1) * P],
                                   k.ps[:, 2 * (i % 2), :].rearrange("p (b t) -> p b t", t=P), ACT.Copy)\
                        .then_inc(copied, 1)
                else:
                    t = i - NT
                    act.activation(g["qT"][:, :, t * P:(t + 1) * P],
                                   k.ps[:, 2 * (i % 2):2 * (i % 2) + 2, :].rearrange("p a (b t) -> p (a b) t", t=P),
                                   ACT.Copy).then_inc(copied, 1)

        @block.gpsimd
        def _(pool):
            vh = kv[:, :, KV * HD:2 * KV * HD].rearrange("p t (h n) -> p t h n", n=HD)
            for c in range(2):
                for t in range(NT):
                    op = pool.tensor_copy(g["vd"][:, t, :, c * HD:(c + 1) * HD], vh[:, t])
            op.then_inc(v_ok, 1)

        @block.vector
        def _(dve):
            link = Chain(dve, chain)
            tt = dve.tensor_tensor
            dve.wait_ge(g_in, 32)
            for a in range(2):
                g1 = gains[:, a, 0:H2].unsqueeze(1).to_broadcast([P, LT, H2])
                g2 = gains[:, a, H2:HD].unsqueeze(1).to_broadcast([P, LT, H2])
                for b, (gg, cs) in enumerate(((g1, cos), (g2, sin), (g1, sin), (g2, cos))):
                    link(tt(tables[:, a, b], cs, gg, ALU.mult))
            dve.wait_ge(sq, 2)
            dve.tensor_reduce(sq_q, sq_buf.rearrange("p t (h n) -> p t h n", n=HD), AX.X, ALU.add).then_inc(root, 1)
            dve.tensor_reduce(sq_k, sqk_buf.rearrange("p t (h n) -> p t h n", n=HD), AX.X, ALU.add).then_inc(root, 1)
            dve.wait_ge(root, 4)
            link(dve.reciprocal(sq_k, sq_k))
            link(dve.reciprocal(sq_q, sq_q))
            link(dve.tensor_scalar(sq_q, sq_q, HD ** -0.5, None, ALU.mult))
            for t in range(NT):
                link(tt(kh[:, t], kh[:, t], sq_k[:, t].unsqueeze(2).to_broadcast([P, KV, HD]), ALU.mult))

            def rope(x, out, heads, a, t):
                parts = [tmp[:, b * 512:b * 512 + heads * H2].rearrange("p (h n) -> p h n", h=heads) for b in range(4)]
                x1, x2 = x[:, :, 0:H2], x[:, :, H2:HD]
                for b, xx in enumerate((x1, x2, x1, x2)):
                    link(tt(parts[b], xx, tables[:, a, b, t].unsqueeze(1).to_broadcast([P, heads, H2]), ALU.mult))
                link(tt(out[:, :, 0:H2], parts[0], parts[1], ALU.subtract))
                return tt(out[:, :, H2:HD], parts[2], parts[3], ALU.add)

            for t in range(NT):
                if t < LT:
                    link(rope(kh[:, t], g["kd"][:, t, :, 0:HD], KV, 1, t))
                else:
                    gk = gains[:, 1, :].unsqueeze(1).to_broadcast([P, KV, HD])
                    link(tt(g["kd"][:, t, :, 0:HD], kh[:, t], gk, ALU.mult))
                dve.tensor_copy(g["kd"][:, t, :, HD:2 * HD], g["kd"][:, t, :, 0:HD]).then_inc(k_ok, 1)
            for t in range(LT):
                link(tt(qh[:, t], qh[:, t], sq_q[:, t].unsqueeze(2).to_broadcast([P, HEADS, HD]), ALU.mult))
                rope(qh[:, t], qh[:, t], HEADS, 0, t).then_inc(q_ok, 1)
                dve.wait_ge(q_ok, t + 1)

        @block.tensor
        def _(pe):
            for i in range(LT + NT):
                if i >= 2:
                    pe.wait_ge(copied, i - 1)
                if i < NT:
                    pe.wait_ge(k_ok, i + 1)
                    for c in range(KV):
                        tr = pe.transpose(k.ps[:, 2 * (i % 2), c * P:(c + 1) * P], g["kd"][:, i, c, :], k.ident)
                else:
                    t = i - NT
                    pe.wait_ge(q_ok, t + 1)
                    for c in range(KD):
                        tr = pe.transpose(k.ps[:, 2 * (i % 2) + c // 4, (c % 4) * P:(c % 4 + 1) * P],
                                          q[:, t, c * P:(c + 1) * P], k.ident)
                tr.then_inc(turned, 1)


def layer_even(k):
    norm_stage(k, lambda t: k.h[:, t, :], range(NT), k.io["norm1_g"][0:1, :], (0, 1, 0), k.xT, k.rw[:, 0:8 * D])
    v = ssd_views(k)
    ssd_project_stage(k, v)
    conv_stage(k, v)
    ssd_diagonal_stage(k, v)
    ssd_states_stage(k, v)
    gate_stage(k, v)
    yT = k.r2.rearrange("p (c t) -> p c t", c=KD)
    norm_stage(k, lambda t: v["y"][:, t, :], range(NT), k.io["ssm_norm_g"][0:1, :], None, yT, k.rw[:, 9312:9312 + 8 * D])
    n = {"qT": k.rw[:, 0:6144].rearrange("p (c t) -> p c t", c=KD),
         "v": k.rw[:, 6144:12288].rearrange("p (t n) -> p t n", t=NT),
         "kT": k.r3.rearrange("p (c t) -> p c t", c=KD),
         "ring": [k.rw[:, 12288 + s * 4096:12288 + (s + 1) * 4096] for s in range(2)]}
    na_project_stage(k, n)
    oT = k.rw[:, 12288:18432].rearrange("p (c t) -> p c t", c=KD)
    bias = {"tile": k.rw[:, 18432:18432 + 2 * 14 * GRID].rearrange("p (s r c) -> p s r c", s=2, r=14),
            "mask": k.const[:, C_NAMASK:C_NAMASK + GRID]}
    pt = k.xt_r.rearrange("p (s k t) -> p s k t", s=2, k=NT)
    pt_ctx = k.rw[:, 20224:20224 + 4 * N_CTX].rearrange("p (s k t) -> p s k t", s=2, k=CT)

    def rows_of(ap, h, a, b):
        r = (h % 2) * HD
        return ap[r:r + HD, h // 2, a:b]

    attention_stage(k, "na", lambda h, u: rows_of(n["qT"], h, u * P, (u + 1) * P), lambda h, a, b: rows_of(n["kT"], h, a, b),
                    lambda h, kt: n["v"][:, kt, (h // 2) * P:(h // 2 + 1) * P], oT, CT, bias, pt, pt_ctx)
    output_stage(k, "about", k.io["ab_w_out"][0],
                 lambda kk, t: (yT if kk < KD else oT)[:, kk % KD, t * P:(t + 1) * P], range(NT), 0,
                 [k.rw[:, s * 4096:(s + 1) * 4096] for s in range(3)], k.xt_r)


def layer_odd(k):
    norm_stage(k, lambda t: k.h[:, t, :], range(NT), k.io["norm1_g"][1:2, :], (1, 1, 0), k.xT, k.rw[:, 0:8 * D])
    g = {"q": k.r2[:, 0:4096].rearrange("p (t n) -> p t n", t=LT),
         "kv": k.r3[:, 0:3072].rearrange("p (t n) -> p t n", t=NT),
         "ring": [k.rw[:, 9312 + s * 4096:9312 + (s + 1) * 4096] for s in range(3)],
         "small": k.misc,
         "kd": k.rw[:, 0:3072].rearrange("p (t h n) -> p t h n", t=NT, h=4),
         "vd": k.rw[:, 3072:6144].rearrange("p (t h n) -> p t h n", t=NT, h=4),
         "qT": k.rw[:, 6144:10240].rearrange("p (c t) -> p c t", c=KD),
         "kT": k.rw[:, 10240:13312].rearrange("p (c t) -> p c t", c=4),
         "tmp": k.rw[:, 13312:21600]}
    gqa_project_stage(k, g)
    gqa_rope_stage(k, g)
    oT = k.rw[:, 13312:17408].rearrange("p (c t) -> p c t", c=KD)
    pt = k.xt_r.rearrange("p (s k t) -> p s k t", s=2, k=NT)

    def half(h):
        return slice((h % 2) * HD, (h % 2) * HD + HD)

    attention_stage(k, "gqa", lambda h, u: g["qT"][half(h), h // 2, u * P:(u + 1) * P],
                    lambda h, a, b: g["kT"][half(h), h // 4, a:b], lambda h, kt: g["vd"][:, kt, h // 4, :],
                    oT, 0, None, pt, None)
    output_stage(k, "gqaout", k.io["gqa_w_out"][0], lambda kk, t: oT[:, kk, t * P:(t + 1) * P], range(LT), 1,
                 [k.rw[:, s * 4096:(s + 1) * 4096] for s in range(3)], k.xt_r)


def build(nc, io):
    with ExitStack() as ctx:
        k = Kernel(nc, ctx, io)
        load_stage(k)
        modulation_stage(k)
        layer_even(k)
        moe(k, 0, NT, None)
        layer_odd(k)
        moe(k, 1, LT, None)
        norm_stage(k, lambda t: k.h[:, t, :], range(LT), io["final_g"].rearrange("(a n) -> a n", a=1), None, None,
                   k.rw[:, 0:8 * D], out=io["out"])


def shape_constants():
    import numpy as np
    c = np.zeros((P, C_END), np.float32)
    i, l = np.arange(P)[:, None], np.arange(P)[None, :]
    c[:, C_IDENT:C_IDENT + P] = i == l
    c[:, C_ONES:C_ONES + P] = 1
    c[:, C_TRIF:C_TRIF + P] = i <= l
    c[:, C_TRIB:C_TRIB + P] = i >= l
    c[:, C_TRIS:C_TRIS + P] = i < l
    c[:, C_NEGF:C_NEGF + P] = np.where(i <= l, 0, NEG)
    c[:, C_NEGB:C_NEGB + P] = np.where(i >= l, 0, NEG)
    q, kc = GRID - 1 - np.arange(P)[:, None] % GRID, np.arange(GRID)[None, :]
    start = np.clip(q - 8, 0, GRID - 16)
    c[:, C_NAMASK:C_NAMASK + GRID] = np.where((kc >= start) & (kc < start + 16), 0, NEG)
    c[:, C_TOKID:C_TOKID + NT] = np.arange(P)[:, None] + P * np.arange(NT)[None, :]
    c[:, C_IOTA:C_IOTA + NE] = np.arange(NE)
    c[:, C_EPS] = EPS
    t = np.arange(N_LAT)
    n_freq = HD // 4
    inv = np.float32(10000.0) ** (-np.arange(n_freq, dtype=np.float32) / n_freq)
    ang = np.concatenate([(t // GRID).astype(np.float32)[:, None] * inv, (t % GRID).astype(np.float32)[:, None] * inv], -1)
    for col, f in ((C_COS, np.cos), (C_SIN, np.sin)):
        tab = f(ang).astype(np.float32).reshape(LT, P, HD // 2).transpose(1, 0, 2)
        c[:, col:col + LT * HD // 2] = tab.reshape(P, -1)
    sel = np.zeros((16, 16 * P), np.float32)
    for h in range(16):
        sel[h, h * P:(h + 1) * P] = 1
    return c, sel


_INS = ["x", "c", "ctx", "c_ctx", "w_mod", "b_mod", "norm1_g", "norm2_g", "final_g", "ab_w_in", "ab_w_out",
        "ssm_conv_w", "ssm_conv_b", "ssm_A_log", "ssm_dt_bias", "ssm_D", "ssm_norm_g", "na_rpb", "gqa_w_in",
        "gqa_w_out", "gqa_q_norm", "gqa_k_norm", "router_w", "router_bias", "moe_w_gate", "moe_w_up", "moe_w_down"]


def kernel(**inputs):
    import numpy as _np
    import concourse.bacc as _bacc
    from concourse import mybir as _mybir
    from concourse.bass_utils import run_bass_kernel_spmd as _run

    nc = _bacc.Bacc("TRN2", target_bir_lowering=False, num_devices=1)
    arrays, io = {}, {}
    const, sel = shape_constants()
    for name, a in [(n, inputs[n]) for n in _INS] + [("const", const), ("sel", sel)]:
        a = _np.ascontiguousarray(a)
        arrays[f"in_{name}_dram"] = a
        io[name] = nc.dram_tensor(f"in_{name}_dram", a.shape, _mybir.dt.from_np(a.dtype), kind="ExternalInput").ap()
    out = nc.dram_tensor("out_dram", (N_LAT, D), _mybir.dt.float32, kind="ExternalOutput").ap()
    io["out"] = out
    build(nc, io)
    r = _run(nc, [arrays], core_ids=[0])
    return r.results[0]["out_dram"].reshape(1, N_LAT, D)
```

```python
from contextlib import ExitStack, contextmanager

import concourse.bass as bass
from concourse import mybir

F32 = mybir.dt.float32
F32R = mybir.dt.float32r
BF16 = mybir.dt.bfloat16
I32 = mybir.dt.int32
ALU = mybir.AluOpType
ACT = mybir.ActivationFunctionType
AX = mybir.AxisListType

P = 128
D = 1024
KD = D // P
N_LAT, N_CTX = 512, 256
LT, CT = N_LAT // P, N_CTX // P
NT = LT + CT
TOK = N_LAT + N_CTX
EPS = 1e-6
HEADS, HD = 16, 64
XBC = 1536
O_Z, O_XBC, O_DT, O_Q, O_K, O_V = 0, 1024, 2560, 2592, 3616, 4640
GRID = 64
NEG = -1.0e30
NE, NG, EPG, DE = 32, 8, 4, 512
CAP = TOK
BLK = 128
MOD = 6 * D

C_IDENT, C_ONES, C_TRIF, C_TRIB, C_TRIS, C_NEGF, C_NEGB = [i * P for i in range(7)]
C_NAMASK = 7 * P
C_TOKID = C_NAMASK + GRID
C_IOTA = C_TOKID + NT
C_EPS = C_IOTA + NE
C_COS = C_EPS + 1
C_SIN = C_COS + LT * HD // 2
C_END = (C_SIN + LT * HD // 2 + 7) // 8 * 8
MISC = 4432


def latent_col(t):
    return t * P if t < LT else N_LAT + 4 + (t - LT) * P


CONV_W = N_LAT + 4 + N_CTX
RAW_W = CONV_W + 4


class Chain:

    def __init__(self, eng, sem):
        self.eng, self.sem, self.n = eng, sem, 0

    def __call__(self, ins):
        ins.then_inc(self.sem, 1)
        self.n += 1
        self.eng.wait_ge(self.sem, self.n)


class Kernel:
    def __init__(self, nc, ctx, io):
        self.nc, self.ctx, self.io = nc, ctx, io
        self.n_sems, self.stage_sems, self.old_sems = 0, [], []
        self.passed = nc.alloc_semaphore("loop_wait_passed")
        self.base = (nc.sbuf_base + 31) // 32 * 32
        self.at = 0

        def region(name, n):
            self.at += n
            return ctx.enter_context(nc.sbuf_tensor(name, [P, n], F32))[:, :]

        self.h = region("stream", NT * D).rearrange("p (t d) -> p t d", t=NT)
        self.big_at = self.at
        self.xt_r = region("xt", NT * D)
        self.rw = region("work", 21600)
        self.results_at = self.at
        self.r23 = region("results", 2 * NT * D)
        self.r2, self.r3 = self.r23[:, 0:NT * D], self.r23[:, NT * D:]
        self.const = region("const", C_END)
        self.negb = region("negb", TOK)
        self.identb = region("identb", P // 2)
        self.misc_at = self.at
        self.misc = region("misc", MISC)
        self.ps = ctx.enter_context(nc.psum_tensor("ps", [P, 8, 512], F32))
        c = self.const
        self.ident = c[:, C_IDENT:C_IDENT + P]
        self.ones = c[:, C_ONES:C_ONES + P]
        self.eps = c[:, C_EPS:C_EPS + 1]
        self.xT = self.xt_r.rearrange("p (k t) -> p k t", k=KD)
        dram = nc.dram_tensor
        self.mods = dram("mods", (2, 2 * MOD), F32).ap()
        self.rpb_flat = dram("rpb_flat", (1, HEADS * 15 * 31 + 128), F32).ap()
        self.rows = dram("rows", (TOK, D), F32).ap()
        self.slots = dram("slots", (NE * CAP, 2), I32).ap()
        self.pairs = dram("pairs", (2 * TOK, D), F32).ap()

    def overlay(self, name, start, n, dtype=F32):
        return self.nc.alloc_sbuf_tensor_at(name, [P, n], dtype, offset=self.base + 4 * start)[:, :]

    def sem(self, name):
        self.n_sems += 1
        s = self.nc.alloc_semaphore(f"{name}_{self.n_sems}")
        self.stage_sems.append(s)
        return s

    @contextmanager
    def stage(self):
        if self.old_sems:
            self.nc.clear_and_free_semaphores(self.old_sems)
        self.old_sems, self.stage_sems = self.stage_sems, []
        with self.nc.Block() as block:
            yield block

    def mod_row(self, cond, layer, i):
        o = layer * MOD + i * D
        return self.mods[cond:cond + 1, o:o + D].to_broadcast([P, D])


def load_stage(k):
    nc, io = k.nc, k.io
    loaded, const_in, flat_out, zeroed = k.sem("stream_in"), k.sem("const_in"), k.sem("rpb_flat_out"), k.sem("pad_zeroed")
    zero_out = k.sem("pad_out")
    n = HEADS * 15 * 31
    pad = k.misc[0:1, 0:64]
    with k.stage() as block:

        @block.sync
        def _(sp):
            sp.dma_start(k.const[:, :], io["const"]).then_inc(const_in, 16)
            sp.dma_start(k.h[:, 0:LT, :], io["x"][0].rearrange("(t p) d -> p t d", p=P)).then_inc(loaded, 16)
            sp.dma_start(k.h[:, LT:NT, :], io["ctx"][0].rearrange("(t p) d -> p t d", p=P)).then_inc(loaded, 16)
            sp.dma_start(k.rpb_flat[:, 64:64 + n],
                         io["na_rpb"].rearrange("a h r c -> a (h r c)")).then_inc(flat_out, 16)
            sp.wait_ge(zeroed, 1)
            sp.dma_start(k.rpb_flat[:, 0:64], pad).then_inc(zero_out, 16)
            sp.dma_start(k.rpb_flat[:, 64 + n:128 + n], pad).then_inc(zero_out, 16)
            sp.wait_ge(zero_out, 32)
            sp.wait_ge(flat_out, 16)
            sp.wait_ge(loaded, 32)

        @block.vector
        def _(dve):
            dve.memset(pad, 0.0).then_inc(zeroed, 1)
            dve.wait_ge(const_in, 16)
            dve.tensor_copy(k.identb.bitcast(BF16), k.ident)
            negb = k.negb.bitcast(BF16).rearrange("p (g t l) -> p g t l", g=2, t=NT)
            for g, col in enumerate((C_NEGF, C_NEGB)):
                for t in range(NT):
                    dve.tensor_copy(negb[:, g, t, :], k.const[:, col:col + P])


def modulation_stage(k):
    nc, io = k.nc, k.io
    cond_in, cond_T, cond_ready = k.sem("cond_in"), k.sem("cond_T"), k.sem("cond_ready")
    bias_in, prod_done, added, stored = k.sem("bmod_in"), k.sem("mod_prod"), k.sem("mod_added"), k.sem("mods_out")
    SLOTS, CH = 4, 512
    w_in = [k.sem(f"wmod_in{s}") for s in range(SLOTS)]
    n_chunks = 2 * MOD // CH
    c_rows = k.misc[0:16, 0:P]
    c_cols = k.misc[:, P:P + 16]
    wring = k.rw[:, 0:SLOTS * KD * CH].rearrange("p (s k n) -> p s k n", s=SLOTS, k=KD)
    row = k.r23[0:2, :]
    with k.stage() as block:

        @block.sync
        def _(sp):
            sp.dma_start(c_rows[0:8, :], io["c"].rearrange("a (k p) -> (a k) p", p=P)).then_inc(cond_in, 16)
            sp.dma_start(c_rows[8:16, :], io["c_ctx"].rearrange("(k p) -> k p", p=P)).then_inc(cond_in, 16)
            for cond in range(2):
                sp.dma_start(row[cond:cond + 1, :],
                             io["b_mod"].rearrange("(a l) n -> a (l n)", a=1)).then_inc(bias_in, 16)
            for j in range(n_chunks):
                layer, c0 = divmod(j * CH, MOD)
                if j >= SLOTS:
                    sp.wait_ge(prod_done, j - SLOTS + 1)
                sp.dma_start(wring[:, j % SLOTS],
                             io["w_mod"][layer, :, c0:c0 + CH].rearrange("(k p) n -> p k n", p=P))\
                    .then_inc(w_in[j % SLOTS], 16)
            sp.wait_ge(added, n_chunks)
            sp.dma_start(k.mods, row).then_inc(stored, 16)
            sp.wait_ge(stored, 16)

        @block.scalar
        def _(act):
            act.wait_ge(cond_T, 1)
            act.activation(c_cols, k.ps[:, 7, 0:16], ACT.Silu).then_inc(cond_ready, 1)

        @block.tensor
        def _(pe):
            pe.wait_ge(cond_in, 32)
            pe.transpose(k.ps[:, 7, 0:16], c_rows, k.ident[0:16, 0:16]).then_inc(cond_T, 1)
            pe.wait_ge(cond_ready, 1)
            for j in range(n_chunks):
                pe.wait_ge(w_in[j % SLOTS], 16 * (j // SLOTS + 1))
                if j >= 4:
                    pe.wait_ge(added, j - 3)
                for kk in range(KD):
                    mm = pe.matmul(k.ps[0:2, j % 4, :], c_cols[:, kk:16:8], wring[:, j % SLOTS, kk, :],
                                   start=(kk == 0), stop=(kk == KD - 1))
                mm.then_inc(prod_done, 1)

        @block.vector
        def _(dve):
            dve.wait_ge(bias_in, 32)
            for j in range(n_chunks):
                dve.wait_ge(prod_done, j + 1)
                part = row[:, j * CH:(j + 1) * CH]
                dve.tensor_tensor(part, k.ps[0:2, j % 4, :], part, ALU.add).then_inc(added, 1)


def norm_stage(k, src, tiles, g_row, mod, xT, scratch, rows_out=None, out=None, prefetch=None):
    nc = k.nc
    T = len(tiles)
    g_in, mod_in = k.sem("gain_in"), k.sem("mod_in")
    squared, root, rooted = k.sem("squared"), k.sem("root"), k.sem("rstd")
    rows_ready, gain_ready, chain = k.sem("rows_ready"), k.sem("gain_ready"), k.sem("norm_chain")
    turned, copied = k.sem("turned"), k.sem("turned_copied")
    stored = [k.sem(f"rows_stored{s}") for s in range(2)]
    nr = 2 if mod else 1
    gains = scratch[:, 0:nr * D].rearrange("p (c d) -> p c d", c=nr)
    shifts = scratch[:, 2 * D:4 * D].rearrange("p (c d) -> p c d", c=2)
    g = scratch[:, 4 * D:5 * D] if mod else gains[:, 0, :]
    xn = scratch[:, 5 * D:7 * D].rearrange("p (s d) -> p s d", s=2)
    junk = scratch[:, 7 * D:8 * D]
    stat = k.misc[:, 0:3 * NT].rearrange("p (a t) -> p a t", a=3)
    dst = rows_out if rows_out is not None else out
    with k.stage() as block:

        @block.sync
        def _(sp):
            sp.dma_start(g, g_row.to_broadcast([P, D])).then_inc(g_in, 16)
            if mod:
                for cond in range(2):
                    sp.dma_start(gains[:, cond, :], k.mod_row(cond, mod[0], mod[1])).then_inc(mod_in, 16)
                    sp.dma_start(shifts[:, cond, :], k.mod_row(cond, mod[0], mod[2])).then_inc(mod_in, 16)
            if prefetch:
                prefetch(sp)
            if dst is not None:
                for i, t in enumerate(tiles):
                    sp.wait_ge(rows_ready, i + 1)
                    sp.dma_start(dst[t * P:(t + 1) * P, :], xn[:, i % 2, :]).then_inc(stored[i % 2], 16)
                for s in range(2):
                    sp.wait_ge(stored[s], 16 * (T // 2))

        @block.scalar
        def _(act):
            link = Chain(act, squared)
            for i, t in enumerate(tiles):
                link(act.activation(junk, src(t), ACT.Square, accum_out=stat[:, 0, i:i + 1]))
            act.activation(stat[:, 1, 0:T], stat[:, 0, 0:T], ACT.Sqrt, bias=k.eps, scale=1.0 / D).then_inc(root, 1)
            if xT is not None:
                for i, t in enumerate(tiles):
                    act.wait_ge(turned, i + 1)
                    act.activation(xT[:, :, t * P:(t + 1) * P],
                                   k.ps[:, 2 * (i % 2):2 * (i % 2) + 2, :].rearrange("p a (b c) -> p (a b) c", c=P),
                                   ACT.Copy).then_inc(copied, 1)

        @block.vector
        def _(dve):
            link = Chain(dve, chain)
            dve.wait_ge(g_in, 16)
            if mod:
                dve.wait_ge(mod_in, 64)
                for cond in range(2):
                    dve.scalar_tensor_tensor(out=gains[:, cond, :], in0=gains[:, cond, :], scalar=1.0, in1=g,
                                             op0=ALU.add, op1=ALU.mult).then_inc(gain_ready, 1)
            dve.wait_ge(root, 1)
            dve.reciprocal(stat[:, 2, 0:T], stat[:, 1, 0:T]).then_inc(rooted, 1)
            dve.wait_ge(rooted, 1)
            if mod:
                dve.wait_ge(gain_ready, 2)
            for i, t in enumerate(tiles):
                cond = (0 if t < LT else 1) if mod else 0
                if i >= 2:
                    if xT is not None:
                        dve.wait_ge(turned, i - 1)
                    if dst is not None:
                        dve.wait_ge(stored[i % 2], 16 * (i // 2))
                last = dve.scalar_tensor_tensor(out=xn[:, i % 2, :], in0=src(t), scalar=stat[:, 2, i:i + 1],
                                                in1=gains[:, cond, :], op0=ALU.mult, op1=ALU.mult)
                if mod:
                    link(last)
                    last = dve.tensor_tensor(xn[:, i % 2, :], xn[:, i % 2, :], shifts[:, cond, :], ALU.add)
                last.then_inc(rows_ready, 1)

        if xT is not None:
            @block.tensor
            def _(pe):
                for i in range(T):
                    pe.wait_ge(rows_ready, i + 1)
                    if i >= 2:
                        pe.wait_ge(copied, i - 1)
                    for kk in range(KD):
                        tr = pe.transpose(k.ps[:, 2 * (i % 2) + kk // 4, (kk % 4) * P:(kk % 4 + 1) * P],
                                          xn[:, i % 2, kk * P:(kk + 1) * P], k.ident)
                    tr.then_inc(turned, 1)


def product_stage(k, name, chunks, ring, jobs, evacuate, extra=None):
    nc = k.nc
    R = len(ring)
    w_in = [k.sem(f"{name}_w_in{s}") for s in range(R)]
    prod = k.sem(f"{name}_prod")
    taken = {"v": k.sem(f"{name}_taken_v"), "s": k.sem(f"{name}_taken_s")}
    chain = k.sem(f"{name}_chain")
    extra_in = k.sem(f"{name}_extra_in")
    last_use = [max(j for j, job in enumerate(jobs) if c in job[0]) for c in range(len(chunks))]
    order = [sum(1 for job in jobs[:j + 1] if job[3] == jobs[j][3]) for j in range(len(jobs))]

    def slot(c):
        kk, n = chunks[c].shape[1], chunks[c].shape[2]
        return ring[c % R][:, 0:kk * n].rearrange("p (k n) -> p k n", k=kk)

    with k.stage() as block:

        @block.sync
        def _(sp):
            n_extra = extra(sp, extra_in) if extra else 0
            for c, src in enumerate(chunks):
                if c >= R:
                    sp.wait_ge(prod, max(last_use[:c - R + 1]) + 1)
                sp.dma_start(slot(c), src).then_inc(w_in[c % R], 16)

        @block.tensor
        def _(pe):
            for j, (used, shape, operands, _) in enumerate(jobs):
                for c in used:
                    pe.wait_ge(w_in[c % R], 16 * (c // R + 1))
                for i in range(j - 8, j - 7):
                    if i >= 0:
                        pe.wait_ge(taken[jobs[i][3]], order[i])
                pairs = operands([slot(c) for c in used])
                for i, (lhsT, rhs) in enumerate(pairs):
                    mm = pe.matmul(k.ps[0:shape[0], j % 8, 0:shape[1]], lhsT, rhs,
                                   start=(i == 0), stop=(i == len(pairs) - 1))
                mm.then_inc(prod, 1)

        def take(which, eng):
            link = Chain(eng, chain)
            for j, job in enumerate(jobs):
                if job[3] == which:
                    eng.wait_ge(prod, j + 1)
                    evacuate(which, eng, j, k.ps[0:job[1][0], j % 8, 0:job[1][1]], link)\
                        .then_inc(taken[which], 1)

        @block.scalar
        def _(act):
            take("s", act)

        @block.vector
        def _(dve):
            if extra:
                dve.wait_ge(extra_in, extra.count)
            take("v", dve)


def copy_out(which, eng, dst, src, scale=None):
    if which == "s":
        return eng.activation(dst, src, ACT.Copy, scale=1.0 if scale is None else scale)
    if scale is None:
        return eng.tensor_copy(dst, src)
    return eng.tensor_scalar(dst, src, scale, None, ALU.mult)


def weight_chunk(w, col, n):
    return w[:, col:col + n].rearrange("(k p) n -> p k n", p=P)


def channel_major_jobs(k, chunk, n_tiles, jobs, dsts, dst_of):
    for ct in range(n_tiles):
        for part, (a, b) in enumerate(((0, N_LAT), (N_LAT, TOK))):
            def operands(w, ct=ct, a=a, b=b):
                return [(w[0][:, kk, ct * P:(ct + 1) * P], k.xT[:, kk, a:b]) for kk in range(KD)]
            jobs.append(([chunk], [P, b - a], operands, "vs"[len(jobs) % 2]))
            dsts.append(dst_of(ct, part, a, b))


def token_major_jobs(k, chunk, n, tiles, jobs, dsts, dst_of, engine=None):
    for t in tiles:
        def operands(w, t=t):
            return [(k.xT[:, kk, t * P:(t + 1) * P], w[0][:, kk, 0:n]) for kk in range(KD)]
        jobs.append(([chunk], [P, n], operands, engine or "vs"[len(jobs) % 2]))
        dsts.append(dst_of(t))


def ssd_views(k):
    v = {}
    v["raw"] = k.rw[:, 0:12 * RAW_W].rearrange("p (c n) -> p c n", c=12)
    rest = k.rw[:, 12 * RAW_W:]
    v["ring"] = [rest[:, s * 4096:(s + 1) * 4096] for s in range(3)]
    at = 0

    def part(n):
        nonlocal at
        at += n
        return rest[:, at - n:at]

    v["conv"] = part(2 * CONV_W).rearrange("p (s n) -> p s n", s=2)
    v["btok"] = part(NT * 256).rearrange("p (t n) -> p t n", t=NT)
    v["sel"] = part(16 * P)
    cb_at = at
    v["cb"] = part(2 * TOK).rearrange("p (g n) -> p g n", g=2)
    v["decay"] = part(4 * TOK).rearrange("p (s d n) -> p s d n", s=2, d=2)
    v["xd"] = part(4 * NT * HD).rearrange("p (s d t n) -> p s d t n", s=2, d=2, t=NT)
    sc = rest[:, cb_at:cb_at + 6 * D]
    v["state"] = sc[:, 0:2 * D].rearrange("p (d n) -> p d n", d=2)
    v["xw"] = sc[:, 2 * D:4 * D].rearrange("p (d n) -> p d n", d=2)
    v["yo"] = sc[:, 4 * D:6 * D].rearrange("p (d n) -> p d n", d=2)
    v["xs"] = k.r2.rearrange("p (t n) -> p t n", t=NT)
    v["y"] = k.r3.rearrange("p (t n) -> p t n", t=NT)
    m = k.misc
    at2 = 32

    def small(n):
        nonlocal at2
        at2 += n
        return m[:, at2 - n:at2]

    v["par"] = small(72)
    v["par_rows"] = small(P)[0:72, :]
    v["bc"] = small(80)
    for nm in ("dt", "adt", "nac", "eac", "etot", "wst", "u0", "u1"):
        v[nm] = small(NT * 32).rearrange("p (t n) -> p t n", t=NT)
    v["rowf"] = small(TOK)[0:16, :]
    v["rowb"] = small(TOK)[0:16, :]
    return v


def ssd_project_stage(k, v):
    w = k.io["ab_w_in"][0]
    chunks = [weight_chunk(w, O_XBC + i * 512, 512) for i in range(3)] + [weight_chunk(w, O_DT, 32)]
    jobs, dsts = [], []
    for c in range(3):
        channel_major_jobs(k, c, 4, jobs, dsts,
                           lambda ct, part, a, b, c=c: v["raw"][:, 4 * c + ct, 2 + a + 4 * part:2 + b + 4 * part])
    token_major_jobs(k, 3, 32, range(NT), jobs, dsts, lambda t: v["dt"][:, t, :])
    product_stage(k, "xbc", chunks, v["ring"], jobs,
                  lambda which, eng, j, ps, link: copy_out(which, eng, dsts[j], ps))


def conv_stage(k, v):
    nc, io = k.nc, k.io
    par_in, par_T, par_ok = k.sem("conv_par_in"), k.sem("conv_par_T"), k.sem("conv_par_ready")
    bc_in, sel_in = k.sem("ssd_bc_in"), k.sem("sel_in")
    padded, conved, silued, chain = k.sem("pads_zeroed"), k.sem("conved"), k.sem("silued"), k.sem("conv_chain")
    turned, copied = k.sem("xs_turned"), k.sem("xs_copied")
    aexp, dtv, dte, adt_ok = k.sem("a_exp"), k.sem("dt_abs"), k.sem("dt_exp"), k.sem("adt_ready")
    cum, cum_rows, cum_T, cum_ok, ctot = (k.sem("cum_rows"), k.sem("cum_rows_copied"), k.sem("cum_T"),
                                          k.sem("cum_copied"), k.sem("cum_tot"))
    exps, coef = k.sem("decay_exps"), k.sem("coef")
    raw, conv = v["raw"], v["conv"]
    cw = v["par"][:, 0:60].rearrange("p (w c) -> p w c", w=5)
    cb = v["par"][:, 60:72]
    a_b, dtb_b = v["bc"][:, 0:32], v["bc"][:, 32:64]

    def cols(t):
        return slice(latent_col(t), latent_col(t) + P)

    with k.stage() as block:

        @block.sync
        def _(sp):
            sp.dma_start(v["par_rows"][0:60, :],
                         io["ssm_conv_w"][0].rearrange("w (c p) -> (w c) p", p=P)).then_inc(par_in, 16)
            sp.dma_start(v["par_rows"][60:72, :],
                         io["ssm_conv_b"][0].rearrange("(c p) -> c p", p=P)).then_inc(par_in, 16)
            sp.dma_start(a_b, io["ssm_A_log"].rearrange("a d h -> a (d h)").to_broadcast([P, 32])).then_inc(bc_in, 16)
            sp.dma_start(dtb_b, io["ssm_dt_bias"].rearrange("a d h -> a (d h)").to_broadcast([P, 32]))\
                .then_inc(bc_in, 16)
            sp.dma_start(v["bc"][:, 64:80], io["ssm_D"].to_broadcast([P, 16])).then_inc(bc_in, 16)
            sp.dma_start(v["sel"][0:16, :], io["sel"]).then_inc(sel_in, 16)
            sp.wait_ge(sel_in, 16)

        @block.gpsimd
        def _(pool):
            for c0 in (0, 2 + N_LAT, RAW_W - 2):
                pad = pool.memset(raw[:, :, c0:c0 + (4 if c0 == 2 + N_LAT else 2)], 0.0)
                pad.then_inc(padded, 1)

        @block.vector
        def _(dve):
            link = Chain(dve, chain)
            dve.wait_ge(bc_in, 48)
            bias = dtb_b.unsqueeze(1).to_broadcast([P, NT, 32])
            link(dve.tensor_tensor(v["dt"], v["dt"], bias, ALU.add))
            link(dve.tensor_scalar(v["u0"], v["dt"], -1.0, None, ALU.mult))
            dve.tensor_tensor(v["u0"], v["u0"], v["dt"], ALU.min).then_inc(dtv, 1)
            dve.wait_ge(par_T, 1)
            dve.tensor_copy(v["par"], k.ps[:, 7, 0:72]).then_inc(par_ok, 1)
            dve.wait_ge(par_ok, 1)
            dve.wait_ge(padded, 3)
            dve.wait_ge(dte, 1)
            link(dve.tensor_scalar(v["u1"], v["u0"], 2.0, None, ALU.add))
            link(dve.reciprocal(v["u1"], v["u1"]))
            link(dve.tensor_tensor(v["u0"], v["u0"], v["u1"], ALU.mult))
            link(dve.tensor_tensor(v["u1"], v["u0"], v["u0"], ALU.mult))
            acc = v["adt"]
            link(dve.tensor_scalar(acc, v["u1"], 2.0 / 17, 2.0 / 15, ALU.mult, ALU.add))
            for n in (13, 11, 9, 7, 5, 3, 1):
                link(dve.tensor_tensor(acc, acc, v["u1"], ALU.mult))
                link(dve.tensor_scalar(acc, acc, 2.0 / n, None, ALU.add))
            link(dve.tensor_tensor(acc, acc, v["u0"], ALU.mult))
            link(dve.tensor_scalar(v["dt"], v["dt"], 0.0, None, ALU.max))
            link(dve.tensor_tensor(v["dt"], v["dt"], acc, ALU.add))
            dve.wait_ge(aexp, 1)
            link(dve.tensor_scalar(a_b, a_b, -1.0, None, ALU.mult))
            dve.tensor_tensor(v["adt"], v["dt"], a_b.unsqueeze(1).to_broadcast([P, NT, 32]), ALU.mult)\
                .then_inc(adt_ok, 1)
            for c in range(12):
                if c >= 2:
                    dve.wait_ge(silued, c - 1)
                link(dve.tensor_scalar(conv[:, c % 2, :], raw[:, c, 0:CONV_W], cw[:, 0, c:c + 1], cb[:, c:c + 1],
                                       ALU.mult, ALU.add))
                for w in range(1, 5):
                    last = dve.scalar_tensor_tensor(out=conv[:, c % 2, :], in0=raw[:, c, w:w + CONV_W],
                                                    scalar=cw[:, w, c:c + 1], in1=conv[:, c % 2, :],
                                                    op0=ALU.mult, op1=ALU.add)
                    if w < 4:
                        link(last)
                last.then_inc(conved, 1)
                if c == 2:
                    dve.wait_ge(cum, 4)
                    dve.tensor_copy(v["rowf"][:, 0:512], k.ps[0:16, 4, :])
                    dve.tensor_copy(v["rowf"][:, 512:TOK], k.ps[0:16, 5, 0:256])
                    dve.tensor_copy(v["rowb"][:, 0:512], k.ps[0:16, 6, :])
                    dve.tensor_copy(v["rowb"][:, 512:TOK], k.ps[0:16, 7, 0:256]).then_inc(cum_rows, 1)
                if c == 4:
                    dve.wait_ge(cum_T, 1)
                    dve.wait_ge(ctot, 1)
                    cum_ps = k.ps[:, 4, 0:NT * 32].rearrange("p (t n) -> p t n", t=NT)
                    tot_ps = k.ps[:, 5, 0:NT * 32].rearrange("p (t n) -> p t n", t=NT)
                    link(dve.tensor_scalar(v["nac"], cum_ps, -1.0, None, ALU.mult))
                    link(dve.tensor_tensor(v["wst"], tot_ps, v["nac"], ALU.add))
                    dve.tensor_copy(v["etot"], tot_ps).then_inc(cum_ok, 1)
            dve.wait_ge(exps, 3)
            link(dve.tensor_tensor(v["wst"], v["wst"], v["dt"], ALU.mult))
            for i in range(NT):
                dve.wait_ge(turned, i + 1)
                src = k.ps[:, 2 * (i % 2):2 * (i % 2) + 2, :].rearrange("p a n -> p (a n)")
                dve.tensor_copy(v["xs"][:, i, :], src).then_inc(copied, 1)
            dve.wait_ge(turned, NT + 1)
            dve.tensor_copy(v["btok"], k.ps[:, 4:7, :].rearrange("p a (b n) -> p (a b) n", n=256)).then_inc(copied, 1)

        @block.scalar
        def _(act):
            act.wait_ge(bc_in, 48)
            act.activation(a_b, a_b, ACT.Exp).then_inc(aexp, 1)
            act.wait_ge(dtv, 1)
            act.activation(v["u0"], v["u0"], ACT.Exp).then_inc(dte, 1)
            for c in range(12):
                act.wait_ge(conved, c + 1)
                act.activation(raw[:, c, 0:CONV_W], conv[:, c % 2, :], ACT.Silu).then_inc(silued, 1)
            act.wait_ge(cum_ok, 1)
            act.activation(v["eac"], v["nac"], ACT.Exp, scale=-1.0).then_inc(exps, 1)
            act.activation(v["etot"], v["etot"], ACT.Exp).then_inc(exps, 1)
            act.activation(v["wst"], v["wst"], ACT.Exp).then_inc(exps, 1)

        @block.tensor
        def _(pe):
            pe.wait_ge(par_in, 32)
            pe.transpose(k.ps[:, 7, 0:72], v["par_rows"], k.ident[0:72, 0:72]).then_inc(par_T, 1)
            pe.wait_ge(par_ok, 1)
            pe.wait_ge(adt_ok, 1)
            tri = [k.const[:, C_TRIF:C_TRIF + P], k.const[:, C_TRIB:C_TRIB + P]]
            for d in range(2):
                for half, (t0, t1) in enumerate(((0, LT), (LT, NT))):
                    for t in range(t0, t1):
                        mm = pe.matmul(k.ps[0:16, 4 + 2 * d + half, (t - t0) * P:(t - t0 + 1) * P],
                                       v["adt"][:, t, 16 * d:16 * d + 16], tri[d], start=True, stop=True)
                    mm.then_inc(cum, 1)
            pe.wait_ge(cum_rows, 1)
            for t in range(NT):
                for d, row in enumerate((v["rowf"], v["rowb"])):
                    tr = pe.transpose(k.ps[:, 4, t * 32 + 16 * d:t * 32 + 16 * d + 16], row[:, t * P:(t + 1) * P],
                                      k.ident[0:16, 0:16])
            tr.then_inc(cum_T, 1)
            pe.matmul(k.ps[:, 5, 0:NT * 32], k.ones, v["adt"].rearrange("p t n -> p (t n)"),
                      start=True, stop=True).then_inc(ctot, 1)
            pe.wait_ge(silued, 12)
            for t in range(NT):
                if t >= 2:
                    pe.wait_ge(copied, t - 1)
                for c in range(8):
                    tr = pe.transpose(k.ps[:, 2 * (t % 2) + c // 4, (c % 4) * P:(c % 4 + 1) * P],
                                      raw[:, c, cols(t)], k.ident)
                tr.then_inc(turned, 1)
            pe.wait_ge(cum_ok, 1)
            for t in range(NT):
                for g in range(2):
                    tr = pe.transpose(k.ps[:, 4 + t // 2, (t % 2) * 256 + g * P:(t % 2) * 256 + (g + 1) * P],
                                      raw[:, 8 + g, cols(t)], k.ident)
            tr.then_inc(turned, 1)


def ssd_diagonal_stage(k, v):
    nc = k.nc
    cb_done, cb_ok = k.sem("cb_prod"), k.sem("cb_copied")
    bcast, decayed, scaled, xd_ok = k.sem("cum_bcast"), k.sem("decayed"), k.sem("decay_x_cb"), k.sem("xd_ready")
    yprod, y_ok, chain = k.sem("ydiag_prod"), k.sem("ydiag_taken"), k.sem("ydiag_chain")
    raw = v["raw"]
    rows = (v["rowf"], v["rowb"])
    negb = k.negb.bitcast(BF16).rearrange("p (g n) -> p g n", g=2)
    xs4 = v["xs"].rearrange("p t (h n) -> p t h n", n=HD)
    y4 = v["y"].rearrange("p t (h n) -> p t h n", n=HD)
    NU = 2 * HEADS

    def cum_ps(u):
        return k.ps[:, 2 * (u % 2):2 * (u % 2) + 2, :].rearrange("p a n -> p (a n)")[:, 0:TOK]

    with k.stage() as block:

        @block.tensor
        def _(pe):
            for g in range(2):
                for t in range(NT):
                    c = slice(latent_col(t), latent_col(t) + P)
                    mm = pe.matmul(k.ps[:, 2 * g + t // LT, (t % LT) * P:(t % LT + 1) * P], raw[:, 8 + g, c],
                                   raw[:, 10 + g, c], start=True, stop=True)
                mm.then_inc(cb_done, 1)
            pe.wait_ge(cb_ok, 2)

            def broadcast(u):
                h, d = divmod(u, 2)
                if u >= 2:
                    pe.wait_ge(decayed, u - 1)
                for bank, (a, b) in enumerate(((0, 512), (512, TOK))):
                    out = k.ps[:, 2 * (u % 2) + bank, 0:b - a]
                    pe.matmul(out, v["sel"][0:16, h * P:(h + 1) * P], rows[d][:, a:b], start=True, stop=False)
                    mm = pe.matmul(out, k.identb.bitcast(BF16), negb[:, d, a:b], start=False, stop=True)
                mm.then_inc(bcast, 1)

            broadcast(0)
            broadcast(1)
            for h in range(HEADS):
                if h + 1 < HEADS:
                    broadcast(2 * h + 2)
                    broadcast(2 * h + 3)
                pe.wait_ge(scaled, 2 * h + 2)
                pe.wait_ge(xd_ok, 2 * h + 2)
                if h >= 2:
                    pe.wait_ge(y_ok, h - 1)
                for t in range(NT):
                    for d in range(2):
                        mm = pe.matmul(k.ps[:, 4 + h % 2, t * HD:(t + 1) * HD],
                                       v["decay"][:, h % 2, d, t * P:(t + 1) * P], v["xd"][:, h % 2, d, t, :],
                                       start=(d == 0), stop=(d == 1))
                mm.then_inc(yprod, 1)

        @block.scalar
        def _(act):
            for u in range(NU):
                h, d = divmod(u, 2)
                act.wait_ge(bcast, u + 1)
                if h >= 2:
                    act.wait_ge(yprod, h - 1)
                for t in range(NT):
                    e = act.activation(v["decay"][:, h % 2, d, t * P:(t + 1) * P], cum_ps(u)[:, t * P:(t + 1) * P],
                                       ACT.Exp, bias=v["nac"][:, t, 16 * d + h:16 * d + h + 1])
                e.then_inc(decayed, 1)

        @block.vector
        def _(dve):
            for g in range(2):
                dve.wait_ge(cb_done, g + 1)
                dve.tensor_copy(v["cb"][:, g, :], k.ps[:, 2 * g:2 * g + 2, :].rearrange("p a n -> p (a n)")[:, 0:TOK])\
                    .then_inc(cb_ok, 1)
            dve.wait_ge(cb_ok, 2)

            def take(h):
                dve.wait_ge(yprod, h + 1)
                dve.scalar_tensor_tensor(out=y4[:, :, h, :], in0=xs4[:, :, h, :], scalar=v["bc"][:, 64 + h:65 + h],
                                         in1=k.ps[:, 4 + h % 2, 0:NT * HD].rearrange("p (t n) -> p t n", t=NT),
                                         op0=ALU.mult, op1=ALU.add).then_inc(y_ok, 1)

            for h in range(HEADS):
                for d in range(2):
                    if h >= 2:
                        dve.wait_ge(yprod, h - 1)
                    dt_b = v["dt"][:, :, 16 * d + h:16 * d + h + 1].to_broadcast([P, NT, HD])
                    dve.tensor_tensor(v["xd"][:, h % 2, d, :, :], xs4[:, :, h, :], dt_b, ALU.mult).then_inc(xd_ok, 1)
                    dve.wait_ge(decayed, 2 * h + d + 1)
                    m = v["decay"][:, h % 2, d, :]
                    dve.tensor_tensor(m, m, v["cb"][:, h // 8, :], ALU.mult).then_inc(scaled, 1)
                if h >= 1:
                    take(h - 1)
            take(HEADS - 1)


def ssd_states_stage(k, v):
    nc = k.nc
    weighted, off_prod, st_prod = k.sem("x_weighted"), k.sem("yoff_prod"), k.sem("state_prod")
    state_ok, y_ok, chain = k.sem("state_ready"), k.sem("yoff_taken"), k.sem("state_chain")
    raw, S, xw, yo = v["raw"], v["state"], v["xw"], v["yo"]
    order = [[LT, LT + 1] + list(range(LT)), [LT + 1, LT] + list(range(LT))[::-1]]
    steps = [(i, d) for i in range(NT) for d in range(2)]

    def heads(ap):
        return ap.rearrange("p (h n) -> p h n", n=HD)

    def per_head(coef, t, d):
        return coef[:, t, 16 * d:16 * d + 16].unsqueeze(2).to_broadcast([P, HEADS, HD])

    def off_ps(d):
        return k.ps[:, 4 * d:4 * d + 2, :].rearrange("p a n -> p (a n)")

    def st_ps(d):
        return k.ps[:, 4 * d + 2:4 * d + 4, :].rearrange("p a n -> p (a n)")

    with k.stage() as block:

        @block.tensor
        def _(pe):
            for n, (i, d) in enumerate(steps):
                t = order[d][i]
                c = slice(latent_col(t), latent_col(t) + P)
                if i > 0:
                    pe.wait_ge(state_ok, n - 1)
                    for g in range(2):
                        mm = pe.matmul(k.ps[:, 4 * d + g, :], raw[:, 10 + g, c], S[:, d, g * 512:(g + 1) * 512],
                                       start=True, stop=True)
                    mm.then_inc(off_prod, 1)
                if i < NT - 1:
                    pe.wait_ge(weighted, n + 1)
                    for g in range(2):
                        mm = pe.matmul(k.ps[:, 4 * d + 2 + g, :], v["btok"][:, t, g * P:(g + 1) * P],
                                       xw[:, d, g * 512:(g + 1) * 512], start=True, stop=True)
                    mm.then_inc(st_prod, 1)

        @block.gpsimd
        def _(pool):
            for n, (i, d) in enumerate(steps):
                t = order[d][i]
                if i < NT - 1:
                    if i > 0:
                        pool.wait_ge(st_prod, n - 1)
                    pool.tensor_tensor(heads(xw[:, d, :]), heads(v["xs"][:, t, :]), per_head(v["wst"], t, d),
                                       ALU.mult).then_inc(weighted, 1)

        @block.vector
        def _(dve):
            link = Chain(dve, chain)
            for n, (i, d) in enumerate(steps):
                t = order[d][i]
                if i > 0:
                    dve.wait_ge(off_prod, n - 1)
                    link(dve.tensor_tensor(heads(yo[:, d, :]), heads(off_ps(d)), per_head(v["eac"], t, d), ALU.mult))
                    link(dve.tensor_tensor(v["y"][:, t, :], v["y"][:, t, :], yo[:, d, :], ALU.add))
                if i < NT - 1:
                    dve.wait_ge(st_prod, n + 1)
                    if i == 0:
                        dve.tensor_copy(S[:, d, :], st_ps(d)).then_inc(state_ok, 1)
                    else:
                        link(dve.tensor_tensor(heads(S[:, d, :]), heads(S[:, d, :]), per_head(v["etot"], t, d),
                                               ALU.mult))
                        dve.tensor_tensor(S[:, d, :], S[:, d, :], st_ps(d), ALU.add).then_inc(state_ok, 1)


def gate_stage(k, v):
    w = k.io["ab_w_in"][0]
    chunks = [weight_chunk(w, O_Z + i * 512, 512) for i in range(2)]
    jobs, dsts = [], []
    for c in range(2):
        token_major_jobs(k, c, 512, range(NT), jobs, dsts, lambda t, c=c: (t, c), engine="s")
    z = k.rw[:, 0:6144].rearrange("p (t n) -> p t n", t=NT)
    product_stage(k, "z", chunks, v["ring"], jobs,
                  lambda which, eng, j, ps, link: eng.activation(
                      z[:, dsts[j][0], dsts[j][1] * 512:(dsts[j][1] + 1) * 512], ps, ACT.Silu))
    nc = k.nc
    with k.stage() as block:

        @block.vector
        def _(dve):
            for t in range(0, NT, 2):
                dve.tensor_tensor(v["y"][:, t, :], v["y"][:, t, :], z[:, t, :], ALU.mult)

        @block.gpsimd
        def _(pool):
            for t in range(1, NT, 2):
                pool.tensor_tensor(v["y"][:, t, :], v["y"][:, t, :], z[:, t, :], ALU.mult)


def na_project_stage(k, n):
    w = k.io["ab_w_in"][0]
    chunks = [weight_chunk(w, o + i * 512, 512) for o in (O_Q, O_K, O_V) for i in range(2)]
    jobs, dsts = [], []
    for c in range(4):
        dst = n["qT"] if c < 2 else n["kT"]
        channel_major_jobs(k, c, 4, jobs, dsts,
                           lambda ct, part, a, b, c=c, dst=dst: (dst[:, 4 * (c % 2) + ct, a:b], c < 2, c < 2 and part == 0))
    for c in range(4, 6):
        token_major_jobs(k, c, 512, range(NT), jobs, dsts,
                         lambda t, c=c: (n["v"][:, t, (c - 4) * 512:(c - 3) * 512], False, False))

    def evacuate(which, eng, j, ps, link):
        dst, is_q, latent_q = dsts[j]
        if latent_q:
            dst, ps = backwards(dst), ps.rearrange("p (u t) -> p u t", t=P)
        return copy_out(which, eng, dst, ps, HD ** -0.5 if is_q else None)

    product_stage(k, "naqkv", chunks, n["ring"], jobs, evacuate)


def backwards(ap):
    (ps, pn), (step, n) = ap.ap
    return bass.AP(ap.tensor, ap.offset + (P - 1) * step, [[ps, pn], [P * step, n // P], [-step, P]])


def attention_stage(k, name, qT, kT, vv, oT, n_ctx_units, bias, pt, pt_ctx):
    nc = k.nc
    U = LT + n_ctx_units
    N = HEADS * U
    s_done, mx_done, exp_done, p_ok = k.sem(f"{name}_scores"), k.sem(f"{name}_max"), k.sem(f"{name}_exp"), k.sem(f"{name}_probs")
    turned, pt_ok = k.sem(f"{name}_probs_T"), k.sem(f"{name}_probs_T_copied")
    pv_done, o_ok, chain = k.sem(f"{name}_pv"), k.sem(f"{name}_o_taken"), k.sem(f"{name}_chain")
    chain_act = k.sem(f"{name}_chain_act")
    prob = k.misc[:, 0:3 * TOK].rearrange("p (s n) -> p s n", s=3)
    st = k.misc[:, 3 * TOK:3 * TOK + 18].rearrange("p (s a) -> p s a", s=3)
    bias_in = [k.sem(f"{name}_bias_in{s}") for s in range(2)]
    bias_ok = k.sem(f"{name}_bias_masked")
    groups = []
    for h in range(HEADS):
        groups.append((h, False, h * U + LT - 1))
        if n_ctx_units:
            groups.append((h, True, h * U + U - 1))

    def is_lat(n):
        return n % U < LT

    def scores_ps(n):
        pair = k.ps[:, 2 * (n % 2):2 * (n % 2) + 2, :].rearrange("p a n -> p (a n)")
        return pair[:, 0:TOK] if is_lat(n) else pair[:, N_LAT:TOK]

    def prob_of(n):
        return prob[:, n % 3, 0:TOK] if is_lat(n) else prob[:, n % 3, N_LAT:TOK]

    with k.stage() as block:

        if bias is not None:
            @block.sync
            def _(sp):
                for h in range(HEADS):
                    if h >= 2:
                        sp.wait_ge(mx_done, (h - 2) * U + LT)
                    for r in range(2):
                        base = k.rpb_flat[0:1, 64 + h * 15 * 31 + 31 * (1 - r) + 15 - (GRID - 1):]
                        src = bass.AP(base.tensor, base.offset, [[1, GRID], [31, 14], [1, GRID]])
                        sp.dma_start(bias["tile"][(1 - r) * GRID:(2 - r) * GRID, h % 2, :, :], src)\
                            .then_inc(bias_in[h % 2], 16)

        @block.tensor
        def _(pe):
            def scores(n):
                h, u = divmod(n, U)
                if n >= 2:
                    pe.wait_ge(exp_done, n - 1)
                if is_lat(n):
                    pe.matmul(k.ps[:, 2 * (n % 2), :], qT(h, u), kT(h, 0, N_LAT), start=True, stop=True)
                pe.matmul(k.ps[:, 2 * (n % 2) + 1, 0:N_CTX], qT(h, u), kT(h, N_LAT, TOK), start=True, stop=True)\
                    .then_inc(s_done, 1)

            def turn(n):
                pe.wait_ge(p_ok, n + 1)
                if n >= 1:
                    pe.wait_ge(pt_ok, n)
                keys = NT if is_lat(n) else CT
                for kt in range(keys):
                    tr = pe.transpose(k.ps[:, 4 + kt // 4, (kt % 4) * P:(kt % 4 + 1) * P],
                                      prob_of(n)[:, kt * P:(kt + 1) * P], k.ident)
                tr.then_inc(turned, 1)

            def values(i):
                h, is_ctx, last = groups[i]
                pe.wait_ge(pt_ok, last + 1)
                if i >= 2:
                    pe.wait_ge(o_ok, i - 1)
                keys = CT if is_ctx else NT
                for kt in range(keys):
                    src = pt_ctx[:, h % 2, kt, :] if is_ctx else pt[:, h % 2, kt, :]
                    mm = pe.matmul(k.ps[:, 6 + i % 2, 0:src.shape[1]], vv(h, kt + (LT if is_ctx else 0)), src,
                                   start=(kt == 0), stop=(kt == keys - 1))
                mm.then_inc(pv_done, 1)

            i = 0
            for n in range(N + 4):
                if n < N:
                    scores(n)
                while i < len(groups) and groups[i][2] <= n - 3:
                    values(i)
                    i += 1
                if 2 <= n < N + 2:
                    turn(n - 2)

        @block.scalar
        def _(act):
            for n in range(N + 2):
                if n < N:
                    act.wait_ge(mx_done, n + 1)
                    s = st[:, n % 3, :]
                    if is_lat(n) and bias is not None:
                        act.activation(prob_of(n)[:, 0:N_LAT], prob_of(n)[:, 0:N_LAT], ACT.Exp, bias=s[:, 1:2],
                                       accum_out=s[:, 2:3]).then_inc(chain_act, 1)
                        act.activation(prob_of(n)[:, N_LAT:TOK], scores_ps(n)[:, N_LAT:TOK], ACT.Exp, bias=s[:, 1:2],
                                       accum_out=s[:, 3:4]).then_inc(exp_done, 1)
                    else:
                        act.activation(prob_of(n), scores_ps(n), ACT.Exp, bias=s[:, 1:2],
                                       accum_out=s[:, 2:3]).then_inc(exp_done, 1)
                if n >= 2:
                    m = n - 2
                    h, u = divmod(m, U)
                    act.wait_ge(turned, m + 1)
                    if h >= 2:
                        per = len(groups) // HEADS
                        act.wait_ge(pv_done, per * (h - 2) + (1 if u < LT else per))
                    if is_lat(m):
                        dst = pt[:, h % 2, :, u * P:(u + 1) * P]
                        src = k.ps[:, 4:6, :].rearrange("p a (b n) -> p (a b) n", n=P)[:, 0:NT, :]
                    else:
                        dst = pt_ctx[:, h % 2, :, (u - LT) * P:(u - LT + 1) * P]
                        src = k.ps[:, 4, 0:CT * P].rearrange("p (b n) -> p b n", n=P)
                    act.activation(dst, src, ACT.Copy).then_inc(pt_ok, 1)

        @block.vector
        def _(dve):
            link = Chain(dve, chain)

            def maximum(n):
                h, u = divmod(n, U)
                s = st[:, n % 3, :]
                if u == 0 and bias is not None:
                    dve.wait_ge(bias_in[h % 2], 32 * (h // 2 + 1))
                    tile = bias["tile"][:, h % 2, :, :]
                    mask = bias["mask"].unsqueeze(1).to_broadcast([P, 14, GRID])
                    dve.tensor_tensor(tile, tile, mask, ALU.add).then_inc(bias_ok, 1)
                    dve.wait_ge(bias_ok, h + 1)
                dve.wait_ge(s_done, n + 1)
                if n >= 3:
                    dve.wait_ge(turned, n - 2)
                if is_lat(n) and bias is not None:
                    link(dve.tensor_reduce(s[:, 0:1], scores_ps(n)[:, N_LAT:TOK], AX.X, ALU.max))
                    b = bias["tile"][:, h % 2, 6 - 2 * u:14 - 2 * u, :].rearrange("p r c -> p (r c)")
                    link(dve.tensor_tensor_reduce(prob_of(n)[:, 0:N_LAT], scores_ps(n)[:, 0:N_LAT], b, 1.0,
                                                  s[:, 0:1], ALU.add, ALU.max, s[:, 4:5]))
                    dve.tensor_scalar(s[:, 1:2], s[:, 4:5], -1.0, None, ALU.mult).then_inc(mx_done, 1)
                else:
                    dve.tensor_reduce(s[:, 1:2], scores_ps(n), AX.X, ALU.max, negate=True).then_inc(mx_done, 1)

            def normalise(n):
                s = st[:, n % 3, :]
                dve.wait_ge(exp_done, n + 1)
                if is_lat(n) and bias is not None:
                    dve.wait_ge(chain_act, (n // U) * LT + n % U + 1)
                    link(dve.tensor_tensor(s[:, 2:3], s[:, 2:3], s[:, 3:4], ALU.add))
                link(dve.reciprocal(s[:, 5:6], s[:, 2:3]))
                dve.tensor_scalar(prob_of(n), prob_of(n), s[:, 5:6], None, ALU.mult).then_inc(p_ok, 1)

            def take(i):
                h, is_ctx, _ = groups[i]
                a, b = (N_LAT, N_LAT + N_CTX) if is_ctx else (0, N_LAT)
                r = (h % 2) * HD
                dve.wait_ge(pv_done, i + 1)
                src = k.ps[r:r + HD, 6 + i % 2, 0:b - a]
                if bias is not None and not is_ctx:
                    src = backwards(src)
                dve.tensor_copy(oT[r:r + HD, h // 2, a:b].rearrange("p (u t) -> p u t", t=P),
                                src if len(src.shape) == 3 else src.rearrange("p (u t) -> p u t", t=P)).then_inc(o_ok, 1)

            i = 0
            for n in range(N + 5):
                if n < N:
                    maximum(n)
                if 1 <= n <= N:
                    normalise(n - 1)
                while i < len(groups) and groups[i][2] <= n - 4:
                    take(i)
                    i += 1


def output_stage(k, name, w, lhs_tiles, tiles, layer, ring, scratch):
    n_half = w.shape[0] // (KD * P)
    conds = 2 if len(tiles) > LT else 1
    chunks = [w[a * D:(a + 1) * D, n * 512:(n + 1) * 512].rearrange("(k p) n -> p k n", p=P)
              for n in range(2) for a in range(n_half)]
    gate = scratch[:, 0:2 * D].rearrange("p (c d) -> p c d", c=2)
    tmp = scratch[:, 2 * D:2 * D + 1024].rearrange("p (s n) -> p s n", s=2)
    jobs, where = [], []
    for n in range(2):
        for t in tiles:
            def operands(ws, t=t):
                return [(lhs_tiles(a * KD + kk, t), ws[a][:, kk, :]) for a in range(n_half) for kk in range(KD)]
            jobs.append(([n * n_half + a for a in range(n_half)], [P, 512], operands, "v"))
            where.append((t, n))

    def load_gates(sp, sem):
        for cond in range(conds):
            sp.dma_start(gate[:, cond, :], k.mod_row(cond, layer, 2)).then_inc(sem, 16)
    load_gates.count = 16 * conds

    def evacuate(which, eng, j, ps, link):
        t, n = where[j]
        cols = slice(n * 512, (n + 1) * 512)
        link(eng.tensor_tensor(tmp[:, j % 2, :], ps, gate[:, 0 if t < LT else 1, cols], ALU.mult))
        return eng.tensor_tensor(k.h[:, t, cols], k.h[:, t, cols], tmp[:, j % 2, :], ALU.add)

    product_stage(k, name, chunks, ring, jobs, evacuate, load_gates)


def router_stage(k, T, r):
    nc, io = k.nc, k.io
    rw_in, rb_in = k.sem("router_w_in"), k.sem("router_b_in")
    logit, sig, chain = k.sem("logits"), k.sem("sigmoid"), k.sem("route_chain")
    mask_ok, ranked, dest_ok = k.sem("choice_mask"), k.sem("ranks"), k.sem("slots_known")
    fill_ok, filled, put, idx_in = k.sem("fill_made"), k.sem("table_filled"), k.sem("slots_put"), k.sem("slots_in")
    at = 0

    def part(*shape):
        nonlocal at
        n = 1
        for x in shape:
            n *= x
        at += n
        ap = k.rw[:, at - n:at]
        if len(shape) == 2:
            return ap.rearrange("p (a b) -> p a b", a=shape[0])
        if len(shape) == 3:
            return ap.rearrange("p (a b c) -> p a b c", a=shape[0], b=shape[1])
        return ap

    rw = part(KD, NE)
    rb = part(NE)
    s, sb, prod = part(T, NE), part(T, NE), part(T, NE)
    hi1, hi2, lo1, lo2, gs, gval = [part(T, NG) for _ in range(6)]
    gbest, vmin_g, best, vm1, vm2, wsum = [part(T) for _ in range(6)]
    s_in, b_in, oh1, oh2, val, pr4 = [part(T, EPG) for _ in range(6)]
    e_of = [part(T), part(T)]
    OH = [part(T, NE), part(T, NE)]
    M = part(T, NE)
    rank = [part(T), part(T)]
    dest = part(T, 2).bitcast(I32)
    entry = part(T, 2, 2).bitcast(I32)
    fill = part(NE * CAP // P, 2).bitcast(I32)
    cmax = part(1)
    iota = k.const[:, C_IOTA:C_IOTA + NE]
    tokid = k.const[:, C_TOKID:C_TOKID + T]

    def b2(ap, n):
        return ap.unsqueeze(2).to_broadcast([P, ap.shape[1], n])

    with k.stage() as block:

        @block.sync
        def _(sp):
            sp.dma_start(rw, io["router_w"].rearrange("(k p) e -> p k e", p=P)).then_inc(rw_in, 16)
            sp.dma_start(rb, io["router_bias"].rearrange("(a e) -> a e", a=1).to_broadcast([P, NE])).then_inc(rb_in, 16)
            sp.wait_ge(fill_ok, 2)
            sp.dma_start(k.slots.rearrange("(p n) w -> p n w", p=P), fill).then_inc(filled, 16)
            sp.wait_ge(put, 2 * T * 16)
            sp.dma_start(r["idxs"], k.slots.rearrange("(e c) w -> c e w", c=CAP)[0:P]).then_inc(idx_in, 16)
            sp.wait_ge(idx_in, 16)

        @block.gpsimd
        def _(pool):
            pool.memset(fill[:, :, 0:1], 0).then_inc(fill_ok, 1)
            pool.memset(fill[:, :, 1:2], 4 * TOK).then_inc(fill_ok, 1)
            pool.wait_ge(dest_ok, 2)
            pool.wait_ge(filled, 16)
            for t in range(T):
                for c in range(2):
                    pool.indirect_dma_start(
                        out=k.slots, out_offset=bass.IndirectOffsetOnAxis(ap=dest[:, t, c:c + 1], axis=0),
                        in_=entry[:, t, c, :], in_offset=None).then_inc(put, 16)

        @block.tensor
        def _(pe):
            pe.wait_ge(rw_in, 16)
            for t in range(T):
                for kk in range(KD):
                    mm = pe.matmul(k.ps[:, 7, t * NE:(t + 1) * NE], k.xT[:, kk, t * P:(t + 1) * P], rw[:, kk, :],
                                   start=(kk == 0), stop=(kk == KD - 1))
            mm.then_inc(logit, 1)
            pe.wait_ge(mask_ok, 1)
            for t in range(T):
                for u in range(t + 1):
                    stat = k.const[:, C_TRIS:C_TRIS + P] if u == t else k.ones
                    pe.matmul(k.ps[:, 6, t * NE:(t + 1) * NE], stat, M[:, u, :], start=(u == 0), stop=(u == t))
            for u in range(T):
                mm = pe.matmul(k.ps[:, 5, 0:NE], k.ones, M[:, u, :], start=(u == 0), stop=(u == T - 1))
            mm.then_inc(ranked, 1)

        @block.scalar
        def _(act):
            act.wait_ge(logit, 1)
            act.activation(s, k.ps[:, 7, 0:T * NE].rearrange("p (t e) -> p t e", t=T), ACT.Sigmoid).then_inc(sig, 1)

        @block.vector
        def _(dve):
            link = Chain(dve, chain)
            tt, ts = dve.tensor_tensor, dve.tensor_scalar
            dve.wait_ge(rb_in, 16)
            dve.wait_ge(sig, 1)
            link(tt(sb, s, rb.unsqueeze(1).to_broadcast([P, T, NE]), ALU.add))
            four = sb.rearrange("p t (g j) -> p t g j", j=EPG)
            link(tt(hi1, four[:, :, :, 0], four[:, :, :, 1], ALU.max))
            link(tt(lo1, four[:, :, :, 0], four[:, :, :, 1], ALU.min))
            link(tt(hi2, four[:, :, :, 2], four[:, :, :, 3], ALU.max))
            link(tt(lo2, four[:, :, :, 2], four[:, :, :, 3], ALU.min))
            link(tt(gs, hi1, hi2, ALU.max))
            link(tt(hi1, hi1, hi2, ALU.min))
            link(tt(lo1, lo1, lo2, ALU.max))
            link(tt(hi1, hi1, lo1, ALU.max))
            link(tt(gs, gs, hi1, ALU.add))

            def first_best(values, n, top, val_, vmin, onehot):
                link(dve.tensor_reduce(top, values, AX.X, ALU.max))
                link(tt(val_, values, b2(top, n), ALU.is_equal))
                link(ts(val_, val_, -99.0, None, ALU.mult))
                link(tt(val_, val_, iota[:, 0:n].unsqueeze(1).to_broadcast([P, T, n]), ALU.add))
                link(dve.tensor_reduce(vmin, val_, AX.X, ALU.min))
                link(tt(onehot, val_, b2(vmin, n), ALU.is_equal))

            first_best(gs, NG, gbest, gval, vmin_g, hi2)
            for dst, src in ((b_in, sb), (s_in, s)):
                link(tt(prod.rearrange("p t (g j) -> p t g j", j=EPG), src.rearrange("p t (g j) -> p t g j", j=EPG),
                        hi2.unsqueeze(3).to_broadcast([P, T, NG, EPG]), ALU.mult))
                link(dve.tensor_reduce(dst, prod.rearrange("p t (g j) -> p t j g", j=EPG), AX.X, ALU.add))
            first_best(b_in, EPG, best, val, vm1, oh1)
            link(ts(pr4, oh1, NEG, None, ALU.mult))
            link(tt(b_in, b_in, pr4, ALU.add))
            first_best(b_in, EPG, best, val, vm2, oh2)
            for c, (oh, vm) in enumerate(((oh1, vm1), (oh2, vm2))):
                link(tt(pr4, oh, s_in, ALU.mult))
                link(dve.tensor_reduce(r["wts"][:, c, 0:T], pr4, AX.X, ALU.add))
                link(ts(e_of[c], vmin_g, float(EPG), 99.0 * (EPG + 1), ALU.mult, ALU.add))
                link(tt(e_of[c], e_of[c], vm, ALU.add))
                link(tt(OH[c], b2(e_of[c], NE), iota.unsqueeze(1).to_broadcast([P, T, NE]), ALU.is_equal))
            dve.tensor_tensor(M, OH[0], OH[1], ALU.add).then_inc(mask_ok, 1)
            link(tt(wsum, r["wts"][:, 0, 0:T], r["wts"][:, 1, 0:T], ALU.add))
            link(dve.reciprocal(wsum, wsum))
            for c in range(2):
                link(tt(r["wts"][:, c, 0:T], r["wts"][:, c, 0:T], wsum, ALU.mult))
                link(dve.tensor_copy(entry[:, :, c, 0], tokid))
                link(ts(entry[:, :, c, 1], tokid, float(c * T * P), None, ALU.add))
            dve.wait_ge(ranked, 1)
            for c in range(2):
                link(tt(prod, OH[c], k.ps[:, 6, 0:T * NE].rearrange("p (t e) -> p t e", t=T), ALU.mult))
                link(dve.tensor_reduce(rank[c], prod, AX.X, ALU.add))
                link(ts(e_of[c], e_of[c], float(CAP), None, ALU.mult))
                dve.tensor_tensor(dest[:, :, c], e_of[c], rank[c], ALU.add).then_inc(dest_ok, 1)
            link(dve.tensor_reduce(cmax, k.ps[:, 5, 0:NE], AX.X, ALU.max))
            link(ts(r["more"], cmax, float(BLK) + 0.5, None, ALU.is_gt))


def moe_views(k):
    r = {}
    W = KD * DE
    raw = k.overlay("expert_raw", k.results_at, 3 * W)
    parts = k.overlay("expert_parts", k.big_at, 6 * W, F32R)
    rows = k.overlay("expert_rows", k.big_at + 6 * W, 2 * D)

    def tiles(ap, at, kk, n):
        return ap[:, at:at + kk * n].rearrange("p (k n) -> p k n", k=kk)

    for i, (nm, kk) in enumerate((("wg", KD), ("wu", KD), ("wd", DE // P))):
        r[nm] = tiles(raw, i * W, kk, W // kk)
        r[nm + "_hi"], r[nm + "_lo"] = [tiles(parts, (2 * i + j) * W, kk, W // kk) for j in range(2)]
    r["xb"], r["yo"] = rows[:, 0:D], rows[:, D:2 * D]
    r["hid"] = k.negb[:, 0:DE]
    m = k.misc
    r["idx"] = [m[:, 2 * s:2 * s + 2].bitcast(I32) for s in range(2)]
    r["more"] = m[:, 4:5].bitcast(I32)
    r["wts"] = m[:, 8:8 + 2 * NT].rearrange("p (c t) -> p c t", c=2)
    r["idxs"] = m[:, 32:32 + 2 * NE].bitcast(I32).rearrange("p (e w) -> p e w", w=2)
    turned = k.overlay("expert_rows_T", k.misc_at + 32 + 2 * NE, 4 * D, F32R)
    r["xT"] = [[tiles(turned, (2 * s + j) * D, KD, P) for j in range(2)] for s in range(2)]
    hidden = k.overlay("expert_hidden_T", k.big_at + 6 * W + 2 * D, 2 * DE, F32R)
    r["hT"] = [tiles(hidden, j * DE, DE // P, P) for j in range(2)]
    plain = k.overlay("more_rows_T", k.big_at, D + 2 * DE)
    r["more_xT"], r["more_hT"], r["more_sg"] = tiles(plain, 0, KD, P), tiles(plain, D, DE // P, P), plain[:, D + DE:]
    r["w_in"] = {n: [k.nc.alloc_semaphore(f"{n}{p}_in_{k.n_sems}") for p in range(2)] for n in KINDS}
    r["gate"] = k.xt_r[:, 4 * D:6 * D].rearrange("p (c d) -> p c d", c=2)
    return r


KINDS = ("wg", "wu", "wd")


def load_piece(k, layer, r, eng, n, p, e):
    src = k.io[{"wg": "moe_w_gate", "wu": "moe_w_up", "wd": "moe_w_down"}[n]]
    w = (src[layer, bass.ds(e, 1)] if not isinstance(e, int) else src[layer, e:e + 1])
    half = r[n].shape[1] // 2
    eng.dma_start(r[n][:, p * half:(p + 1) * half, :],
                  w.rearrange("a (k p) n -> p (a k) n", p=P)[:, p * half:(p + 1) * half, :]).then_inc(r["w_in"][n][p], 16)


THREE = ((0, 0), (0, 1), (1, 0))


def split_products(pe, out, stat, move, first=True, last=True):
    for i, (a, b) in enumerate(THREE):
        mm = pe.matmul(out, stat[a], move[b], start=(first and i == 0), stop=(last and i == 2))
    return mm


def expert_loop(eng):
    for e in (0, 1):
        yield 0, e, e
    with eng.Fori(1, NE // 2 - 1) as i:
        yield i, 0, 2 * i
        yield i, 1, 2 * i + 1
    for e in (NE - 2, NE - 1):
        yield NE // 2 - 1, e % 2, e


def wait_from(eng, sem, n):
    if not isinstance(n, int) or n > 0:
        eng.wait_ge(sem, n)


def wait_alone(k, eng, sem, n):
    wait_from(eng, sem, n)
    if not isinstance(n, int):
        eng.sem_inc(k.passed, 1)


def gather_rows(k, pool, dst, idx):
    return pool.indirect_dma_start(out=dst, out_offset=None, in_=k.rows,
                                   in_offset=bass.IndirectOffsetOnAxis(ap=idx[:, 0:1], axis=0),
                                   bounds_check=TOK - 1, oob_is_err=False)


def scatter_rows(k, pool, T, src, idx):
    return pool.indirect_dma_start(out=k.pairs, out_offset=bass.IndirectOffsetOnAxis(ap=idx[:, 1:2], axis=0),
                                   in_=src, in_offset=None, bounds_check=2 * T * P - 1, oob_is_err=False)


def experts_stage(k, layer, T, r):
    nc = k.nc
    hi_ok = {n: k.sem(f"{n}_high") for n in KINDS}
    lo_ok = {n: k.sem(f"{n}_low") for n in KINDS}
    used = {n: k.sem(f"{n}_prod") for n in KINDS}
    x_in, y_out = k.sem("rows_in"), k.sem("pair_rows_out")
    x_turned, xhi_ok, xT_ok, silu_ok, hid_ok = (k.sem("rows_T"), k.sem("rows_T_high"), k.sem("rows_T_low"),
                                                k.sem("gate_silu"), k.sem("hidden"))
    h_turned, hhi_ok, hT_ok, y_ok, idx_ok = (k.sem("hidden_T"), k.sem("hidden_T_high"), k.sem("hidden_T_low"),
                                             k.sem("y_copied"), k.sem("idx_staged"))

    def is_last(e, ahead=0):
        return isinstance(e, int) and e + ahead >= NE - 1

    def piece(ap, p):
        half = ap.shape[1] // 2
        return ap[:, p * half:(p + 1) * half]

    x_ps = k.ps[:, 4:6, :].rearrange("p a (b t) -> p (a b) t", t=P)
    h_ps = k.ps[:, 6, :].rearrange("p (b t) -> p b t", t=P)

    with k.stage() as block:
        k.stage_sems += [s for n in KINDS for s in r["w_in"][n]]

        @block.sync
        def _(sp):
            def load(n, p, e):
                sp.wait_ge(lo_ok[n], 2 * e - 1 + p)
                load_piece(k, layer, r, sp, n, p, e)

            for p in range(2):
                load("wg", p, 1)
            for i, s, e in expert_loop(sp):
                if not is_last(e):
                    for p in range(2):
                        load("wu", p, e + 1)
                    if not is_last(e, 1):
                        for p in range(2):
                            load("wg", p, e + 2)
                    for p in range(2):
                        load("wd", p, e + 1)

        @block.gpsimd
        def _(pool):
            def stage_index(slot, count, e):
                at = r["idxs"][:, e, :] if isinstance(e, int) else r["idxs"][:, bass.ds(e, 1), :].rearrange("p a w -> p (a w)")
                pool.tensor_copy(r["idx"][slot], at).then_inc(idx_ok, 1)
                wait_alone(k, pool, idx_ok, count)

            def fetch(e):
                wait_alone(k, pool, x_in, 16 * e)
                stage_index(0, e + 1 if isinstance(e, int) and e < 2 else 2 * e - 1, e)
                wait_alone(k, pool, x_turned, e)
                gather_rows(k, pool, r["xb"], r["idx"][0]).then_inc(x_in, 16)

            fetch(0)
            fetch(1)
            for i, s, e in expert_loop(pool):
                if not is_last(e, 1):
                    fetch(e + 2)
                wait_alone(k, pool, y_out, 16 * e)
                stage_index(1, NE + e + 1 if is_last(e, 1) else 2 * e + 4, e)
                wait_alone(k, pool, y_ok, e + 1)
                scatter_rows(k, pool, T, r["yo"], r["idx"][1]).then_inc(y_out, 16)
            pool.wait_ge(y_out, 16 * NE)

        @block.tensor
        def _(pe):
            def turn_rows(e):
                pe.wait_ge(x_in, 16 * e + 16)
                wait_from(pe, xT_ok, e)
                for kk in range(KD):
                    tr = pe.transpose(k.ps[:, 4 + kk // 4, (kk % 4) * P:(kk % 4 + 1) * P],
                                      r["xb"][:, kk * P:(kk + 1) * P], k.ident)
                tr.then_inc(x_turned, 1)

            def gate_up(n, p, s, e):
                pe.wait_ge(lo_ok[n], 2 * e + 1 + p)
                for kk in range(p * KD // 2, (p + 1) * KD // 2):
                    mm = split_products(pe, k.ps[:, 0 if n == "wg" else 1, :], [x[:, kk, :] for x in r["xT"][s]],
                                        (r[n + "_hi"][:, kk, :], r[n + "_lo"][:, kk, :]), kk == 0, kk == KD - 1)
                mm.then_inc(used[n], 1)

            turn_rows(0)
            pe.wait_ge(xT_ok, 1)
            for p in range(2):
                gate_up("wg", p, 0, 0)
            turn_rows(1)
            for i, s, e in expert_loop(pe):
                wait_from(pe, hid_ok, e)
                for p in range(2):
                    gate_up("wu", p, s, e)
                if not is_last(e):
                    pe.wait_ge(silu_ok, e + 1)
                    pe.wait_ge(xT_ok, e + 2)
                    gate_up("wg", 0, 1 - s, e + 1)
                pe.wait_ge(hid_ok, e + 1)
                for kk in range(DE // P):
                    tr = pe.transpose(k.ps[:, 6, kk * P:(kk + 1) * P], r["hid"][:, kk * P:(kk + 1) * P], k.ident)
                tr.then_inc(h_turned, 1)
                if not is_last(e):
                    gate_up("wg", 1, 1 - s, e + 1)
                if not is_last(e, 1):
                    turn_rows(e + 2)
                wait_from(pe, y_ok, e)
                pe.wait_ge(hT_ok, e + 1)
                for p in range(2):
                    pe.wait_ge(lo_ok["wd"], 2 * e + 1 + p)
                    for half in range(2):
                        c = slice(half * 512, (half + 1) * 512)
                        for kk in range(p * DE // P // 2, (p + 1) * DE // P // 2):
                            mm = split_products(pe, k.ps[:, 2 + half, :], [x[:, kk, :] for x in r["hT"]],
                                                (r["wd_hi"][:, kk, c], r["wd_lo"][:, kk, c]),
                                                kk == 0, kk == DE // P - 1)
                    mm.then_inc(used["wd"], 1)

        @block.scalar
        def _(act):
            def high(n, p, e):
                act.wait_ge(r["w_in"][n][p], 16 * (e + 1))
                wait_from(act, used[n], 2 * e - 1 + p)
                act.activation(piece(r[n + "_hi"], p), piece(r[n], p), ACT.Copy).then_inc(hi_ok[n], 1)

            def high_rows_T(s, e):
                act.wait_ge(x_turned, e + 1)
                act.activation(r["xT"][s][0], x_ps, ACT.Copy).then_inc(xhi_ok, 1)

            def copy_y(e):
                act.wait_ge(used["wd"], 2 * e + 2)
                wait_from(act, y_out, 16 * e)
                act.activation(r["yo"], k.ps[:, 2:4, :].rearrange("p a n -> p (a n)"), ACT.Copy).then_inc(y_ok, 1)

            def silu(e):
                act.wait_ge(used["wg"], 2 * e + 2)
                wait_from(act, h_turned, e)
                act.activation(r["hid"], k.ps[:, 0, :], ACT.Silu).then_inc(silu_ok, 1)

            high("wg", 0, 0)
            high_rows_T(0, 0)
            for n, p, e in (("wg", 1, 0), ("wu", 0, 0), ("wu", 1, 0)):
                high(n, p, e)
            high_rows_T(1, 1)
            high("wg", 0, 1)
            silu(0)
            high("wg", 1, 1)
            for i, s, e in expert_loop(act):
                for p in range(2):
                    high("wd", p, e)
                if not is_last(e):
                    high("wu", 0, e + 1)
                act.wait_ge(h_turned, e + 1)
                act.activation(r["hT"][0], h_ps, ACT.Copy).then_inc(hhi_ok, 1)
                if not is_last(e):
                    high("wu", 1, e + 1)
                    silu(e + 1)
                if not is_last(e, 1):
                    high_rows_T(s, e + 2)
                    for p in range(2):
                        high("wg", p, e + 2)
                copy_y(e)

        @block.vector
        def _(dve):
            def low(n, p, e):
                dve.wait_ge(hi_ok[n], 2 * e + 1 + p)
                dve.tensor_tensor(piece(r[n + "_lo"], p), piece(r[n], p), piece(r[n + "_hi"], p).bitcast(F32),
                                  ALU.subtract).then_inc(lo_ok[n], 1)

            def low_rows_T(s, e):
                dve.wait_ge(xhi_ok, e + 1)
                dve.tensor_tensor(r["xT"][s][1], x_ps, r["xT"][s][0].bitcast(F32), ALU.subtract).then_inc(xT_ok, 1)

            low("wg", 0, 0)
            low_rows_T(0, 0)
            for n, p, e in (("wg", 1, 0), ("wu", 0, 0), ("wu", 1, 0)):
                low(n, p, e)
            low_rows_T(1, 1)
            for p in range(2):
                low("wg", p, 1)
            for i, s, e in expert_loop(dve):
                for p in range(2):
                    low("wd", p, e)
                dve.wait_ge(silu_ok, e + 1)
                dve.wait_ge(used["wu"], 2 * e + 2)
                dve.tensor_tensor(r["hid"], r["hid"], k.ps[:, 1, :], ALU.mult).then_inc(hid_ok, 1)
                if not is_last(e):
                    low("wu", 0, e + 1)
                dve.wait_ge(hhi_ok, e + 1)
                dve.tensor_tensor(r["hT"][1], h_ps, r["hT"][0].bitcast(F32), ALU.subtract).then_inc(hT_ok, 1)
                if not is_last(e):
                    low("wu", 1, e + 1)
                if not is_last(e, 1):
                    low_rows_T(s, e + 2)
                    for p in range(2):
                        low("wg", p, e + 2)


def more_blocks_stage(k, layer, T, r):
    nc, io = k.nc, k.io
    w_in, idx_in, x_in, y_out = k.sem("more_w_in"), k.sem("more_idx_in"), k.sem("more_rows_in"), k.sem("more_pairs_out")
    gu_done, d_done, x_turned, xT_ok = k.sem("more_gu"), k.sem("more_down"), k.sem("more_rows_T"), k.sem("more_rows_T_copied")
    silu_ok, hid_ok, h_turned, hT_ok, y_ok = (k.sem("more_silu"), k.sem("more_hidden"), k.sem("more_hidden_T"),
                                              k.sem("more_hidden_T_copied"), k.sem("more_y"))
    J = T * P // BLK - 1
    wg, wu, wd, yo, hid, xb, idx = [r[n] for n in ("wg", "wu", "wd", "yo", "hid", "xb")] + [r["idx"][0]]
    xT, hT, sg = r["more_xT"], r["more_hT"], r["more_sg"]

    def blocks(eng):
        with eng.Fori(0, NE) as e:
            with eng.Fori(0, J) as j:
                yield e * J + j + 1

    with k.stage() as block:

        @block.sync
        def _(sp):
            more = sp.value_load(r["more"][0:1, 0:1], min_val=0, max_val=1)
            with sp.If(more > 0):
                with sp.Fori(0, NE) as e:
                    for dst, src in ((wg, io["moe_w_gate"]), (wu, io["moe_w_up"]), (wd, io["moe_w_down"])):
                        sp.dma_start(dst, src[layer, bass.ds(e, 1)].rearrange("a (k p) n -> p (a k) n", p=P))\
                            .then_inc(w_in, 16)
                    with sp.Fori(0, J) as j:
                        n = e * J + j + 1
                        sp.dma_start(idx, k.slots[bass.ds(e * CAP + j * BLK + BLK, P), :]).then_inc(idx_in, 16)
                        wait_alone(k, sp, y_out, 16 * n)

        @block.gpsimd
        def _(pool):
            more = pool.value_load(r["more"][0:1, 0:1], min_val=0, max_val=1)
            with pool.If(more > 0):
                for n in blocks(pool):
                    wait_alone(k, pool, idx_in, 16 * n)
                    gather_rows(k, pool, xb, idx).then_inc(x_in, 16)
                    wait_alone(k, pool, y_ok, n)
                    scatter_rows(k, pool, T, yo, idx).then_inc(y_out, 16)
                    wait_alone(k, pool, y_out, 16 * n)

        @block.tensor
        def _(pe):
            more = pe.value_load(r["more"][0:1, 0:1], min_val=0, max_val=1)
            with pe.If(more > 0):
                with pe.Fori(0, NE) as e:
                    wait_alone(k, pe, w_in, 48 * e + 48)
                    with pe.Fori(0, J) as j:
                        n = e * J + j + 1
                        pe.wait_ge(x_in, 16 * n)
                        for kk in range(KD):
                            tr = pe.transpose(k.ps[:, 4 + kk // 4, (kk % 4) * P:(kk % 4 + 1) * P],
                                              xb[:, kk * P:(kk + 1) * P], k.ident)
                        tr.then_inc(x_turned, 1)
                        pe.wait_ge(xT_ok, n)
                        for bank, w in ((0, wg), (1, wu)):
                            for kk in range(KD):
                                mm = pe.matmul(k.ps[:, bank, :], xT[:, kk, :], w[:, kk, :],
                                               start=(kk == 0), stop=(kk == KD - 1))
                        mm.then_inc(gu_done, 1)
                        pe.wait_ge(hid_ok, n)
                        for kk in range(DE // P):
                            tr = pe.transpose(k.ps[:, 6, kk * P:(kk + 1) * P], hid[:, kk * P:(kk + 1) * P], k.ident)
                        tr.then_inc(h_turned, 1)
                        pe.wait_ge(hT_ok, n)
                        for half in range(2):
                            for kk in range(DE // P):
                                mm = pe.matmul(k.ps[:, 2 + half, :], hT[:, kk, :],
                                               wd[:, kk, half * 512:(half + 1) * 512],
                                               start=(kk == 0), stop=(kk == DE // P - 1))
                        mm.then_inc(d_done, 1)
                        wait_alone(k, pe, y_ok, n)

        @block.scalar
        def _(act):
            more = act.value_load(r["more"][0:1, 0:1], min_val=0, max_val=1)
            with act.If(more > 0):
                for n in blocks(act):
                    act.wait_ge(x_turned, n)
                    act.activation(xT, k.ps[:, 4:6, :].rearrange("p a (b t) -> p (a b) t", t=P), ACT.Copy)\
                        .then_inc(xT_ok, 1)
                    act.wait_ge(gu_done, n)
                    act.activation(sg, k.ps[:, 0, :], ACT.Silu).then_inc(silu_ok, 1)
                    act.wait_ge(h_turned, n)
                    act.activation(hT, k.ps[:, 6, :].rearrange("p (b t) -> p b t", t=P), ACT.Copy).then_inc(hT_ok, 1)

        @block.vector
        def _(dve):
            more = dve.value_load(r["more"][0:1, 0:1], min_val=0, max_val=1)
            with dve.If(more > 0):
                for n in blocks(dve):
                    dve.wait_ge(silu_ok, n)
                    dve.tensor_tensor(hid, sg, k.ps[:, 1, :], ALU.mult).then_inc(hid_ok, 1)
                    dve.wait_ge(d_done, n)
                    dve.tensor_copy(yo, k.ps[:, 2:4, :].rearrange("p a n -> p (a n)")).then_inc(y_ok, 1)


def combine_stage(k, layer, T, r):
    nc = k.nc
    gate_in, chain, done = k.sem("moe_gate_in"), k.sem("combine_chain"), k.sem("combined")
    y_in = [k.sem(f"pairs_in{s}") for s in range(2)]
    buf = k.xt_r[:, 0:4 * D].rearrange("p (s c d) -> p s c d", s=2, c=2)
    conds = 2 if T > LT else 1
    with k.stage() as block:

        @block.sync
        def _(sp):
            for cond in range(conds):
                sp.dma_start(r["gate"][:, cond, :], k.mod_row(cond, layer, 5)).then_inc(gate_in, 16)
            for t in range(T):
                if t >= 2:
                    sp.wait_ge(done, t - 1)
                for c in range(2):
                    sp.dma_start(buf[:, t % 2, c, :], k.pairs[(c * T + t) * P:(c * T + t + 1) * P, :])\
                        .then_inc(y_in[t % 2], 16)

        @block.vector
        def _(dve):
            link = Chain(dve, chain)
            dve.wait_ge(gate_in, 16 * conds)
            for t in range(T):
                a, b = buf[:, t % 2, 0, :], buf[:, t % 2, 1, :]
                dve.wait_ge(y_in[t % 2], 32 * (t // 2 + 1))
                link(dve.tensor_scalar(a, a, r["wts"][:, 0, t:t + 1], None, ALU.mult))
                link(dve.scalar_tensor_tensor(out=a, in0=b, scalar=r["wts"][:, 1, t:t + 1], in1=a,
                                              op0=ALU.mult, op1=ALU.add))
                link(dve.tensor_tensor(a, a, r["gate"][:, 0 if t < LT else 1, :], ALU.mult))
                dve.tensor_tensor(k.h[:, t, :], k.h[:, t, :], a, ALU.add).then_inc(done, 1)


def moe(k, layer, T, xT_scratch):
    r = moe_views(k)

    def first_expert(sp):
        for n in KINDS:
            for p in range(2):
                load_piece(k, layer, r, sp, n, p, 0)

    norm_stage(k, lambda t: k.h[:, t, :], range(T), k.io["norm2_g"][layer:layer + 1, :], (layer, 4, 3), k.xT,
               k.rw[:, 0:8 * D], rows_out=k.rows, prefetch=first_expert)
    router_stage(k, T, r)
    experts_stage(k, layer, T, r)
    more_blocks_stage(k, layer, T, r)
    combine_stage(k, layer, T, r)


def gqa_project_stage(k, g):
    w = k.io["gqa_w_in"][0]
    chunks = [weight_chunk(w, i * 512, 512) for i in range(3)]
    jobs, dsts = [], []
    for c in range(2):
        token_major_jobs(k, c, 512, range(LT), jobs, dsts, lambda t, c=c: g["q"][:, t, c * 512:(c + 1) * 512])
    token_major_jobs(k, 2, 512, range(NT), jobs, dsts, lambda t: g["kv"][:, t, :])
    product_stage(k, "gqkv", chunks, g["ring"], jobs,
                  lambda which, eng, j, ps, link: copy_out(which, eng, dsts[j], ps))


def gqa_rope_stage(k, g):
    nc, io = k.nc, k.io
    KV = 4
    H2 = HD // 2
    g_in, tab, chain, sq, root = k.sem("qk_gain_in"), k.sem("rope_tables"), k.sem("rope_chain"), k.sem("qk_squared"), k.sem("qk_root")
    q_ok, k_ok, v_ok, turned, copied = k.sem("q_roped"), k.sem("k_roped"), k.sem("v_doubled"), k.sem("qk_T"), k.sem("qk_T_copied")
    q, kv = g["q"], g["kv"]
    qh = q.rearrange("p t (h n) -> p t h n", n=HD)
    kh = kv[:, :, 0:KV * HD].rearrange("p t (h n) -> p t h n", n=HD)
    gains = g["small"][:, 0:2 * HD].rearrange("p (a n) -> p a n", a=2)
    tables = g["small"][:, 128:128 + 8 * LT * H2].rearrange("p (a b t n) -> p a b t n", a=2, b=4, t=LT)
    at = 128 + 8 * LT * H2
    sq_q = g["small"][:, at:at + LT * HEADS].rearrange("p (t h) -> p t h", t=LT)
    sq_k = g["small"][:, at + 64:at + 64 + NT * KV].rearrange("p (t h) -> p t h", t=NT)
    tmp = g["tmp"]
    cos = k.const[:, C_COS:C_COS + LT * H2].rearrange("p (t n) -> p t n", t=LT)
    sin = k.const[:, C_SIN:C_SIN + LT * H2].rearrange("p (t n) -> p t n", t=LT)
    sq_buf = tmp[:, 0:LT * D].rearrange("p (t n) -> p t n", t=LT)
    sqk_buf = tmp[:, LT * D:LT * D + NT * KV * HD].rearrange("p (t n) -> p t n", t=NT)

    with k.stage() as block:

        @block.sync
        def _(sp):
            sp.dma_start(gains[:, 0, :], io["gqa_q_norm"].to_broadcast([P, HD])).then_inc(g_in, 16)
            sp.dma_start(gains[:, 1, :], io["gqa_k_norm"].to_broadcast([P, HD])).then_inc(g_in, 16)

        @block.scalar
        def _(act):
            act.activation(sq_buf, q, ACT.Square).then_inc(sq, 1)
            act.activation(sqk_buf, kv[:, :, 0:KV * HD], ACT.Square).then_inc(sq, 1)
            act.wait_ge(root, 2)
            act.activation(sq_q, sq_q, ACT.Sqrt, bias=k.eps, scale=1.0 / HD).then_inc(root, 1)
            act.activation(sq_k, sq_k, ACT.Sqrt, bias=k.eps, scale=1.0 / HD).then_inc(root, 1)
            for i in range(LT + NT):
                act.wait_ge(turned, i + 1)
                if i < NT:
                    act.activation(g["kT"][:, :, i * P:(i + 1) * P],
                                   k.ps[:, 2 * (i % 2), :].rearrange("p (b t) -> p b t", t=P), ACT.Copy)\
                        .then_inc(copied, 1)
                else:
                    t = i - NT
                    act.activation(g["qT"][:, :, t * P:(t + 1) * P],
                                   k.ps[:, 2 * (i % 2):2 * (i % 2) + 2, :].rearrange("p a (b t) -> p (a b) t", t=P),
                                   ACT.Copy).then_inc(copied, 1)

        @block.gpsimd
        def _(pool):
            vh = kv[:, :, KV * HD:2 * KV * HD].rearrange("p t (h n) -> p t h n", n=HD)
            for c in range(2):
                for t in range(NT):
                    op = pool.tensor_copy(g["vd"][:, t, :, c * HD:(c + 1) * HD], vh[:, t])
            op.then_inc(v_ok, 1)

        @block.vector
        def _(dve):
            link = Chain(dve, chain)
            tt = dve.tensor_tensor
            dve.wait_ge(g_in, 32)
            for a in range(2):
                g1 = gains[:, a, 0:H2].unsqueeze(1).to_broadcast([P, LT, H2])
                g2 = gains[:, a, H2:HD].unsqueeze(1).to_broadcast([P, LT, H2])
                for b, (gg, cs) in enumerate(((g1, cos), (g2, sin), (g1, sin), (g2, cos))):
                    link(tt(tables[:, a, b], cs, gg, ALU.mult))
            dve.wait_ge(sq, 2)
            dve.tensor_reduce(sq_q, sq_buf.rearrange("p t (h n) -> p t h n", n=HD), AX.X, ALU.add).then_inc(root, 1)
            dve.tensor_reduce(sq_k, sqk_buf.rearrange("p t (h n) -> p t h n", n=HD), AX.X, ALU.add).then_inc(root, 1)
            dve.wait_ge(root, 4)
            link(dve.reciprocal(sq_k, sq_k))
            link(dve.reciprocal(sq_q, sq_q))
            link(dve.tensor_scalar(sq_q, sq_q, HD ** -0.5, None, ALU.mult))
            for t in range(NT):
                link(tt(kh[:, t], kh[:, t], sq_k[:, t].unsqueeze(2).to_broadcast([P, KV, HD]), ALU.mult))

            def rope(x, out, heads, a, t):
                parts = [tmp[:, b * 512:b * 512 + heads * H2].rearrange("p (h n) -> p h n", h=heads) for b in range(4)]
                x1, x2 = x[:, :, 0:H2], x[:, :, H2:HD]
                for b, xx in enumerate((x1, x2, x1, x2)):
                    link(tt(parts[b], xx, tables[:, a, b, t].unsqueeze(1).to_broadcast([P, heads, H2]), ALU.mult))
                link(tt(out[:, :, 0:H2], parts[0], parts[1], ALU.subtract))
                return tt(out[:, :, H2:HD], parts[2], parts[3], ALU.add)

            for t in range(NT):
                if t < LT:
                    link(rope(kh[:, t], g["kd"][:, t, :, 0:HD], KV, 1, t))
                else:
                    gk = gains[:, 1, :].unsqueeze(1).to_broadcast([P, KV, HD])
                    link(tt(g["kd"][:, t, :, 0:HD], kh[:, t], gk, ALU.mult))
                dve.tensor_copy(g["kd"][:, t, :, HD:2 * HD], g["kd"][:, t, :, 0:HD]).then_inc(k_ok, 1)
            for t in range(LT):
                link(tt(qh[:, t], qh[:, t], sq_q[:, t].unsqueeze(2).to_broadcast([P, HEADS, HD]), ALU.mult))
                rope(qh[:, t], qh[:, t], HEADS, 0, t).then_inc(q_ok, 1)
                dve.wait_ge(q_ok, t + 1)

        @block.tensor
        def _(pe):
            for i in range(LT + NT):
                if i >= 2:
                    pe.wait_ge(copied, i - 1)
                if i < NT:
                    pe.wait_ge(k_ok, i + 1)
                    for c in range(KV):
                        tr = pe.transpose(k.ps[:, 2 * (i % 2), c * P:(c + 1) * P], g["kd"][:, i, c, :], k.ident)
                else:
                    t = i - NT
                    pe.wait_ge(q_ok, t + 1)
                    for c in range(KD):
                        tr = pe.transpose(k.ps[:, 2 * (i % 2) + c // 4, (c % 4) * P:(c % 4 + 1) * P],
                                          q[:, t, c * P:(c + 1) * P], k.ident)
                tr.then_inc(turned, 1)


def layer_even(k):
    norm_stage(k, lambda t: k.h[:, t, :], range(NT), k.io["norm1_g"][0:1, :], (0, 1, 0), k.xT, k.rw[:, 0:8 * D])
    v = ssd_views(k)
    ssd_project_stage(k, v)
    conv_stage(k, v)
    ssd_diagonal_stage(k, v)
    ssd_states_stage(k, v)
    gate_stage(k, v)
    yT = k.r2.rearrange("p (c t) -> p c t", c=KD)
    norm_stage(k, lambda t: v["y"][:, t, :], range(NT), k.io["ssm_norm_g"][0:1, :], None, yT, k.rw[:, 9312:9312 + 8 * D])
    n = {"qT": k.rw[:, 0:6144].rearrange("p (c t) -> p c t", c=KD),
         "v": k.rw[:, 6144:12288].rearrange("p (t n) -> p t n", t=NT),
         "kT": k.r3.rearrange("p (c t) -> p c t", c=KD),
         "ring": [k.rw[:, 12288 + s * 4096:12288 + (s + 1) * 4096] for s in range(2)]}
    na_project_stage(k, n)
    oT = k.rw[:, 12288:18432].rearrange("p (c t) -> p c t", c=KD)
    bias = {"tile": k.rw[:, 18432:18432 + 2 * 14 * GRID].rearrange("p (s r c) -> p s r c", s=2, r=14),
            "mask": k.const[:, C_NAMASK:C_NAMASK + GRID]}
    pt = k.xt_r.rearrange("p (s k t) -> p s k t", s=2, k=NT)
    pt_ctx = k.rw[:, 20224:20224 + 4 * N_CTX].rearrange("p (s k t) -> p s k t", s=2, k=CT)

    def rows_of(ap, h, a, b):
        r = (h % 2) * HD
        return ap[r:r + HD, h // 2, a:b]

    attention_stage(k, "na", lambda h, u: rows_of(n["qT"], h, u * P, (u + 1) * P), lambda h, a, b: rows_of(n["kT"], h, a, b),
                    lambda h, kt: n["v"][:, kt, (h // 2) * P:(h // 2 + 1) * P], oT, CT, bias, pt, pt_ctx)
    output_stage(k, "about", k.io["ab_w_out"][0],
                 lambda kk, t: (yT if kk < KD else oT)[:, kk % KD, t * P:(t + 1) * P], range(NT), 0,
                 [k.rw[:, s * 4096:(s + 1) * 4096] for s in range(3)], k.xt_r)


def layer_odd(k):
    norm_stage(k, lambda t: k.h[:, t, :], range(NT), k.io["norm1_g"][1:2, :], (1, 1, 0), k.xT, k.rw[:, 0:8 * D])
    g = {"q": k.r2[:, 0:4096].rearrange("p (t n) -> p t n", t=LT),
         "kv": k.r3[:, 0:3072].rearrange("p (t n) -> p t n", t=NT),
         "ring": [k.rw[:, 9312 + s * 4096:9312 + (s + 1) * 4096] for s in range(3)],
         "small": k.misc,
         "kd": k.rw[:, 0:3072].rearrange("p (t h n) -> p t h n", t=NT, h=4),
         "vd": k.rw[:, 3072:6144].rearrange("p (t h n) -> p t h n", t=NT, h=4),
         "qT": k.rw[:, 6144:10240].rearrange("p (c t) -> p c t", c=KD),
         "kT": k.rw[:, 10240:13312].rearrange("p (c t) -> p c t", c=4),
         "tmp": k.rw[:, 13312:21600]}
    gqa_project_stage(k, g)
    gqa_rope_stage(k, g)
    oT = k.rw[:, 13312:17408].rearrange("p (c t) -> p c t", c=KD)
    pt = k.xt_r.rearrange("p (s k t) -> p s k t", s=2, k=NT)

    def half(h):
        return slice((h % 2) * HD, (h % 2) * HD + HD)

    attention_stage(k, "gqa", lambda h, u: g["qT"][half(h), h // 2, u * P:(u + 1) * P],
                    lambda h, a, b: g["kT"][half(h), h // 4, a:b], lambda h, kt: g["vd"][:, kt, h // 4, :],
                    oT, 0, None, pt, None)
    output_stage(k, "gqaout", k.io["gqa_w_out"][0], lambda kk, t: oT[:, kk, t * P:(t + 1) * P], range(LT), 1,
                 [k.rw[:, s * 4096:(s + 1) * 4096] for s in range(3)], k.xt_r)


def build(nc, io):
    with ExitStack() as ctx:
        k = Kernel(nc, ctx, io)
        load_stage(k)
        modulation_stage(k)
        layer_even(k)
        moe(k, 0, NT, None)
        layer_odd(k)
        moe(k, 1, LT, None)
        norm_stage(k, lambda t: k.h[:, t, :], range(LT), io["final_g"].rearrange("(a n) -> a n", a=1), None, None,
                   k.rw[:, 0:8 * D], out=io["out"])


def shape_constants():
    import numpy as np
    c = np.zeros((P, C_END), np.float32)
    i, l = np.arange(P)[:, None], np.arange(P)[None, :]
    c[:, C_IDENT:C_IDENT + P] = i == l
    c[:, C_ONES:C_ONES + P] = 1
    c[:, C_TRIF:C_TRIF + P] = i <= l
    c[:, C_TRIB:C_TRIB + P] = i >= l
    c[:, C_TRIS:C_TRIS + P] = i < l
    c[:, C_NEGF:C_NEGF + P] = np.where(i <= l, 0, NEG)
    c[:, C_NEGB:C_NEGB + P] = np.where(i >= l, 0, NEG)
    q, kc = GRID - 1 - np.arange(P)[:, None] % GRID, np.arange(GRID)[None, :]
    start = np.clip(q - 8, 0, GRID - 16)
    c[:, C_NAMASK:C_NAMASK + GRID] = np.where((kc >= start) & (kc < start + 16), 0, NEG)
    c[:, C_TOKID:C_TOKID + NT] = np.arange(P)[:, None] + P * np.arange(NT)[None, :]
    c[:, C_IOTA:C_IOTA + NE] = np.arange(NE)
    c[:, C_EPS] = EPS
    t = np.arange(N_LAT)
    n_freq = HD // 4
    inv = np.float32(10000.0) ** (-np.arange(n_freq, dtype=np.float32) / n_freq)
    ang = np.concatenate([(t // GRID).astype(np.float32)[:, None] * inv, (t % GRID).astype(np.float32)[:, None] * inv], -1)
    for col, f in ((C_COS, np.cos), (C_SIN, np.sin)):
        tab = f(ang).astype(np.float32).reshape(LT, P, HD // 2).transpose(1, 0, 2)
        c[:, col:col + LT * HD // 2] = tab.reshape(P, -1)
    sel = np.zeros((16, 16 * P), np.float32)
    for h in range(16):
        sel[h, h * P:(h + 1) * P] = 1
    return c, sel


_INS = ["x", "c", "ctx", "c_ctx", "w_mod", "b_mod", "norm1_g", "norm2_g", "final_g", "ab_w_in", "ab_w_out",
        "ssm_conv_w", "ssm_conv_b", "ssm_A_log", "ssm_dt_bias", "ssm_D", "ssm_norm_g", "na_rpb", "gqa_w_in",
        "gqa_w_out", "gqa_q_norm", "gqa_k_norm", "router_w", "router_bias", "moe_w_gate", "moe_w_up", "moe_w_down"]


def kernel(**inputs):
    import numpy as _np
    import concourse.bacc as _bacc
    from concourse import mybir as _mybir
    from concourse.bass_utils import run_bass_kernel_spmd as _run

    nc = _bacc.Bacc("TRN2", target_bir_lowering=False, num_devices=1)
    arrays, io = {}, {}
    const, sel = shape_constants()
    for name, a in [(n, inputs[n]) for n in _INS] + [("const", const), ("sel", sel)]:
        a = _np.ascontiguousarray(a)
        arrays[f"in_{name}_dram"] = a
        io[name] = nc.dram_tensor(f"in_{name}_dram", a.shape, _mybir.dt.from_np(a.dtype), kind="ExternalInput").ap()
    out = nc.dram_tensor("out_dram", (N_LAT, D), _mybir.dt.float32, kind="ExternalOutput").ap()
    io["out"] = out
    build(nc, io)
    r = _run(nc, [arrays], core_ids=[0])
    return r.results[0]["out_dram"].reshape(1, N_LAT, D)
```

```python
from contextlib import ExitStack, contextmanager

import concourse.bass as bass
from concourse import mybir

F32 = mybir.dt.float32
F32R = mybir.dt.float32r
BF16 = mybir.dt.bfloat16
I32 = mybir.dt.int32
ALU = mybir.AluOpType
ACT = mybir.ActivationFunctionType
AX = mybir.AxisListType

P = 128
D = 1024
KD = D // P
N_LAT, N_CTX = 512, 256
LT, CT = N_LAT // P, N_CTX // P
NT = LT + CT
TOK = N_LAT + N_CTX
EPS = 1e-6
HEADS, HD = 16, 64
XBC = 1536
O_Z, O_XBC, O_DT, O_Q, O_K, O_V = 0, 1024, 2560, 2592, 3616, 4640
GRID = 64
NEG = -1.0e30
NE, NG, EPG, DE = 32, 8, 4, 512
CAP = TOK
BLK = 128
MOD = 6 * D

C_IDENT, C_ONES, C_TRIF, C_TRIB, C_TRIS, C_NEGF, C_NEGB = [i * P for i in range(7)]
C_NAMASK = 7 * P
C_TOKID = C_NAMASK + GRID
C_IOTA = C_TOKID + NT
C_EPS = C_IOTA + NE
C_COS = C_EPS + 1
C_SIN = C_COS + LT * HD // 2
C_END = (C_SIN + LT * HD // 2 + 7) // 8 * 8
MISC = 4944
SEL_ROWS = 48


def latent_col(t):
    return t * P if t < LT else N_LAT + 4 + (t - LT) * P


CONV_W = N_LAT + 4 + N_CTX
RAW_W = CONV_W + 4


class Chain:

    def __init__(self, eng, sem):
        self.eng, self.sem, self.n = eng, sem, 0

    def __call__(self, ins):
        ins.then_inc(self.sem, 1)
        self.n += 1
        self.eng.wait_ge(self.sem, self.n)


class Kernel:
    def __init__(self, nc, ctx, io):
        self.nc, self.ctx, self.io = nc, ctx, io
        self.n_sems, self.stage_sems, self.old_sems = 0, [], []
        self.passed = nc.alloc_semaphore("loop_wait_passed")
        self.base = (nc.sbuf_base + 31) // 32 * 32
        self.at = 0

        def region(name, n):
            self.at += n
            return ctx.enter_context(nc.sbuf_tensor(name, [P, n], F32))[:, :]

        self.h = region("stream", NT * D).rearrange("p (t d) -> p t d", t=NT)
        self.big_at = self.at
        self.xt_r = region("xt", NT * D)
        self.work_at = self.at
        self.rw = region("work", 21600)
        self.results_at = self.at
        self.r23 = region("results", 2 * NT * D)
        self.r2, self.r3 = self.r23[:, 0:NT * D], self.r23[:, NT * D:]
        self.const = region("const", C_END)
        self.negb = region("negb", TOK)
        self.identb = region("identb", P // 2)
        self.misc_at = self.at
        self.misc = region("misc", MISC)
        self.ps = ctx.enter_context(nc.psum_tensor("ps", [P, 8, 512], F32))
        c = self.const
        self.ident = c[:, C_IDENT:C_IDENT + P]
        self.ones = c[:, C_ONES:C_ONES + P]
        self.eps = c[:, C_EPS:C_EPS + 1]
        self.xT = self.xt_r.rearrange("p (k t) -> p k t", k=KD)
        dram = nc.dram_tensor
        self.mods = dram("mods", (2, 2 * MOD), F32).ap()
        self.rpb_flat = dram("rpb_flat", (1, HEADS * 15 * 31 + 128), F32).ap()
        self.rows = dram("rows", (TOK, D), F32).ap()
        self.slots = dram("slots", (NE * CAP, 2), I32).ap()
        self.pairs = dram("pairs", (2 * TOK, D), F32).ap()

    def overlay(self, name, start, n, dtype=F32):
        return self.nc.alloc_sbuf_tensor_at(name, [P, n], dtype, offset=self.base + 4 * start)[:, :]

    def sem(self, name):
        self.n_sems += 1
        s = self.nc.alloc_semaphore(f"{name}_{self.n_sems}")
        self.stage_sems.append(s)
        return s

    @contextmanager
    def stage(self):
        if self.old_sems:
            self.nc.clear_and_free_semaphores(self.old_sems)
        self.old_sems, self.stage_sems = self.stage_sems, []
        with self.nc.Block() as block:
            yield block

    def mod_row(self, cond, layer, i):
        o = layer * MOD + i * D
        return self.mods[cond:cond + 1, o:o + D].to_broadcast([P, D])


def load_stage(k):
    nc, io = k.nc, k.io
    const_in, flat_out, zeroed = k.sem("const_in"), k.sem("rpb_flat_out"), k.sem("pad_zeroed")
    zero_out = k.sem("pad_out")
    n = HEADS * 15 * 31
    pad = k.misc[0:1, 0:64]
    with k.stage() as block:

        @block.sync
        def _(sp):
            sp.dma_start(k.const[:, :], io["const"]).then_inc(const_in, 16)
            sp.dma_start(k.rpb_flat[:, 64:64 + n],
                         io["na_rpb"].rearrange("a h r c -> a (h r c)")).then_inc(flat_out, 16)
            sp.wait_ge(zeroed, 1)
            sp.dma_start(k.rpb_flat[:, 0:64], pad).then_inc(zero_out, 16)
            sp.dma_start(k.rpb_flat[:, 64 + n:128 + n], pad).then_inc(zero_out, 16)
            sp.wait_ge(zero_out, 32)
            sp.wait_ge(flat_out, 16)

        @block.vector
        def _(dve):
            dve.memset(pad, 0.0).then_inc(zeroed, 1)
            dve.wait_ge(const_in, 16)
            dve.tensor_copy(k.identb.bitcast(BF16), k.ident)
            negb = k.negb.bitcast(BF16).rearrange("p (g t l) -> p g t l", g=2, t=NT)
            for g, col in enumerate((C_NEGF, C_NEGB)):
                for t in range(NT):
                    dve.tensor_copy(negb[:, g, t, :], k.const[:, col:col + P])


def modulation_stage(k, load_stream):
    nc, io = k.nc, k.io
    cond_in, cond_T, silu_ok, hi_ok = k.sem("cond_in"), k.sem("cond_T"), k.sem("cond_silu"), k.sem("cond_high")
    CH = 512
    c_rows = k.misc[0:16, 0:P]
    c_cols = k.misc[:, P:P + 16]
    parts = k.overlay("cond_parts", k.misc_at + 2 * P, 32, F32R)
    c_hi, c_lo = parts[:, 0:16], parts[:, 16:32]
    row = k.r23[0:2, :]
    stored = k.nc.alloc_semaphore("mods_out")

    def load_bias(sp, sem):
        for cond in range(2):
            sp.dma_start(row[cond:cond + 1, :], io["b_mod"].rearrange("(a l) n -> a (l n)", a=1)).then_inc(sem, 16)
    load_bias.count = 32

    def operands(kk, w):
        return (c_hi[:, kk:16:8], c_lo[:, kk:16:8]), w

    groups = []
    for j in range(2 * MOD // CH):
        layer, c0 = divmod(j * CH, MOD)
        groups.append((pieces_of(io["w_mod"][layer], c0, CH, 4), [([2, CH], operands, "v")]))

    def store(sp):
        sp.dma_start(k.mods, row).then_inc(stored, 16)
        sp.wait_ge(stored, 16)

    def evacuate(which, eng, j, ps, link):
        part = row[:, j * CH:(j + 1) * CH]
        return eng.tensor_tensor(part, ps, part, ALU.add)

    product = Product(k, "mod", groups, rings(k, "mod", k.work_at, 4, k.work_at + 8192, 3, 2048), evacuate, load_bias, store)

    with k.stage() as block:

        @block.sync
        def _(sp):
            sp.dma_start(c_rows[0:8, :], io["c"].rearrange("a (k p) -> (a k) p", p=P)).then_inc(cond_in, 16)
            sp.dma_start(c_rows[8:16, :], io["c_ctx"].rearrange("(k p) -> k p", p=P)).then_inc(cond_in, 16)
            product.early(sp)

        @block.tensor
        def _(pe):
            pe.wait_ge(cond_in, 32)
            pe.transpose(k.ps[:, 7, 0:16], c_rows, k.ident[0:16, 0:16]).then_inc(cond_T, 1)

        @block.scalar
        def _(act):
            act.wait_ge(cond_T, 1)
            act.activation(c_cols, k.ps[:, 7, 0:16], ACT.Silu).then_inc(silu_ok, 1)
            act.wait_ge(silu_ok, 1)
            act.activation(c_hi, c_cols, ACT.Copy).then_inc(hi_ok, 1)

        @block.vector
        def _(dve):
            dve.wait_ge(hi_ok, 1)
            dve.tensor_tensor(c_lo, c_cols, c_hi.bitcast(F32), ALU.subtract)

    product.run(load_stream)


def norm_stage(k, src, tiles, g_row, mod, xT, scratch, rows_out=None, out=None, prefetch=None,
               split=None):
    nc = k.nc
    T = len(tiles)
    g_in, mod_in = k.sem("gain_in"), k.sem("mod_in")
    squared, root, rooted = k.sem("squared"), k.sem("root"), k.sem("rstd")
    rows_ready, gain_ready, chain = k.sem("rows_ready"), k.sem("gain_ready"), k.sem("norm_chain")
    turned, copied = k.sem("turned"), k.sem("turned_copied")
    hi_ok, lo_ok = k.sem("turned_high"), k.sem("turned_low")
    turning = xT is not None or split is not None

    def turned_ps(i):
        return k.ps[:, 2 * (i % 2):2 * (i % 2) + 2, :].rearrange("p a (b c) -> p (a b) c", c=P)

    stored = [k.sem(f"rows_stored{s}") for s in range(2)]
    nr = 2 if mod else 1
    gains = scratch[:, 0:nr * D].rearrange("p (c d) -> p c d", c=nr)
    shifts = scratch[:, 2 * D:4 * D].rearrange("p (c d) -> p c d", c=2)
    g = scratch[:, 4 * D:5 * D] if mod else gains[:, 0, :]
    xn = scratch[:, 5 * D:7 * D].rearrange("p (s d) -> p s d", s=2)
    junk = scratch[:, 7 * D:8 * D]
    stat = k.misc[:, 0:3 * NT].rearrange("p (a t) -> p a t", a=3)
    dst = rows_out if rows_out is not None else out
    with k.stage() as block:

        @block.sync
        def _(sp):
            sp.dma_start(g, g_row.to_broadcast([P, D])).then_inc(g_in, 16)
            if mod:
                for cond in range(2):
                    sp.dma_start(gains[:, cond, :], k.mod_row(cond, mod[0], mod[1])).then_inc(mod_in, 16)
                    sp.dma_start(shifts[:, cond, :], k.mod_row(cond, mod[0], mod[2])).then_inc(mod_in, 16)
            if prefetch:
                prefetch(sp)
            if dst is not None:
                for i, t in enumerate(tiles):
                    sp.wait_ge(rows_ready, i + 1)
                    sp.dma_start(dst[t * P:(t + 1) * P, :], xn[:, i % 2, :]).then_inc(stored[i % 2], 16)
                for s in range(2):
                    sp.wait_ge(stored[s], 16 * (T // 2))

        @block.scalar
        def _(act):
            link = Chain(act, squared)
            for i, t in enumerate(tiles):
                link(act.activation(junk, src(t), ACT.Square, accum_out=stat[:, 0, i:i + 1]))
            act.activation(stat[:, 1, 0:T], stat[:, 0, 0:T], ACT.Sqrt, bias=k.eps, scale=1.0 / D).then_inc(root, 1)
            if turning:
                for i, t in enumerate(tiles):
                    act.wait_ge(turned, i + 1)
                    if xT is not None:
                        act.activation(xT[:, :, t * P:(t + 1) * P], turned_ps(i), ACT.Copy).then_inc(copied, 1)
                    if split:
                        if xT is not None:
                            act.wait_ge(copied, i + 1)
                        act.activation(split[0][:, :, t * P:(t + 1) * P], turned_ps(i), ACT.Copy).then_inc(hi_ok, 1)

        @block.vector
        def _(dve):
            link = Chain(dve, chain)

            def low(i):
                t = tiles[i]
                dve.wait_ge(hi_ok, i + 1)
                dve.tensor_tensor(split[1][:, :, t * P:(t + 1) * P], turned_ps(i),
                                  split[0][:, :, t * P:(t + 1) * P].bitcast(F32), ALU.subtract).then_inc(lo_ok, 1)

            dve.wait_ge(g_in, 16)
            if mod:
                dve.wait_ge(mod_in, 64)
                for cond in range(2):
                    dve.scalar_tensor_tensor(out=gains[:, cond, :], in0=gains[:, cond, :], scalar=1.0, in1=g,
                                             op0=ALU.add, op1=ALU.mult).then_inc(gain_ready, 1)
            dve.wait_ge(root, 1)
            dve.reciprocal(stat[:, 2, 0:T], stat[:, 1, 0:T]).then_inc(rooted, 1)
            dve.wait_ge(rooted, 1)
            if mod:
                dve.wait_ge(gain_ready, 2)
            for i, t in enumerate(tiles):
                cond = (0 if t < LT else 1) if mod else 0
                if i >= 2:
                    if turning:
                        dve.wait_ge(turned, i - 1)
                    if dst is not None:
                        dve.wait_ge(stored[i % 2], 16 * (i // 2))
                last = dve.scalar_tensor_tensor(out=xn[:, i % 2, :], in0=src(t), scalar=stat[:, 2, i:i + 1],
                                                in1=gains[:, cond, :], op0=ALU.mult, op1=ALU.mult)
                if mod:
                    link(last)
                    last = dve.tensor_tensor(xn[:, i % 2, :], xn[:, i % 2, :], shifts[:, cond, :], ALU.add)
                last.then_inc(rows_ready, 1)
                if split and i >= 1:
                    low(i - 1)
            if split:
                low(T - 1)

        if turning:
            @block.tensor
            def _(pe):
                for i in range(T):
                    pe.wait_ge(rows_ready, i + 1)
                    if i >= 2:
                        if xT is not None:
                            pe.wait_ge(copied, i - 1)
                        if split:
                            pe.wait_ge(lo_ok, i - 1)
                    for kk in range(KD):
                        tr = pe.transpose(k.ps[:, 2 * (i % 2) + kk // 4, (kk % 4) * P:(kk % 4 + 1) * P],
                                          xn[:, i % 2, kk * P:(kk + 1) * P], k.ident)
                    tr.then_inc(turned, 1)


class Product:

    def __init__(self, k, name, groups, ring, evacuate, extra=None, finish=None):
        self.k, self.name, self.groups, self.ring = k, name, groups, ring
        self.evacuate, self.extra, self.finish = evacuate, extra, finish
        self.pieces = [piece for ps, _ in groups for piece in ps]
        self.w_in = [k.nc.alloc_semaphore(f"{name}_w_in{s}") for s in range(len(ring[0]))]
        self.loaded = 0

    def slot(self, slots, c):
        _, kk, n = self.pieces[c][0].shape
        return slots[c % len(slots)][:, 0:kk * n].rearrange("p (k n) -> p k n", k=kk)

    def load(self, sp, c):
        sp.dma_start(self.slot(self.ring[0], c), self.pieces[c][0]).then_inc(self.w_in[c % len(self.w_in)], 16)

    def early(self, sp):
        for c in range(min(len(self.w_in), len(self.pieces))):
            self.load(sp, c)
            self.loaded += 1

    def run(self, prefetch=None):
        product_stage(self, self.k, self.name, self.w_in, self.evacuate, self.extra, self.finish, prefetch)


def product_stage(p, k, name, w_in, evacuate, extra, finish, prefetch):
    raw_ring, high_ring, low_ring = p.ring
    groups, pieces, slot = p.groups, p.pieces, p.slot
    R, S = len(raw_ring), len(high_ring)
    hi_ok, lo_ok, used = k.sem(f"{name}_w_high"), k.sem(f"{name}_w_low"), k.sem(f"{name}_w_used")
    prod = k.sem(f"{name}_prod")
    taken = {"v": k.sem(f"{name}_taken_v"), "s": k.sem(f"{name}_taken_s")}
    chain = k.sem(f"{name}_chain")
    extra_in = k.sem(f"{name}_extra_in")
    jobs = [job for _, js in groups for job in js]
    order = [sum(1 for job in jobs[:j + 1] if job[2] == jobs[j][2]) for j in range(len(jobs))]
    runs = []
    first_job = 0
    for ps, js in groups:
        for i in range(len(ps)):
            runs.append((len(runs), i == 0, i == len(ps) - 1, range(first_job, first_job + len(js))))
        first_job += len(js)

    def bank(j):
        (m, n), _, _ = jobs[j]
        return k.ps[0:m, j % 8, 0:n]

    def free_slot(eng, c):
        if c >= S:
            _, _, last, js = runs[c - S]
            if last:
                eng.wait_ge(prod, js[-1] + 1)
            else:
                eng.wait_ge(used, sum(1 for run in runs[:c - S + 1] if not run[2]))

    def split_and_take(which, eng, split):
        link = Chain(eng, chain)
        for c in range(min(S, len(pieces))):
            split(c)
        for c, _, last, js in runs:
            for j in js:
                if last and jobs[j][2] == which:
                    eng.wait_ge(prod, j + 1)
                    evacuate(which, eng, j, bank(j), link).then_inc(taken[which], 1)
            if c + S < len(pieces):
                split(c + S)

    with k.stage() as block:
        k.stage_sems += w_in

        @block.sync
        def _(sp):
            if extra:
                extra(sp, extra_in)
            for c in range(p.loaded, len(pieces)):
                if c >= R:
                    sp.wait_ge(lo_ok, c - R + 1)
                p.load(sp, c)
            if prefetch:
                prefetch(sp)
            if finish:
                for which in taken:
                    if any(job[2] == which for job in jobs):
                        sp.wait_ge(taken[which], sum(1 for job in jobs if job[2] == which))
                finish(sp)

        @block.tensor
        def _(pe):
            for c, first, last, js in runs:
                pe.wait_ge(lo_ok, c + 1)
                hi, lo = slot(high_ring, c), slot(low_ring, c)
                for j in js:
                    if first and j >= 8:
                        pe.wait_ge(taken[jobs[j - 8][2]], order[j - 8])
                    for kk in range(hi.shape[1]):
                        stat, move = jobs[j][1](pieces[c][1] + kk, (hi[:, kk, :], lo[:, kk, :]))
                        mm = split_products(pe, bank(j), stat, move, first and kk == 0,
                                            last and kk == hi.shape[1] - 1)
                    if last:
                        mm.then_inc(prod, 1)
                    elif j == js[-1]:
                        mm.then_inc(used, 1)

        @block.scalar
        def _(act):
            def high(c):
                act.wait_ge(w_in[c % R], 16 * (c // R + 1))
                free_slot(act, c)
                act.activation(slot(high_ring, c), slot(raw_ring, c), ACT.Copy).then_inc(hi_ok, 1)
            split_and_take("s", act, high)

        @block.vector
        def _(dve):
            if extra:
                dve.wait_ge(extra_in, extra.count)

            def low(c):
                dve.wait_ge(hi_ok, c + 1)
                dve.tensor_tensor(slot(low_ring, c), slot(raw_ring, c), slot(high_ring, c).bitcast(F32),
                                  ALU.subtract).then_inc(lo_ok, 1)
            split_and_take("v", dve, low)

def rings(k, name, raw_at, n_raw, split_at, n_split, size=1024):
    raw = k.overlay(f"{name}_raw", raw_at, n_raw * size)
    parts = k.overlay(f"{name}_parts", split_at, 2 * n_split * size, F32R)
    return ([raw[:, s * size:(s + 1) * size] for s in range(n_raw)],
            [parts[:, 2 * s * size:(2 * s + 1) * size] for s in range(n_split)],
            [parts[:, (2 * s + 1) * size:(2 * s + 2) * size] for s in range(n_split)])


def split_views(k, name, hi_at, lo_at, n):
    return tuple(k.overlay(f"{name}_{part}", at, KD * n, F32R).rearrange("p (k t) -> p k t", k=KD)
                 for part, at in (("high", hi_at), ("low", lo_at)))


def copy_out(which, eng, dst, src, scale=None):
    if which == "s":
        return eng.activation(dst, src, ACT.Copy, scale=1.0 if scale is None else scale)
    if scale is None:
        return eng.tensor_copy(dst, src)
    return eng.tensor_scalar(dst, src, scale, None, ALU.mult)


def pieces_of(w, col, n, depth):
    return [(w[a * P:(a + depth) * P, col:col + n].rearrange("(k p) n -> p k n", p=P), a)
            for a in range(0, w.shape[0] // P, depth)]


def channel_major_group(x, pieces, n_tiles, groups, dsts, dst_of):
    jobs = []
    for ct in range(n_tiles):
        for part, (a, b) in enumerate(((0, N_LAT), (N_LAT, TOK))):
            def operands(kk, w, ct=ct, a=a, b=b):
                return [part_[:, ct * P:(ct + 1) * P] for part_ in w], [x_[:, kk, a:b] for x_ in x]
            jobs.append(([P, b - a], operands, "vs"[len(jobs) % 2]))
            dsts.append(dst_of(ct, part, a, b))
    groups.append((pieces, jobs))


def token_major_group(x, pieces, n, tiles, groups, dsts, dst_of, engine=None):
    jobs = []
    for t in tiles:
        def operands(kk, w, t=t):
            return [x_[:, kk, t * P:(t + 1) * P] for x_ in x], w
        jobs.append(([P, n], operands, engine or "vs"[len(jobs) % 2]))
        dsts.append(dst_of(t))
    groups.append((pieces, jobs))


def ssd_views(k):
    v = {}
    v["raw"] = k.rw[:, 0:12 * RAW_W].rearrange("p (c n) -> p c n", c=12)
    rest = k.rw[:, 12 * RAW_W:]
    rest_at = k.work_at + 12 * RAW_W
    v["ring"] = rings(k, "xbc", rest_at, 4, rest_at + 4096, 4)
    at = 0

    def part(n):
        nonlocal at
        at += n
        return rest[:, at - n:at]

    v["conv"] = part(2 * CONV_W).rearrange("p (s n) -> p s n", s=2)
    v["btok"] = part(NT * 256).rearrange("p (t n) -> p t n", t=NT)
    sel_at = at
    v["sel"] = part(16 * P)[0:SEL_ROWS, :]
    cb_at = at
    v["cb"] = part(2 * TOK).rearrange("p (g n) -> p g n", g=2)
    v["decay"] = part(4 * TOK).rearrange("p (s d n) -> p s d n", s=2, d=2)
    v["xd"] = part(4 * NT * HD).rearrange("p (s d t n) -> p s d t n", s=2, d=2, t=NT)
    sc = rest[:, cb_at:cb_at + 6 * D]
    v["diag"] = sc[:, 0:6 * 5 * P].rearrange("p (c w n) -> p c w n", c=6, w=5)
    v["state"] = sc[:, 0:2 * D].rearrange("p (d n) -> p d n", d=2)
    v["xw"] = sc[:, 2 * D:4 * D].rearrange("p (d n) -> p d n", d=2)
    v["yo"] = sc[:, 4 * D:6 * D].rearrange("p (d n) -> p d n", d=2)
    v["z"] = k.rw[:, 0:6144].rearrange("p (t n) -> p t n", t=NT)
    v["xs"] = k.r2.rearrange("p (t n) -> p t n", t=NT)
    v["y"] = k.r3.rearrange("p (t n) -> p t n", t=NT)
    m = k.misc
    at2 = 32

    def small(n):
        nonlocal at2
        at2 += n
        return m[:, at2 - n:at2]

    v["par"] = small(72)
    v["par_rows"] = small(P)[0:72, :]
    v["bc"] = small(80)
    for nm in ("dt", "adt", "nac", "eac", "etot", "wst", "u0", "u1"):
        v[nm] = small(NT * 32).rearrange("p (t n) -> p t n", t=NT)
    v["rowf"] = small(TOK)[0:16, :]
    v["rowb"] = small(TOK)[0:16, :]
    stacked = k.overlay("cum_parts", k.misc_at + at2, 2 * TOK, F32R)[0:SEL_ROWS, :]
    v["row_parts"] = [stacked[:, d * TOK:(d + 1) * TOK] for d in range(2)]
    v["sel_r"] = k.overlay("sel_r", rest_at + sel_at, 16 * P, F32R)[0:SEL_ROWS, :]
    return v


def ssd_projection(k, v, x):
    w = k.io["ab_w_in"][0]
    groups, dsts = [], []
    for c in range(6):
        channel_major_group(x, pieces_of(w, O_XBC + c * 256, 256, 4), 2, groups, dsts,
                            lambda ct, part, a, b, c=c: v["raw"][:, 2 * c + ct, 2 + a + 4 * part:2 + b + 4 * part])
    token_major_group(x, pieces_of(w, O_DT, 32, KD), 32, range(NT), groups, dsts, lambda t: v["dt"][:, t, :])
    return Product(k, "xbc", groups, v["ring"], lambda which, eng, j, ps, link: copy_out(which, eng, dsts[j], ps))


def conv_stage(k, v):
    nc, io = k.nc, k.io
    par_in, par_T, par_ok = k.sem("conv_par_in"), k.sem("conv_par_T"), k.sem("conv_par_ready")
    bc_in, sel_in = k.sem("ssd_bc_in"), k.sem("sel_in")
    padded, conved, silued, chain = k.sem("pads_zeroed"), k.sem("conved"), k.sem("silued"), k.sem("conv_chain")
    diag_ok, pe_conved, pe_silued = k.sem("tap_diagonals"), k.sem("conved_on_pe"), k.sem("silued_from_pe")
    turned, copied = k.sem("xs_turned"), k.sem("xs_copied")
    HALF = 6
    aexp, dtv, dte, adt_ok = k.sem("a_exp"), k.sem("dt_abs"), k.sem("dt_exp"), k.sem("adt_ready")
    cum, cum_rows, cum_T, cum_ok, ctot = (k.sem("cum_rows"), k.sem("cum_rows_copied"), k.sem("cum_T"),
                                          k.sem("cum_copied"), k.sem("cum_tot"))
    exps, coef = k.sem("decay_exps"), k.sem("coef")
    raw, conv = v["raw"], v["conv"]
    cw = v["par"][:, 0:60].rearrange("p (w c) -> p w c", w=5)
    cb = v["par"][:, 60:72]
    a_b, dtb_b = v["bc"][:, 0:32], v["bc"][:, 32:64]

    def cols(t):
        return slice(latent_col(t), latent_col(t) + P)

    def conv_ps(i):
        return k.ps[:, 2 * (i % 2):2 * (i % 2) + 2, :].rearrange("p a n -> p (a n)")[:, 0:CONV_W]

    with k.stage() as block:

        @block.sync
        def _(sp):
            sp.dma_start(v["par_rows"][0:60, :],
                         io["ssm_conv_w"][0].rearrange("w (c p) -> (w c) p", p=P)).then_inc(par_in, 16)
            sp.dma_start(v["par_rows"][60:72, :],
                         io["ssm_conv_b"][0].rearrange("(c p) -> c p", p=P)).then_inc(par_in, 16)
            sp.dma_start(a_b, io["ssm_A_log"].rearrange("a d h -> a (d h)").to_broadcast([P, 32])).then_inc(bc_in, 16)
            sp.dma_start(dtb_b, io["ssm_dt_bias"].rearrange("a d h -> a (d h)").to_broadcast([P, 32]))\
                .then_inc(bc_in, 16)
            sp.dma_start(v["bc"][:, 64:80], io["ssm_D"].to_broadcast([P, 16])).then_inc(bc_in, 16)
            sp.dma_start(v["sel"], io["sel"]).then_inc(sel_in, 16)

        @block.gpsimd
        def _(pool):
            for c0 in (0, 2 + N_LAT, RAW_W - 2):
                pad = pool.memset(raw[:, :, c0:c0 + (4 if c0 == 2 + N_LAT else 2)], 0.0)
                pad.then_inc(padded, 1)

        @block.vector
        def _(dve):
            link = Chain(dve, chain)
            dve.wait_ge(bc_in, 48)
            bias = dtb_b.unsqueeze(1).to_broadcast([P, NT, 32])
            link(dve.tensor_tensor(v["dt"], v["dt"], bias, ALU.add))
            link(dve.tensor_scalar(v["u0"], v["dt"], -1.0, None, ALU.mult))
            dve.tensor_tensor(v["u0"], v["u0"], v["dt"], ALU.min).then_inc(dtv, 1)
            dve.wait_ge(par_T, 1)
            dve.tensor_copy(v["par"], k.ps[:, 7, 0:72]).then_inc(par_ok, 1)
            dve.wait_ge(par_ok, 1)
            dve.wait_ge(padded, 3)
            dve.wait_ge(dte, 1)
            link(dve.tensor_scalar(v["u1"], v["u0"], 2.0, None, ALU.add))
            link(dve.reciprocal(v["u1"], v["u1"]))
            link(dve.tensor_tensor(v["u0"], v["u0"], v["u1"], ALU.mult))
            link(dve.tensor_tensor(v["u1"], v["u0"], v["u0"], ALU.mult))
            acc = v["adt"]
            link(dve.tensor_scalar(acc, v["u1"], 2.0 / 17, 2.0 / 15, ALU.mult, ALU.add))
            for n in (13, 11, 9, 7, 5, 3, 1):
                link(dve.tensor_tensor(acc, acc, v["u1"], ALU.mult))
                link(dve.tensor_scalar(acc, acc, 2.0 / n, None, ALU.add))
            link(dve.tensor_tensor(acc, acc, v["u0"], ALU.mult))
            link(dve.tensor_scalar(v["dt"], v["dt"], 0.0, None, ALU.max))
            link(dve.tensor_tensor(v["dt"], v["dt"], acc, ALU.add))
            dve.wait_ge(aexp, 1)
            link(dve.tensor_scalar(a_b, a_b, -1.0, None, ALU.mult))
            dve.tensor_tensor(v["adt"], v["dt"], a_b.unsqueeze(1).to_broadcast([P, NT, 32]), ALU.mult)\
                .then_inc(adt_ok, 1)
            for c in range(HALF):
                if c >= 2:
                    dve.wait_ge(silued, c - 1)
                link(dve.tensor_scalar(conv[:, c % 2, :], raw[:, c, 0:CONV_W], cw[:, 0, c:c + 1], cb[:, c:c + 1],
                                       ALU.mult, ALU.add))
                for w in range(1, 5):
                    last = dve.scalar_tensor_tensor(out=conv[:, c % 2, :], in0=raw[:, c, w:w + CONV_W],
                                                    scalar=cw[:, w, c:c + 1], in1=conv[:, c % 2, :],
                                                    op0=ALU.mult, op1=ALU.add)
                    if w < 4:
                        link(last)
                last.then_inc(conved, 1)
                if c == 2:
                    dve.wait_ge(cum, 4)
                    dve.tensor_copy(v["rowf"][:, 0:512], k.ps[0:16, 4, :])
                    dve.tensor_copy(v["rowf"][:, 512:TOK], k.ps[0:16, 5, 0:256])
                    dve.tensor_copy(v["rowb"][:, 0:512], k.ps[0:16, 6, :])
                    dve.tensor_copy(v["rowb"][:, 512:TOK], k.ps[0:16, 7, 0:256]).then_inc(cum_rows, 1)
                    dve.wait_ge(cum_rows, 1)
                    dve.wait_ge(sel_in, 16)
                    for parts, row in zip(v["row_parts"], (v["rowf"], v["rowb"])):
                        link(dve.tensor_scalar(parts, v["sel"][:, 0:TOK], 0.0, None, ALU.mult))
                        link(dve.tensor_copy(parts[0:16, :], row))
                        link(dve.tensor_tensor(parts[32:48, :], row, parts[0:16, :].bitcast(F32), ALU.subtract))
                    dve.tensor_copy(v["sel_r"], v["sel"])
                if c == 4:
                    dve.wait_ge(cum_T, 1)
                    dve.wait_ge(ctot, 1)
                    cum_ps = k.ps[:, 4, 0:NT * 32].rearrange("p (t n) -> p t n", t=NT)
                    tot_ps = k.ps[:, 5, 0:NT * 32].rearrange("p (t n) -> p t n", t=NT)
                    link(dve.tensor_scalar(v["nac"], cum_ps, -1.0, None, ALU.mult))
                    link(dve.tensor_tensor(v["wst"], tot_ps, v["nac"], ALU.add))
                    dve.tensor_copy(v["etot"], tot_ps).then_inc(cum_ok, 1)
            dve.wait_ge(exps, 3)
            link(dve.tensor_tensor(v["wst"], v["wst"], v["dt"], ALU.mult))
            for i in range(NT):
                dve.wait_ge(turned, i + 1)
                src = k.ps[:, 2 * (i % 2):2 * (i % 2) + 2, :].rearrange("p a n -> p (a n)")
                dve.tensor_copy(v["xs"][:, i, :], src).then_inc(copied, 1)
            dve.wait_ge(turned, NT + 1)
            dve.tensor_copy(v["btok"], k.ps[:, 4:7, :].rearrange("p a (b n) -> p (a b) n", n=256)).then_inc(copied, 1)

        @block.scalar
        def _(act):
            act.wait_ge(bc_in, 48)
            act.activation(a_b, a_b, ACT.Exp).then_inc(aexp, 1)
            act.wait_ge(dtv, 1)
            act.activation(v["u0"], v["u0"], ACT.Exp).then_inc(dte, 1)
            act.wait_ge(par_ok, 1)
            for i in range(HALF):
                for w in range(5):
                    act.activation(v["diag"][:, i, w, :], k.ident, ACT.Copy,
                                   scale=cw[:, w, HALF + i:HALF + i + 1]).then_inc(diag_ok, 1)
            for c in range(HALF):
                act.wait_ge(pe_conved, c + 1)
                act.activation(raw[:, HALF + c, 0:CONV_W], conv_ps(c), ACT.Silu, bias=cb[:, HALF + c:HALF + c + 1])\
                    .then_inc(pe_silued, 1)
                act.wait_ge(conved, c + 1)
                act.activation(raw[:, c, 0:CONV_W], conv[:, c % 2, :], ACT.Silu).then_inc(silued, 1)
            act.wait_ge(cum_ok, 1)
            act.activation(v["eac"], v["nac"], ACT.Exp, scale=-1.0).then_inc(exps, 1)
            act.activation(v["etot"], v["etot"], ACT.Exp).then_inc(exps, 1)
            act.activation(v["wst"], v["wst"], ACT.Exp).then_inc(exps, 1)

        @block.tensor
        def _(pe):
            pe.wait_ge(par_in, 32)
            pe.transpose(k.ps[:, 7, 0:72], v["par_rows"], k.ident[0:72, 0:72]).then_inc(par_T, 1)
            pe.wait_ge(padded, 3)

            def convolve(i):
                pe.wait_ge(diag_ok, 5 * (i + 1))
                if i >= 2:
                    pe.wait_ge(pe_silued, i - 1)
                for a, b in ((0, 512), (512, CONV_W)):
                    for w in range(5):
                        mm = pe.matmul(k.ps[:, 2 * (i % 2) + a // 512, 0:b - a], v["diag"][:, i, w, :],
                                       raw[:, HALF + i, w + a:w + b], start=(w == 0), stop=(w == 4))
                mm.then_inc(pe_conved, 1)

            convolve(0)
            pe.wait_ge(par_ok, 1)
            pe.wait_ge(adt_ok, 1)
            tri = [k.const[:, C_TRIF:C_TRIF + P], k.const[:, C_TRIB:C_TRIB + P]]
            for d in range(2):
                for half, (t0, t1) in enumerate(((0, LT), (LT, NT))):
                    for t in range(t0, t1):
                        mm = pe.matmul(k.ps[0:16, 4 + 2 * d + half, (t - t0) * P:(t - t0 + 1) * P],
                                       v["adt"][:, t, 16 * d:16 * d + 16], tri[d], start=True, stop=True)
                    mm.then_inc(cum, 1)
            convolve(1)
            convolve(2)
            pe.wait_ge(cum_rows, 1)
            for t in range(NT):
                for d, row in enumerate((v["rowf"], v["rowb"])):
                    tr = pe.transpose(k.ps[:, 4, t * 32 + 16 * d:t * 32 + 16 * d + 16], row[:, t * P:(t + 1) * P],
                                      k.ident[0:16, 0:16])
            tr.then_inc(cum_T, 1)
            pe.matmul(k.ps[:, 5, 0:NT * 32], k.ones, v["adt"].rearrange("p t n -> p (t n)"),
                      start=True, stop=True).then_inc(ctot, 1)
            for i in range(3, HALF):
                convolve(i)
            pe.wait_ge(silued, HALF)
            pe.wait_ge(pe_silued, HALF)
            for t in range(NT):
                if t >= 2:
                    pe.wait_ge(copied, t - 1)
                for c in range(8):
                    tr = pe.transpose(k.ps[:, 2 * (t % 2) + c // 4, (c % 4) * P:(c % 4 + 1) * P],
                                      raw[:, c, cols(t)], k.ident)
                tr.then_inc(turned, 1)
            pe.wait_ge(cum_ok, 1)
            for t in range(NT):
                for g in range(2):
                    tr = pe.transpose(k.ps[:, 4 + t // 2, (t % 2) * 256 + g * P:(t % 2) * 256 + (g + 1) * P],
                                      raw[:, 8 + g, cols(t)], k.ident)
            tr.then_inc(turned, 1)


def ssd_diagonal_stage(k, v):
    nc = k.nc
    cb_done, cb_ok = k.sem("cb_prod"), k.sem("cb_copied")
    bcast, decayed, scaled, xd_ok = k.sem("cum_bcast"), k.sem("decayed"), k.sem("decay_x_cb"), k.sem("xd_ready")
    yprod, y_ok, chain = k.sem("ydiag_prod"), k.sem("ydiag_taken"), k.sem("ydiag_chain")
    raw = v["raw"]
    negb = k.negb.bitcast(BF16).rearrange("p (g n) -> p g n", g=2)
    xs4 = v["xs"].rearrange("p t (h n) -> p t h n", n=HD)
    y4 = v["y"].rearrange("p t (h n) -> p t h n", n=HD)
    NU = 2 * HEADS

    def cum_ps(u):
        return k.ps[:, 2 * (u % 2):2 * (u % 2) + 2, :].rearrange("p a n -> p (a n)")[:, 0:TOK]

    with k.stage() as block:

        @block.tensor
        def _(pe):
            for g in range(2):
                for t in range(NT):
                    c = slice(latent_col(t), latent_col(t) + P)
                    mm = pe.matmul(k.ps[:, 2 * g + t // LT, (t % LT) * P:(t % LT + 1) * P], raw[:, 8 + g, c],
                                   raw[:, 10 + g, c], start=True, stop=True)
                mm.then_inc(cb_done, 1)
            pe.wait_ge(cb_ok, 2)

            def broadcast(u):
                h, d = divmod(u, 2)
                if u >= 2:
                    pe.wait_ge(decayed, u - 1)
                for bank, (a, b) in enumerate(((0, 512), (512, TOK))):
                    out = k.ps[:, 2 * (u % 2) + bank, 0:b - a]
                    pe.matmul(out, v["sel_r"][:, h * P:(h + 1) * P], v["row_parts"][d][:, a:b], start=True, stop=False)
                    mm = pe.matmul(out, k.identb.bitcast(BF16), negb[:, d, a:b], start=False, stop=True)
                mm.then_inc(bcast, 1)

            broadcast(0)
            broadcast(1)
            for h in range(HEADS):
                if h + 1 < HEADS:
                    broadcast(2 * h + 2)
                    broadcast(2 * h + 3)
                pe.wait_ge(scaled, 2 * h + 2)
                pe.wait_ge(xd_ok, 2 * h + 2)
                if h >= 2:
                    pe.wait_ge(y_ok, h - 1)
                for t in range(NT):
                    for d in range(2):
                        mm = pe.matmul(k.ps[:, 4 + h % 2, t * HD:(t + 1) * HD],
                                       v["decay"][:, h % 2, d, t * P:(t + 1) * P], v["xd"][:, h % 2, d, t, :],
                                       start=(d == 0), stop=(d == 1))
                mm.then_inc(yprod, 1)

        @block.scalar
        def _(act):
            for u in range(NU):
                h, d = divmod(u, 2)
                act.wait_ge(bcast, u + 1)
                if h >= 2:
                    act.wait_ge(yprod, h - 1)
                for t in range(NT):
                    e = act.activation(v["decay"][:, h % 2, d, t * P:(t + 1) * P], cum_ps(u)[:, t * P:(t + 1) * P],
                                       ACT.Exp, bias=v["nac"][:, t, 16 * d + h:16 * d + h + 1])
                e.then_inc(decayed, 1)

        @block.vector
        def _(dve):
            for g in range(2):
                dve.wait_ge(cb_done, g + 1)
                dve.tensor_copy(v["cb"][:, g, :], k.ps[:, 2 * g:2 * g + 2, :].rearrange("p a n -> p (a n)")[:, 0:TOK])\
                    .then_inc(cb_ok, 1)
            dve.wait_ge(cb_ok, 2)

            def take(h):
                dve.wait_ge(yprod, h + 1)
                dve.scalar_tensor_tensor(out=y4[:, :, h, :], in0=xs4[:, :, h, :], scalar=v["bc"][:, 64 + h:65 + h],
                                         in1=k.ps[:, 4 + h % 2, 0:NT * HD].rearrange("p (t n) -> p t n", t=NT),
                                         op0=ALU.mult, op1=ALU.add).then_inc(y_ok, 1)

            for h in range(HEADS):
                for d in range(2):
                    if h >= 2:
                        dve.wait_ge(yprod, h - 1)
                    dt_b = v["dt"][:, :, 16 * d + h:16 * d + h + 1].to_broadcast([P, NT, HD])
                    dve.tensor_tensor(v["xd"][:, h % 2, d, :, :], xs4[:, :, h, :], dt_b, ALU.mult).then_inc(xd_ok, 1)
                    dve.wait_ge(decayed, 2 * h + d + 1)
                    m = v["decay"][:, h % 2, d, :]
                    dve.tensor_tensor(m, m, v["cb"][:, h // 8, :], ALU.mult).then_inc(scaled, 1)
                if h >= 1:
                    take(h - 1)
            take(HEADS - 1)


def ssd_states_stage(k, v):
    nc = k.nc
    weighted, off_prod, st_prod = k.sem("x_weighted"), k.sem("yoff_prod"), k.sem("state_prod")
    state_ok, y_ok, chain = k.sem("state_ready"), k.sem("yoff_taken"), k.sem("state_chain")
    raw, S, xw, yo = v["raw"], v["state"], v["xw"], v["yo"]
    order = [[LT, LT + 1] + list(range(LT)), [LT + 1, LT] + list(range(LT))[::-1]]
    steps = [(i, d) for i in range(NT) for d in range(2)]

    def heads(ap):
        return ap.rearrange("p (h n) -> p h n", n=HD)

    def per_head(coef, t, d):
        return coef[:, t, 16 * d:16 * d + 16].unsqueeze(2).to_broadcast([P, HEADS, HD])

    def off_ps(d):
        return k.ps[:, 4 * d:4 * d + 2, :].rearrange("p a n -> p (a n)")

    def st_ps(d):
        return k.ps[:, 4 * d + 2:4 * d + 4, :].rearrange("p a n -> p (a n)")

    with k.stage() as block:

        @block.tensor
        def _(pe):
            for n, (i, d) in enumerate(steps):
                t = order[d][i]
                c = slice(latent_col(t), latent_col(t) + P)
                if i > 0:
                    pe.wait_ge(state_ok, n - 1)
                    for g in range(2):
                        mm = pe.matmul(k.ps[:, 4 * d + g, :], raw[:, 10 + g, c], S[:, d, g * 512:(g + 1) * 512],
                                       start=True, stop=True)
                    mm.then_inc(off_prod, 1)
                if i < NT - 1:
                    pe.wait_ge(weighted, n + 1)
                    for g in range(2):
                        mm = pe.matmul(k.ps[:, 4 * d + 2 + g, :], v["btok"][:, t, g * P:(g + 1) * P],
                                       xw[:, d, g * 512:(g + 1) * 512], start=True, stop=True)
                    mm.then_inc(st_prod, 1)

        @block.gpsimd
        def _(pool):
            for n, (i, d) in enumerate(steps):
                t = order[d][i]
                if i < NT - 1:
                    if i > 0:
                        pool.wait_ge(st_prod, n - 1)
                    pool.tensor_tensor(heads(xw[:, d, :]), heads(v["xs"][:, t, :]), per_head(v["wst"], t, d),
                                       ALU.mult).then_inc(weighted, 1)

        @block.vector
        def _(dve):
            link = Chain(dve, chain)
            for n, (i, d) in enumerate(steps):
                t = order[d][i]
                if i > 0:
                    dve.wait_ge(off_prod, n - 1)
                    link(dve.tensor_tensor(heads(yo[:, d, :]), heads(off_ps(d)), per_head(v["eac"], t, d), ALU.mult))
                    link(dve.tensor_tensor(v["y"][:, t, :], v["y"][:, t, :], yo[:, d, :], ALU.add))
                if i < NT - 1:
                    dve.wait_ge(st_prod, n + 1)
                    if i == 0:
                        dve.tensor_copy(S[:, d, :], st_ps(d)).then_inc(state_ok, 1)
                    else:
                        link(dve.tensor_tensor(heads(S[:, d, :]), heads(S[:, d, :]), per_head(v["etot"], t, d),
                                               ALU.mult))
                        dve.tensor_tensor(S[:, d, :], S[:, d, :], st_ps(d), ALU.add).then_inc(state_ok, 1)


def split_stage(k, plain, parts, prefetch):
    hi_ok = k.sem("split_high")
    with k.stage() as block:

        @block.sync
        def _(sp):
            prefetch(sp)

        @block.scalar
        def _(act):
            for kk in range(0, KD, 2):
                act.activation(parts[0][:, kk:kk + 2, :], plain[:, kk:kk + 2, :], ACT.Copy).then_inc(hi_ok, 1)

        @block.vector
        def _(dve):
            for kk in range(0, KD, 2):
                dve.wait_ge(hi_ok, kk // 2 + 1)
                dve.tensor_tensor(parts[1][:, kk:kk + 2, :], plain[:, kk:kk + 2, :],
                                  parts[0][:, kk:kk + 2, :].bitcast(F32), ALU.subtract)


def gate_projection(k, v, x):
    w = k.io["ab_w_in"][0]
    groups, dsts = [], []
    for c in range(2):
        token_major_group(x, pieces_of(w, O_Z + c * 512, 512, 2), 512, range(NT), groups, dsts,
                          lambda t, c=c: v["z"][:, t, c * 512:(c + 1) * 512], engine="s")
    return Product(k, "z", groups, rings(k, "z", k.work_at + 6144, 4, k.work_at + 12288, 4),
                   lambda which, eng, j, ps, link: eng.activation(dsts[j], ps, ACT.Silu))


def gate_stage(k, v):
    z = v["z"]
    nc = k.nc
    with k.stage() as block:

        @block.vector
        def _(dve):
            for t in range(0, NT, 2):
                dve.tensor_tensor(v["y"][:, t, :], v["y"][:, t, :], z[:, t, :], ALU.mult)

        @block.gpsimd
        def _(pool):
            for t in range(1, NT, 2):
                pool.tensor_tensor(v["y"][:, t, :], v["y"][:, t, :], z[:, t, :], ALU.mult)


def na_projection(k, n, x):
    w = k.io["ab_w_in"][0]
    groups, dsts = [], []
    for c in range(8):
        dst = n["qT"] if c < 4 else n["kT"]
        channel_major_group(x, pieces_of(w, O_Q + c * 256, 256, 4), 2, groups, dsts,
                            lambda ct, part, a, b, c=c, dst=dst: (dst[:, 2 * (c % 4) + ct, a:b], c < 4, c < 4 and part == 0))
    for c in range(2):
        token_major_group(x, pieces_of(w, O_V + c * 512, 512, 2), 512, range(NT), groups, dsts,
                          lambda t, c=c: (n["v"][:, t, c * 512:(c + 1) * 512], False, False))

    def evacuate(which, eng, j, ps, link):
        dst, is_q, latent_q = dsts[j]
        if latent_q:
            dst, ps = backwards(dst), ps.rearrange("p (u t) -> p u t", t=P)
        return copy_out(which, eng, dst, ps, HD ** -0.5 if is_q else None)

    return Product(k, "naqkv", groups, n["ring"], evacuate)


def backwards(ap):
    (ps, pn), (step, n) = ap.ap
    return bass.AP(ap.tensor, ap.offset + (P - 1) * step, [[ps, pn], [P * step, n // P], [-step, P]])


def attention_stage(k, name, qT, kT, vv, oT, n_ctx_units, bias, pt, pt_ctx, prefetch):
    nc = k.nc
    U = LT + n_ctx_units
    N = HEADS * U
    s_done, mx_done, exp_done, p_ok = k.sem(f"{name}_scores"), k.sem(f"{name}_max"), k.sem(f"{name}_exp"), k.sem(f"{name}_probs")
    turned, pt_ok = k.sem(f"{name}_probs_T"), k.sem(f"{name}_probs_T_copied")
    pv_done, o_ok, chain = k.sem(f"{name}_pv"), k.sem(f"{name}_o_taken"), k.sem(f"{name}_chain")
    chain_act = k.sem(f"{name}_chain_act")
    prob = k.misc[:, 0:3 * TOK].rearrange("p (s n) -> p s n", s=3)
    st = k.misc[:, 3 * TOK:3 * TOK + 18].rearrange("p (s a) -> p s a", s=3)
    bias_in = [k.sem(f"{name}_bias_in{s}") for s in range(2)]
    bias_ok = k.sem(f"{name}_bias_masked")
    groups = []
    for h in range(HEADS):
        groups.append((h, False, h * U + LT - 1))
        if n_ctx_units:
            groups.append((h, True, h * U + U - 1))

    def is_lat(n):
        return n % U < LT

    def scores_ps(n):
        pair = k.ps[:, 2 * (n % 2):2 * (n % 2) + 2, :].rearrange("p a n -> p (a n)")
        return pair[:, 0:TOK] if is_lat(n) else pair[:, N_LAT:TOK]

    def prob_of(n):
        return prob[:, n % 3, 0:TOK] if is_lat(n) else prob[:, n % 3, N_LAT:TOK]

    with k.stage() as block:

        @block.sync
        def _(sp):
            prefetch(sp)
            if bias is not None:
                for h in range(HEADS):
                    if h >= 2:
                        sp.wait_ge(mx_done, (h - 2) * U + LT)
                    for r in range(2):
                        base = k.rpb_flat[0:1, 64 + h * 15 * 31 + 31 * (1 - r) + 15 - (GRID - 1):]
                        src = bass.AP(base.tensor, base.offset, [[1, GRID], [31, 14], [1, GRID]])
                        sp.dma_start(bias["tile"][(1 - r) * GRID:(2 - r) * GRID, h % 2, :, :], src)\
                            .then_inc(bias_in[h % 2], 16)

        @block.tensor
        def _(pe):
            def scores(n):
                h, u = divmod(n, U)
                if n >= 2:
                    pe.wait_ge(exp_done, n - 1)
                if is_lat(n):
                    pe.matmul(k.ps[:, 2 * (n % 2), :], qT(h, u), kT(h, 0, N_LAT), start=True, stop=True)
                pe.matmul(k.ps[:, 2 * (n % 2) + 1, 0:N_CTX], qT(h, u), kT(h, N_LAT, TOK), start=True, stop=True)\
                    .then_inc(s_done, 1)

            def turn(n):
                pe.wait_ge(p_ok, n + 1)
                if n >= 1:
                    pe.wait_ge(pt_ok, n)
                keys = NT if is_lat(n) else CT
                for kt in range(keys):
                    tr = pe.transpose(k.ps[:, 4 + kt // 4, (kt % 4) * P:(kt % 4 + 1) * P],
                                      prob_of(n)[:, kt * P:(kt + 1) * P], k.ident)
                tr.then_inc(turned, 1)

            def values(i):
                h, is_ctx, last = groups[i]
                pe.wait_ge(pt_ok, last + 1)
                if i >= 2:
                    pe.wait_ge(o_ok, i - 1)
                keys = CT if is_ctx else NT
                for kt in range(keys):
                    src = pt_ctx[:, h % 2, kt, :] if is_ctx else pt[:, h % 2, kt, :]
                    mm = pe.matmul(k.ps[:, 6 + i % 2, 0:src.shape[1]], vv(h, kt + (LT if is_ctx else 0)), src,
                                   start=(kt == 0), stop=(kt == keys - 1))
                mm.then_inc(pv_done, 1)

            i = 0
            for n in range(N + 4):
                if n < N:
                    scores(n)
                while i < len(groups) and groups[i][2] <= n - 3:
                    values(i)
                    i += 1
                if 2 <= n < N + 2:
                    turn(n - 2)

        @block.scalar
        def _(act):
            for n in range(N + 2):
                if n < N:
                    act.wait_ge(mx_done, n + 1)
                    s = st[:, n % 3, :]
                    if is_lat(n) and bias is not None:
                        act.activation(prob_of(n)[:, 0:N_LAT], prob_of(n)[:, 0:N_LAT], ACT.Exp, bias=s[:, 1:2],
                                       accum_out=s[:, 2:3]).then_inc(chain_act, 1)
                        act.activation(prob_of(n)[:, N_LAT:TOK], scores_ps(n)[:, N_LAT:TOK], ACT.Exp, bias=s[:, 1:2],
                                       accum_out=s[:, 3:4]).then_inc(exp_done, 1)
                    else:
                        act.activation(prob_of(n), scores_ps(n), ACT.Exp, bias=s[:, 1:2],
                                       accum_out=s[:, 2:3]).then_inc(exp_done, 1)
                if n >= 2:
                    m = n - 2
                    h, u = divmod(m, U)
                    act.wait_ge(turned, m + 1)
                    if h >= 2:
                        per = len(groups) // HEADS
                        act.wait_ge(pv_done, per * (h - 2) + (1 if u < LT else per))
                    if is_lat(m):
                        dst = pt[:, h % 2, :, u * P:(u + 1) * P]
                        src = k.ps[:, 4:6, :].rearrange("p a (b n) -> p (a b) n", n=P)[:, 0:NT, :]
                    else:
                        dst = pt_ctx[:, h % 2, :, (u - LT) * P:(u - LT + 1) * P]
                        src = k.ps[:, 4, 0:CT * P].rearrange("p (b n) -> p b n", n=P)
                    act.activation(dst, src, ACT.Copy).then_inc(pt_ok, 1)

        @block.vector
        def _(dve):
            link = Chain(dve, chain)

            def maximum(n):
                h, u = divmod(n, U)
                s = st[:, n % 3, :]
                if u == 0 and bias is not None:
                    dve.wait_ge(bias_in[h % 2], 32 * (h // 2 + 1))
                    tile = bias["tile"][:, h % 2, :, :]
                    mask = bias["mask"].unsqueeze(1).to_broadcast([P, 14, GRID])
                    dve.tensor_tensor(tile, tile, mask, ALU.add).then_inc(bias_ok, 1)
                    dve.wait_ge(bias_ok, h + 1)
                dve.wait_ge(s_done, n + 1)
                if n >= 3:
                    dve.wait_ge(turned, n - 2)
                if is_lat(n) and bias is not None:
                    link(dve.tensor_reduce(s[:, 0:1], scores_ps(n)[:, N_LAT:TOK], AX.X, ALU.max))
                    b = bias["tile"][:, h % 2, 6 - 2 * u:14 - 2 * u, :].rearrange("p r c -> p (r c)")
                    link(dve.tensor_tensor_reduce(prob_of(n)[:, 0:N_LAT], scores_ps(n)[:, 0:N_LAT], b, 1.0,
                                                  s[:, 0:1], ALU.add, ALU.max, s[:, 4:5]))
                    dve.tensor_scalar(s[:, 1:2], s[:, 4:5], -1.0, None, ALU.mult).then_inc(mx_done, 1)
                else:
                    dve.tensor_reduce(s[:, 1:2], scores_ps(n), AX.X, ALU.max, negate=True).then_inc(mx_done, 1)

            def normalise(n):
                s = st[:, n % 3, :]
                dve.wait_ge(exp_done, n + 1)
                if is_lat(n) and bias is not None:
                    dve.wait_ge(chain_act, (n // U) * LT + n % U + 1)
                    link(dve.tensor_tensor(s[:, 2:3], s[:, 2:3], s[:, 3:4], ALU.add))
                link(dve.reciprocal(s[:, 5:6], s[:, 2:3]))
                dve.tensor_scalar(prob_of(n), prob_of(n), s[:, 5:6], None, ALU.mult).then_inc(p_ok, 1)

            def take(i):
                h, is_ctx, _ = groups[i]
                a, b = (N_LAT, N_LAT + N_CTX) if is_ctx else (0, N_LAT)
                r = (h % 2) * HD
                dve.wait_ge(pv_done, i + 1)
                src = k.ps[r:r + HD, 6 + i % 2, 0:b - a]
                if bias is not None and not is_ctx:
                    src = backwards(src)
                src = src if len(src.shape) == 3 else src.rearrange("p (u t) -> p u t", t=P)
                hi, lo = [x[r:r + HD, h // 2, a:b].rearrange("p (u t) -> p u t", t=P) for x in oT]
                link(dve.tensor_copy(hi, src))
                dve.tensor_tensor(lo, src, hi.bitcast(F32), ALU.subtract).then_inc(o_ok, 1)

            i = 0
            for n in range(N + 5):
                if n < N:
                    maximum(n)
                if 1 <= n <= N:
                    normalise(n - 1)
                while i < len(groups) and groups[i][2] <= n - 4:
                    take(i)
                    i += 1


def output_projection(k, name, w, x, tiles, layer, split_at, n_split, work):
    conds = 2 if len(tiles) > LT else 1
    gate = work[:, 0:2 * D].rearrange("p (c d) -> p c d", c=2)
    tmp = work[:, 2 * D:2 * D + 1024].rearrange("p (s n) -> p s n", s=2)
    groups, where = [], []
    for n in range(2):
        token_major_group(x, pieces_of(w, n * 512, 512, 2), 512, tiles, groups, where, lambda t, n=n: (t, n), engine="v")

    def load_gates(sp, sem):
        for cond in range(conds):
            sp.dma_start(gate[:, cond, :], k.mod_row(cond, layer, 2)).then_inc(sem, 16)
    load_gates.count = 16 * conds

    def evacuate(which, eng, j, ps, link):
        t, n = where[j]
        cols = slice(n * 512, (n + 1) * 512)
        link(eng.tensor_tensor(tmp[:, j % 2, :], ps, gate[:, 0 if t < LT else 1, cols], ALU.mult))
        return eng.tensor_tensor(k.h[:, t, cols], k.h[:, t, cols], tmp[:, j % 2, :], ALU.add)

    return Product(k, name, groups, rings(k, name, k.misc_at + 2560, 2, split_at, n_split), evacuate, load_gates)


def router_stage(k, T, r):
    nc, io = k.nc, k.io
    rw_in, rb_in = k.sem("router_w_in"), k.sem("router_b_in")
    logit, sig, chain = k.sem("logits"), k.sem("sigmoid"), k.sem("route_chain")
    mask_ok, ranked, dest_ok = k.sem("choice_mask"), k.sem("ranks"), k.sem("slots_known")
    fill_ok, filled, put, idx_in = k.sem("fill_made"), k.sem("table_filled"), k.sem("slots_put"), k.sem("slots_in")
    at = 0

    def part(*shape):
        nonlocal at
        n = 1
        for x in shape:
            n *= x
        at += n
        ap = k.rw[:, at - n:at]
        if len(shape) == 2:
            return ap.rearrange("p (a b) -> p a b", a=shape[0])
        if len(shape) == 3:
            return ap.rearrange("p (a b c) -> p a b c", a=shape[0], b=shape[1])
        return ap

    rw = part(KD, NE)
    rb = part(NE)
    s, sb, prod = part(T, NE), part(T, NE), part(T, NE)
    hi1, hi2, lo1, lo2, gs, gval = [part(T, NG) for _ in range(6)]
    gbest, vmin_g, best, vm1, vm2, wsum = [part(T) for _ in range(6)]
    s_in, b_in, oh1, oh2, val, pr4 = [part(T, EPG) for _ in range(6)]
    e_of = [part(T), part(T)]
    OH = [part(T, NE), part(T, NE)]
    M = part(T, NE)
    rank = [part(T), part(T)]
    dest = part(T, 2).bitcast(I32)
    entry = part(T, 2, 2).bitcast(I32)
    fill = part(NE * CAP // P, 2).bitcast(I32)
    cmax = part(1)
    iota = k.const[:, C_IOTA:C_IOTA + NE]
    tokid = k.const[:, C_TOKID:C_TOKID + T]

    def b2(ap, n):
        return ap.unsqueeze(2).to_broadcast([P, ap.shape[1], n])

    with k.stage() as block:

        @block.sync
        def _(sp):
            sp.dma_start(rw, io["router_w"].rearrange("(k p) e -> p k e", p=P)).then_inc(rw_in, 16)
            sp.dma_start(rb, io["router_bias"].rearrange("(a e) -> a e", a=1).to_broadcast([P, NE])).then_inc(rb_in, 16)
            sp.wait_ge(fill_ok, 1)
            sp.dma_start(k.slots.rearrange("(p n) w -> p n w", p=P), fill).then_inc(filled, 16)
            sp.wait_ge(put, 2 * T * 16)
            sp.dma_start(r["idxs"], k.slots.rearrange("(e c) w -> c e w", c=CAP)[0:P]).then_inc(idx_in, 16)
            sp.wait_ge(idx_in, 16)

        @block.gpsimd
        def _(pool):
            pool.memset(fill, 4 * TOK).then_inc(fill_ok, 1)
            pool.wait_ge(dest_ok, 2)
            pool.wait_ge(filled, 16)
            for t in range(T):
                for c in range(2):
                    pool.indirect_dma_start(
                        out=k.slots, out_offset=bass.IndirectOffsetOnAxis(ap=dest[:, t, c:c + 1], axis=0),
                        in_=entry[:, t, c, :], in_offset=None).then_inc(put, 16)

        @block.tensor
        def _(pe):
            pe.wait_ge(rw_in, 16)
            for t in range(T):
                for kk in range(KD):
                    mm = pe.matmul(k.ps[:, 7, t * NE:(t + 1) * NE], k.xT[:, kk, t * P:(t + 1) * P], rw[:, kk, :],
                                   start=(kk == 0), stop=(kk == KD - 1))
            mm.then_inc(logit, 1)
            pe.wait_ge(mask_ok, 1)
            for t in range(T):
                for u in range(t + 1):
                    stat = k.const[:, C_TRIS:C_TRIS + P] if u == t else k.ones
                    pe.matmul(k.ps[:, 6, t * NE:(t + 1) * NE], stat, M[:, u, :], start=(u == 0), stop=(u == t))
            for u in range(T):
                mm = pe.matmul(k.ps[:, 5, 0:NE], k.ones, M[:, u, :], start=(u == 0), stop=(u == T - 1))
            mm.then_inc(ranked, 1)

        @block.scalar
        def _(act):
            act.wait_ge(logit, 1)
            act.activation(s, k.ps[:, 7, 0:T * NE].rearrange("p (t e) -> p t e", t=T), ACT.Sigmoid).then_inc(sig, 1)

        @block.vector
        def _(dve):
            link = Chain(dve, chain)
            tt, ts = dve.tensor_tensor, dve.tensor_scalar
            dve.wait_ge(rb_in, 16)
            dve.wait_ge(sig, 1)
            link(tt(sb, s, rb.unsqueeze(1).to_broadcast([P, T, NE]), ALU.add))
            four = sb.rearrange("p t (g j) -> p t g j", j=EPG)
            link(tt(hi1, four[:, :, :, 0], four[:, :, :, 1], ALU.max))
            link(tt(lo1, four[:, :, :, 0], four[:, :, :, 1], ALU.min))
            link(tt(hi2, four[:, :, :, 2], four[:, :, :, 3], ALU.max))
            link(tt(lo2, four[:, :, :, 2], four[:, :, :, 3], ALU.min))
            link(tt(gs, hi1, hi2, ALU.max))
            link(tt(hi1, hi1, hi2, ALU.min))
            link(tt(lo1, lo1, lo2, ALU.max))
            link(tt(hi1, hi1, lo1, ALU.max))
            link(tt(gs, gs, hi1, ALU.add))

            def first_best(values, n, top, val_, vmin, onehot):
                link(dve.tensor_reduce(top, values, AX.X, ALU.max))
                link(tt(val_, values, b2(top, n), ALU.is_equal))
                link(ts(val_, val_, -99.0, None, ALU.mult))
                link(tt(val_, val_, iota[:, 0:n].unsqueeze(1).to_broadcast([P, T, n]), ALU.add))
                link(dve.tensor_reduce(vmin, val_, AX.X, ALU.min))
                link(tt(onehot, val_, b2(vmin, n), ALU.is_equal))

            first_best(gs, NG, gbest, gval, vmin_g, hi2)
            for dst, src in ((b_in, sb), (s_in, s)):
                link(tt(prod.rearrange("p t (g j) -> p t g j", j=EPG), src.rearrange("p t (g j) -> p t g j", j=EPG),
                        hi2.unsqueeze(3).to_broadcast([P, T, NG, EPG]), ALU.mult))
                link(dve.tensor_reduce(dst, prod.rearrange("p t (g j) -> p t j g", j=EPG), AX.X, ALU.add))
            first_best(b_in, EPG, best, val, vm1, oh1)
            link(ts(pr4, oh1, NEG, None, ALU.mult))
            link(tt(b_in, b_in, pr4, ALU.add))
            first_best(b_in, EPG, best, val, vm2, oh2)
            for c, (oh, vm) in enumerate(((oh1, vm1), (oh2, vm2))):
                link(tt(pr4, oh, s_in, ALU.mult))
                link(dve.tensor_reduce(r["wts"][:, c, 0:T], pr4, AX.X, ALU.add))
                link(ts(e_of[c], vmin_g, float(EPG), 99.0 * (EPG + 1), ALU.mult, ALU.add))
                link(tt(e_of[c], e_of[c], vm, ALU.add))
                link(tt(OH[c], b2(e_of[c], NE), iota.unsqueeze(1).to_broadcast([P, T, NE]), ALU.is_equal))
            dve.tensor_tensor(M, OH[0], OH[1], ALU.add).then_inc(mask_ok, 1)
            link(tt(wsum, r["wts"][:, 0, 0:T], r["wts"][:, 1, 0:T], ALU.add))
            link(dve.reciprocal(wsum, wsum))
            for c in range(2):
                link(tt(r["wts"][:, c, 0:T], r["wts"][:, c, 0:T], wsum, ALU.mult))
                link(dve.tensor_copy(entry[:, :, c, 0], tokid))
                link(ts(entry[:, :, c, 1], tokid, float(c * T * P), None, ALU.add))
            dve.wait_ge(ranked, 1)
            for c in range(2):
                link(tt(prod, OH[c], k.ps[:, 6, 0:T * NE].rearrange("p (t e) -> p t e", t=T), ALU.mult))
                link(dve.tensor_reduce(rank[c], prod, AX.X, ALU.add))
                link(ts(e_of[c], e_of[c], float(CAP), None, ALU.mult))
                dve.tensor_tensor(dest[:, :, c], e_of[c], rank[c], ALU.add).then_inc(dest_ok, 1)
            link(dve.tensor_reduce(cmax, k.ps[:, 5, 0:NE], AX.X, ALU.max))
            link(ts(r["more"], cmax, float(BLK) + 0.5, None, ALU.is_gt))


def moe_views(k):
    r = {}
    W = KD * DE
    raw = k.overlay("expert_raw", k.results_at, 3 * W)
    parts = k.overlay("expert_parts", k.big_at, 6 * W, F32R)
    rows = k.overlay("expert_rows", k.big_at + 6 * W, 2 * D)

    def tiles(ap, at, kk, n):
        return ap[:, at:at + kk * n].rearrange("p (k n) -> p k n", k=kk)

    for i, (nm, kk) in enumerate((("wg", KD), ("wu", KD), ("wd", DE // P))):
        r[nm] = tiles(raw, i * W, kk, W // kk)
        r[nm + "_hi"], r[nm + "_lo"] = [tiles(parts, (2 * i + j) * W, kk, W // kk) for j in range(2)]
    r["xb"], r["yo"] = rows[:, 0:D], rows[:, D:2 * D]
    r["hid"] = k.negb[:, 0:DE]
    m = k.misc
    r["idx"] = [m[:, 2 * s:2 * s + 2].bitcast(I32) for s in range(2)]
    r["more"] = m[:, 4:5].bitcast(I32)
    r["wts"] = m[:, 8:8 + 2 * NT].rearrange("p (c t) -> p c t", c=2)
    r["idxs"] = m[:, 32:32 + 2 * NE].bitcast(I32).rearrange("p (e w) -> p e w", w=2)
    turned = k.overlay("expert_rows_T", k.misc_at + 32 + 2 * NE, 4 * D, F32R)
    r["xT"] = [[tiles(turned, (2 * s + j) * D, KD, P) for j in range(2)] for s in range(2)]
    hidden = k.overlay("expert_hidden_T", k.big_at + 6 * W + 2 * D, 2 * DE, F32R)
    r["hT"] = [tiles(hidden, j * DE, DE // P, P) for j in range(2)]
    plain = k.overlay("more_rows_T", k.big_at, D + 2 * DE)
    r["more_xT"], r["more_hT"], r["more_sg"] = tiles(plain, 0, KD, P), tiles(plain, D, DE // P, P), plain[:, D + DE:]
    r["w_in"] = {n: [k.nc.alloc_semaphore(f"{n}{p}_in_{k.n_sems}") for p in range(2)] for n in KINDS}
    r["gate"] = k.xt_r[:, 4 * D:6 * D].rearrange("p (c d) -> p c d", c=2)
    return r


KINDS = ("wg", "wu", "wd")


def load_piece(k, layer, r, eng, n, p, e):
    src = k.io[{"wg": "moe_w_gate", "wu": "moe_w_up", "wd": "moe_w_down"}[n]]
    w = (src[layer, bass.ds(e, 1)] if not isinstance(e, int) else src[layer, e:e + 1])
    half = r[n].shape[1] // 2
    eng.dma_start(r[n][:, p * half:(p + 1) * half, :],
                  w.rearrange("a (k p) n -> p (a k) n", p=P)[:, p * half:(p + 1) * half, :]).then_inc(r["w_in"][n][p], 16)


THREE = ((0, 0), (0, 1), (1, 0))


def split_products(pe, out, stat, move, first=True, last=True):
    for i, (a, b) in enumerate(THREE):
        mm = pe.matmul(out, stat[a], move[b], start=(first and i == 0), stop=(last and i == 2))
    return mm


def expert_loop(eng):
    for e in (0, 1):
        yield 0, e, e
    with eng.Fori(1, NE // 2 - 1) as i:
        yield i, 0, 2 * i
        yield i, 1, 2 * i + 1
    for e in (NE - 2, NE - 1):
        yield NE // 2 - 1, e % 2, e


def wait_from(eng, sem, n):
    if not isinstance(n, int) or n > 0:
        eng.wait_ge(sem, n)


def wait_alone(k, eng, sem, n):
    wait_from(eng, sem, n)
    if not isinstance(n, int):
        eng.sem_inc(k.passed, 1)


def gather_rows(k, pool, dst, idx):
    return pool.indirect_dma_start(out=dst, out_offset=None, in_=k.rows,
                                   in_offset=bass.IndirectOffsetOnAxis(ap=idx[:, 0:1], axis=0),
                                   bounds_check=TOK - 1, oob_is_err=False)


def scatter_rows(k, pool, T, src, idx):
    return pool.indirect_dma_start(out=k.pairs, out_offset=bass.IndirectOffsetOnAxis(ap=idx[:, 1:2], axis=0),
                                   in_=src, in_offset=None, bounds_check=2 * T * P - 1, oob_is_err=False)


def experts_stage(k, layer, T, r):
    nc = k.nc
    hi_ok = {n: k.sem(f"{n}_high") for n in KINDS}
    lo_ok = {n: k.sem(f"{n}_low") for n in KINDS}
    used = {n: k.sem(f"{n}_prod") for n in KINDS}
    x_in, y_out, cleared = k.sem("rows_in"), k.sem("pair_rows_out"), k.sem("rows_cleared")
    x_turned, xhi_ok, xT_ok, silu_ok, hid_ok = (k.sem("rows_T"), k.sem("rows_T_high"), k.sem("rows_T_low"),
                                                k.sem("gate_silu"), k.sem("hidden"))
    h_turned, hhi_ok, hT_ok, y_ok, idx_ok = (k.sem("hidden_T"), k.sem("hidden_T_high"), k.sem("hidden_T_low"),
                                             k.sem("y_copied"), k.sem("idx_staged"))

    def is_last(e, ahead=0):
        return isinstance(e, int) and e + ahead >= NE - 1

    def piece(ap, p):
        half = ap.shape[1] // 2
        return ap[:, p * half:(p + 1) * half]

    x_ps = k.ps[:, 4:6, :].rearrange("p a (b t) -> p (a b) t", t=P)
    h_ps = k.ps[:, 6, :].rearrange("p (b t) -> p b t", t=P)

    with k.stage() as block:
        k.stage_sems += [s for n in KINDS for s in r["w_in"][n]]

        @block.sync
        def _(sp):
            def load(n, p, e):
                sp.wait_ge(lo_ok[n], 2 * e - 1 + p)
                load_piece(k, layer, r, sp, n, p, e)

            for p in range(2):
                load("wg", p, 1)
            for i, s, e in expert_loop(sp):
                if not is_last(e):
                    for p in range(2):
                        load("wu", p, e + 1)
                    if not is_last(e, 1):
                        for p in range(2):
                            load("wg", p, e + 2)
                    for p in range(2):
                        load("wd", p, e + 1)

        @block.gpsimd
        def _(pool):
            def stage_index(slot, count, e):
                at = r["idxs"][:, e, :] if isinstance(e, int) else r["idxs"][:, bass.ds(e, 1), :].rearrange("p a w -> p (a w)")
                pool.tensor_copy(r["idx"][slot], at).then_inc(idx_ok, 1)
                wait_alone(k, pool, idx_ok, count)

            def fetch(e):
                wait_alone(k, pool, x_in, 16 * e)
                stage_index(0, e + 1 if isinstance(e, int) and e < 2 else 2 * e - 1, e)
                wait_alone(k, pool, x_turned, e)
                gather_rows(k, pool, r["xb"], r["idx"][0]).then_inc(x_in, 16)

            pool.memset(r["xb"], 0.0).then_inc(cleared, 1)
            pool.wait_ge(cleared, 1)
            fetch(0)
            fetch(1)
            for i, s, e in expert_loop(pool):
                if not is_last(e, 1):
                    fetch(e + 2)
                wait_alone(k, pool, y_out, 16 * e)
                stage_index(1, NE + e + 1 if is_last(e, 1) else 2 * e + 4, e)
                wait_alone(k, pool, y_ok, e + 1)
                scatter_rows(k, pool, T, r["yo"], r["idx"][1]).then_inc(y_out, 16)
            pool.wait_ge(y_out, 16 * NE)

        @block.tensor
        def _(pe):
            def turn_rows(e):
                pe.wait_ge(x_in, 16 * e + 16)
                wait_from(pe, xT_ok, e)
                for kk in range(KD):
                    tr = pe.transpose(k.ps[:, 4 + kk // 4, (kk % 4) * P:(kk % 4 + 1) * P],
                                      r["xb"][:, kk * P:(kk + 1) * P], k.ident)
                tr.then_inc(x_turned, 1)

            def gate_up(n, p, s, e):
                pe.wait_ge(lo_ok[n], 2 * e + 1 + p)
                for kk in range(p * KD // 2, (p + 1) * KD // 2):
                    mm = split_products(pe, k.ps[:, 0 if n == "wg" else 1, :], [x[:, kk, :] for x in r["xT"][s]],
                                        (r[n + "_hi"][:, kk, :], r[n + "_lo"][:, kk, :]), kk == 0, kk == KD - 1)
                mm.then_inc(used[n], 1)

            turn_rows(0)
            pe.wait_ge(xT_ok, 1)
            for p in range(2):
                gate_up("wg", p, 0, 0)
            turn_rows(1)
            for i, s, e in expert_loop(pe):
                wait_from(pe, hid_ok, e)
                for p in range(2):
                    gate_up("wu", p, s, e)
                if not is_last(e):
                    pe.wait_ge(silu_ok, e + 1)
                    pe.wait_ge(xT_ok, e + 2)
                    gate_up("wg", 0, 1 - s, e + 1)
                pe.wait_ge(hid_ok, e + 1)
                for kk in range(DE // P):
                    tr = pe.transpose(k.ps[:, 6, kk * P:(kk + 1) * P], r["hid"][:, kk * P:(kk + 1) * P], k.ident)
                tr.then_inc(h_turned, 1)
                if not is_last(e):
                    gate_up("wg", 1, 1 - s, e + 1)
                if not is_last(e, 1):
                    turn_rows(e + 2)
                wait_from(pe, y_ok, e)
                pe.wait_ge(hT_ok, e + 1)
                for p in range(2):
                    pe.wait_ge(lo_ok["wd"], 2 * e + 1 + p)
                    for half in range(2):
                        c = slice(half * 512, (half + 1) * 512)
                        for kk in range(p * DE // P // 2, (p + 1) * DE // P // 2):
                            mm = split_products(pe, k.ps[:, 2 + half, :], [x[:, kk, :] for x in r["hT"]],
                                                (r["wd_hi"][:, kk, c], r["wd_lo"][:, kk, c]),
                                                kk == 0, kk == DE // P - 1)
                    mm.then_inc(used["wd"], 1)

        @block.scalar
        def _(act):
            def high(n, p, e):
                act.wait_ge(r["w_in"][n][p], 16 * (e + 1))
                wait_from(act, used[n], 2 * e - 1 + p)
                act.activation(piece(r[n + "_hi"], p), piece(r[n], p), ACT.Copy).then_inc(hi_ok[n], 1)

            def high_rows_T(s, e):
                act.wait_ge(x_turned, e + 1)
                act.activation(r["xT"][s][0], x_ps, ACT.Copy).then_inc(xhi_ok, 1)

            def copy_y(e):
                act.wait_ge(used["wd"], 2 * e + 2)
                wait_from(act, y_out, 16 * e)
                act.activation(r["yo"], k.ps[:, 2:4, :].rearrange("p a n -> p (a n)"), ACT.Copy).then_inc(y_ok, 1)

            def silu(e):
                act.wait_ge(used["wg"], 2 * e + 2)
                wait_from(act, h_turned, e)
                act.activation(r["hid"], k.ps[:, 0, :], ACT.Silu).then_inc(silu_ok, 1)

            high("wg", 0, 0)
            high_rows_T(0, 0)
            for n, p, e in (("wg", 1, 0), ("wu", 0, 0), ("wu", 1, 0)):
                high(n, p, e)
            high_rows_T(1, 1)
            high("wg", 0, 1)
            silu(0)
            high("wg", 1, 1)
            for i, s, e in expert_loop(act):
                for p in range(2):
                    high("wd", p, e)
                if not is_last(e):
                    high("wu", 0, e + 1)
                act.wait_ge(h_turned, e + 1)
                act.activation(r["hT"][0], h_ps, ACT.Copy).then_inc(hhi_ok, 1)
                if not is_last(e):
                    high("wu", 1, e + 1)
                    silu(e + 1)
                if not is_last(e, 1):
                    high_rows_T(s, e + 2)
                    for p in range(2):
                        high("wg", p, e + 2)
                copy_y(e)

        @block.vector
        def _(dve):
            def low(n, p, e):
                dve.wait_ge(hi_ok[n], 2 * e + 1 + p)
                dve.tensor_tensor(piece(r[n + "_lo"], p), piece(r[n], p), piece(r[n + "_hi"], p).bitcast(F32),
                                  ALU.subtract).then_inc(lo_ok[n], 1)

            def low_rows_T(s, e):
                dve.wait_ge(xhi_ok, e + 1)
                dve.tensor_tensor(r["xT"][s][1], x_ps, r["xT"][s][0].bitcast(F32), ALU.subtract).then_inc(xT_ok, 1)

            low("wg", 0, 0)
            low_rows_T(0, 0)
            for n, p, e in (("wg", 1, 0), ("wu", 0, 0), ("wu", 1, 0)):
                low(n, p, e)
            low_rows_T(1, 1)
            for p in range(2):
                low("wg", p, 1)
            for i, s, e in expert_loop(dve):
                for p in range(2):
                    low("wd", p, e)
                dve.wait_ge(silu_ok, e + 1)
                dve.wait_ge(used["wu"], 2 * e + 2)
                dve.tensor_tensor(r["hid"], r["hid"], k.ps[:, 1, :], ALU.mult).then_inc(hid_ok, 1)
                if not is_last(e):
                    low("wu", 0, e + 1)
                dve.wait_ge(hhi_ok, e + 1)
                dve.tensor_tensor(r["hT"][1], h_ps, r["hT"][0].bitcast(F32), ALU.subtract).then_inc(hT_ok, 1)
                if not is_last(e):
                    low("wu", 1, e + 1)
                if not is_last(e, 1):
                    low_rows_T(s, e + 2)
                    for p in range(2):
                        low("wg", p, e + 2)


def more_blocks_stage(k, layer, T, r):
    nc, io = k.nc, k.io
    w_in, idx_in, x_in, y_out = k.sem("more_w_in"), k.sem("more_idx_in"), k.sem("more_rows_in"), k.sem("more_pairs_out")
    gu_done, d_done, x_turned, xT_ok = k.sem("more_gu"), k.sem("more_down"), k.sem("more_rows_T"), k.sem("more_rows_T_copied")
    silu_ok, hid_ok, h_turned, hT_ok, y_ok = (k.sem("more_silu"), k.sem("more_hidden"), k.sem("more_hidden_T"),
                                              k.sem("more_hidden_T_copied"), k.sem("more_y"))
    J = T * P // BLK - 1
    wg, wu, wd, yo, hid, xb, idx = [r[n] for n in ("wg", "wu", "wd", "yo", "hid", "xb")] + [r["idx"][0]]
    xT, hT, sg = r["more_xT"], r["more_hT"], r["more_sg"]

    def blocks(eng):
        with eng.Fori(0, NE) as e:
            with eng.Fori(0, J) as j:
                yield e * J + j + 1

    with k.stage() as block:

        @block.sync
        def _(sp):
            more = sp.value_load(r["more"][0:1, 0:1], min_val=0, max_val=1)
            with sp.If(more > 0):
                with sp.Fori(0, NE) as e:
                    for dst, src in ((wg, io["moe_w_gate"]), (wu, io["moe_w_up"]), (wd, io["moe_w_down"])):
                        sp.dma_start(dst, src[layer, bass.ds(e, 1)].rearrange("a (k p) n -> p (a k) n", p=P))\
                            .then_inc(w_in, 16)
                    with sp.Fori(0, J) as j:
                        n = e * J + j + 1
                        sp.dma_start(idx, k.slots[bass.ds(e * CAP + j * BLK + BLK, P), :]).then_inc(idx_in, 16)
                        wait_alone(k, sp, y_out, 16 * n)

        @block.gpsimd
        def _(pool):
            more = pool.value_load(r["more"][0:1, 0:1], min_val=0, max_val=1)
            with pool.If(more > 0):
                for n in blocks(pool):
                    wait_alone(k, pool, idx_in, 16 * n)
                    gather_rows(k, pool, xb, idx).then_inc(x_in, 16)
                    wait_alone(k, pool, y_ok, n)
                    scatter_rows(k, pool, T, yo, idx).then_inc(y_out, 16)
                    wait_alone(k, pool, y_out, 16 * n)

        @block.tensor
        def _(pe):
            more = pe.value_load(r["more"][0:1, 0:1], min_val=0, max_val=1)
            with pe.If(more > 0):
                with pe.Fori(0, NE) as e:
                    wait_alone(k, pe, w_in, 48 * e + 48)
                    with pe.Fori(0, J) as j:
                        n = e * J + j + 1
                        pe.wait_ge(x_in, 16 * n)
                        for kk in range(KD):
                            tr = pe.transpose(k.ps[:, 4 + kk // 4, (kk % 4) * P:(kk % 4 + 1) * P],
                                              xb[:, kk * P:(kk + 1) * P], k.ident)
                        tr.then_inc(x_turned, 1)
                        pe.wait_ge(xT_ok, n)
                        for bank, w in ((0, wg), (1, wu)):
                            for kk in range(KD):
                                mm = pe.matmul(k.ps[:, bank, :], xT[:, kk, :], w[:, kk, :],
                                               start=(kk == 0), stop=(kk == KD - 1))
                        mm.then_inc(gu_done, 1)
                        pe.wait_ge(hid_ok, n)
                        for kk in range(DE // P):
                            tr = pe.transpose(k.ps[:, 6, kk * P:(kk + 1) * P], hid[:, kk * P:(kk + 1) * P], k.ident)
                        tr.then_inc(h_turned, 1)
                        pe.wait_ge(hT_ok, n)
                        for half in range(2):
                            for kk in range(DE // P):
                                mm = pe.matmul(k.ps[:, 2 + half, :], hT[:, kk, :],
                                               wd[:, kk, half * 512:(half + 1) * 512],
                                               start=(kk == 0), stop=(kk == DE // P - 1))
                        mm.then_inc(d_done, 1)
                        wait_alone(k, pe, y_ok, n)

        @block.scalar
        def _(act):
            more = act.value_load(r["more"][0:1, 0:1], min_val=0, max_val=1)
            with act.If(more > 0):
                for n in blocks(act):
                    act.wait_ge(x_turned, n)
                    act.activation(xT, k.ps[:, 4:6, :].rearrange("p a (b t) -> p (a b) t", t=P), ACT.Copy)\
                        .then_inc(xT_ok, 1)
                    act.wait_ge(gu_done, n)
                    act.activation(sg, k.ps[:, 0, :], ACT.Silu).then_inc(silu_ok, 1)
                    act.wait_ge(h_turned, n)
                    act.activation(hT, k.ps[:, 6, :].rearrange("p (b t) -> p b t", t=P), ACT.Copy).then_inc(hT_ok, 1)

        @block.vector
        def _(dve):
            more = dve.value_load(r["more"][0:1, 0:1], min_val=0, max_val=1)
            with dve.If(more > 0):
                for n in blocks(dve):
                    dve.wait_ge(silu_ok, n)
                    dve.tensor_tensor(hid, sg, k.ps[:, 1, :], ALU.mult).then_inc(hid_ok, 1)
                    dve.wait_ge(d_done, n)
                    dve.tensor_copy(yo, k.ps[:, 2:4, :].rearrange("p a n -> p (a n)")).then_inc(y_ok, 1)


def combine_stage(k, layer, T, r):
    nc = k.nc
    gate_in, chain = k.sem("moe_gate_in"), k.sem("combine_chain")
    y_in, weighted = [k.sem(f"pairs_in{t}") for t in range(T)], k.sem("first_weighted")
    buf = k.rw[:, 0:2 * T * D].rearrange("p (t c d) -> p t c d", t=T, c=2)
    conds = 2 if T > LT else 1
    with k.stage() as block:

        @block.sync
        def _(sp):
            for cond in range(conds):
                sp.dma_start(r["gate"][:, cond, :], k.mod_row(cond, layer, 5)).then_inc(gate_in, 16)
            for t in range(T):
                for c in range(2):
                    sp.dma_start(buf[:, t, c, :], k.pairs[(c * T + t) * P:(c * T + t + 1) * P, :])\
                        .then_inc(y_in[t], 16)

        @block.scalar
        def _(act):
            for t in range(T):
                act.wait_ge(y_in[t], 32)
                a = buf[:, t, 0, :]
                act.activation(a, a, ACT.Copy, scale=r["wts"][:, 0, t:t + 1]).then_inc(weighted, 1)

        @block.vector
        def _(dve):
            link = Chain(dve, chain)
            dve.wait_ge(gate_in, 16 * conds)
            for t in range(T):
                a, b = buf[:, t, 0, :], buf[:, t, 1, :]
                dve.wait_ge(y_in[t], 32)
                dve.wait_ge(weighted, t + 1)
                link(dve.scalar_tensor_tensor(out=a, in0=b, scalar=r["wts"][:, 1, t:t + 1], in1=a,
                                              op0=ALU.mult, op1=ALU.add))
                link(dve.tensor_tensor(a, a, r["gate"][:, 0 if t < LT else 1, :], ALU.mult))
                dve.tensor_tensor(k.h[:, t, :], k.h[:, t, :], a, ALU.add)


def moe(k, layer, T):
    r = moe_views(k)

    def first_expert(sp):
        for n in KINDS:
            for p in range(2):
                load_piece(k, layer, r, sp, n, p, 0)

    norm_stage(k, lambda t: k.h[:, t, :], range(T), k.io["norm2_g"][layer:layer + 1, :], (layer, 4, 3), k.xT,
               k.rw[:, 0:8 * D], rows_out=k.rows, prefetch=first_expert)
    router_stage(k, T, r)
    experts_stage(k, layer, T, r)
    more_blocks_stage(k, layer, T, r)
    combine_stage(k, layer, T, r)


def gqa_projection(k, g, x):
    w = k.io["gqa_w_in"][0]
    groups, dsts = [], []
    for c in range(2):
        token_major_group(x, pieces_of(w, c * 512, 512, 2), 512, range(LT), groups, dsts,
                          lambda t, c=c: g["q"][:, t, c * 512:(c + 1) * 512])
    token_major_group(x, pieces_of(w, 1024, 512, 2), 512, range(NT), groups, dsts, lambda t: g["kv"][:, t, :])
    return Product(k, "gqkv", groups, g["ring"], lambda which, eng, j, ps, link: copy_out(which, eng, dsts[j], ps))


def gqa_rope_stage(k, g):
    nc, io = k.nc, k.io
    KV = 4
    H2 = HD // 2
    g_in, tab, chain, sq, root = k.sem("qk_gain_in"), k.sem("rope_tables"), k.sem("rope_chain"), k.sem("qk_squared"), k.sem("qk_root")
    q_ok, k_ok, v_ok, turned, copied = k.sem("q_roped"), k.sem("k_roped"), k.sem("v_doubled"), k.sem("qk_T"), k.sem("qk_T_copied")
    q, kv = g["q"], g["kv"]
    qh = q.rearrange("p t (h n) -> p t h n", n=HD)
    kh = kv[:, :, 0:KV * HD].rearrange("p t (h n) -> p t h n", n=HD)
    gains = g["small"][:, 0:2 * HD].rearrange("p (a n) -> p a n", a=2)
    tables = g["small"][:, 128:128 + 8 * LT * H2].rearrange("p (a b t n) -> p a b t n", a=2, b=4, t=LT)
    at = 128 + 8 * LT * H2
    sq_q = g["small"][:, at:at + LT * HEADS].rearrange("p (t h) -> p t h", t=LT)
    sq_k = g["small"][:, at + 64:at + 64 + NT * KV].rearrange("p (t h) -> p t h", t=NT)
    tmp = g["tmp"]
    cos = k.const[:, C_COS:C_COS + LT * H2].rearrange("p (t n) -> p t n", t=LT)
    sin = k.const[:, C_SIN:C_SIN + LT * H2].rearrange("p (t n) -> p t n", t=LT)
    sq_buf = tmp[:, 0:LT * D].rearrange("p (t n) -> p t n", t=LT)
    sqk_buf = tmp[:, LT * D:LT * D + NT * KV * HD].rearrange("p (t n) -> p t n", t=NT)

    with k.stage() as block:

        @block.sync
        def _(sp):
            sp.dma_start(gains[:, 0, :], io["gqa_q_norm"].to_broadcast([P, HD])).then_inc(g_in, 16)
            sp.dma_start(gains[:, 1, :], io["gqa_k_norm"].to_broadcast([P, HD])).then_inc(g_in, 16)

        @block.scalar
        def _(act):
            act.activation(sq_buf, q, ACT.Square).then_inc(sq, 1)
            act.activation(sqk_buf, kv[:, :, 0:KV * HD], ACT.Square).then_inc(sq, 1)
            act.wait_ge(root, 2)
            act.activation(sq_q, sq_q, ACT.Sqrt, bias=k.eps, scale=1.0 / HD).then_inc(root, 1)
            act.activation(sq_k, sq_k, ACT.Sqrt, bias=k.eps, scale=1.0 / HD).then_inc(root, 1)
            for i in range(LT + NT):
                act.wait_ge(turned, i + 1)
                if i < NT:
                    act.activation(g["kT"][:, :, i * P:(i + 1) * P],
                                   k.ps[:, 2 * (i % 2), :].rearrange("p (b t) -> p b t", t=P), ACT.Copy)\
                        .then_inc(copied, 1)
                else:
                    t = i - NT
                    act.activation(g["qT"][:, :, t * P:(t + 1) * P],
                                   k.ps[:, 2 * (i % 2):2 * (i % 2) + 2, :].rearrange("p a (b t) -> p (a b) t", t=P),
                                   ACT.Copy).then_inc(copied, 1)

        @block.gpsimd
        def _(pool):
            vh = kv[:, :, KV * HD:2 * KV * HD].rearrange("p t (h n) -> p t h n", n=HD)
            for c in range(2):
                for t in range(NT):
                    op = pool.tensor_copy(g["vd"][:, t, :, c * HD:(c + 1) * HD], vh[:, t])
            op.then_inc(v_ok, 1)

        @block.vector
        def _(dve):
            link = Chain(dve, chain)
            tt = dve.tensor_tensor
            dve.wait_ge(g_in, 32)
            for a in range(2):
                g1 = gains[:, a, 0:H2].unsqueeze(1).to_broadcast([P, LT, H2])
                g2 = gains[:, a, H2:HD].unsqueeze(1).to_broadcast([P, LT, H2])
                for b, (gg, cs) in enumerate(((g1, cos), (g2, sin), (g1, sin), (g2, cos))):
                    link(tt(tables[:, a, b], cs, gg, ALU.mult))
            dve.wait_ge(sq, 2)
            dve.tensor_reduce(sq_q, sq_buf.rearrange("p t (h n) -> p t h n", n=HD), AX.X, ALU.add).then_inc(root, 1)
            dve.tensor_reduce(sq_k, sqk_buf.rearrange("p t (h n) -> p t h n", n=HD), AX.X, ALU.add).then_inc(root, 1)
            dve.wait_ge(root, 4)
            link(dve.reciprocal(sq_k, sq_k))
            link(dve.reciprocal(sq_q, sq_q))
            link(dve.tensor_scalar(sq_q, sq_q, HD ** -0.5, None, ALU.mult))
            for t in range(NT):
                link(tt(kh[:, t], kh[:, t], sq_k[:, t].unsqueeze(2).to_broadcast([P, KV, HD]), ALU.mult))

            def rope(x, out, heads, a, t):
                parts = [tmp[:, b * 512:b * 512 + heads * H2].rearrange("p (h n) -> p h n", h=heads) for b in range(4)]
                x1, x2 = x[:, :, 0:H2], x[:, :, H2:HD]
                for b, xx in enumerate((x1, x2, x1, x2)):
                    link(tt(parts[b], xx, tables[:, a, b, t].unsqueeze(1).to_broadcast([P, heads, H2]), ALU.mult))
                link(tt(out[:, :, 0:H2], parts[0], parts[1], ALU.subtract))
                return tt(out[:, :, H2:HD], parts[2], parts[3], ALU.add)

            for t in range(NT):
                if t < LT:
                    link(rope(kh[:, t], g["kd"][:, t, :, 0:HD], KV, 1, t))
                else:
                    gk = gains[:, 1, :].unsqueeze(1).to_broadcast([P, KV, HD])
                    link(tt(g["kd"][:, t, :, 0:HD], kh[:, t], gk, ALU.mult))
                dve.tensor_copy(g["kd"][:, t, :, HD:2 * HD], g["kd"][:, t, :, 0:HD]).then_inc(k_ok, 1)
            for t in range(LT):
                link(tt(qh[:, t], qh[:, t], sq_q[:, t].unsqueeze(2).to_broadcast([P, HEADS, HD]), ALU.mult))
                rope(qh[:, t], qh[:, t], HEADS, 0, t).then_inc(q_ok, 1)
                dve.wait_ge(q_ok, t + 1)

        @block.tensor
        def _(pe):
            for i in range(LT + NT):
                if i >= 2:
                    pe.wait_ge(copied, i - 1)
                if i < NT:
                    pe.wait_ge(k_ok, i + 1)
                    for c in range(KV):
                        tr = pe.transpose(k.ps[:, 2 * (i % 2), c * P:(c + 1) * P], g["kd"][:, i, c, :], k.ident)
                else:
                    t = i - NT
                    pe.wait_ge(q_ok, t + 1)
                    for c in range(KD):
                        tr = pe.transpose(k.ps[:, 2 * (i % 2) + c // 4, (c % 4) * P:(c % 4 + 1) * P],
                                          q[:, t, c * P:(c + 1) * P], k.ident)
                tr.then_inc(turned, 1)


def layer_even(k):
    W, R2, R3 = k.work_at, k.results_at, k.results_at + NT * D
    x = split_views(k, "xbc_x", R2, R3, TOK)
    v = ssd_views(k)
    xbc = ssd_projection(k, v, x)
    norm_stage(k, lambda t: k.h[:, t, :], range(NT), k.io["norm1_g"][0:1, :], (0, 1, 0), k.xT, k.rw[:, 0:8 * D],
               prefetch=xbc.early, split=x)
    xbc.run()
    conv_stage(k, v)
    ssd_diagonal_stage(k, v)
    ssd_states_stage(k, v)
    x = split_views(k, "x", R2, k.big_at, TOK)
    z = gate_projection(k, v, x)
    split_stage(k, k.xT, x, z.early)
    z.run()
    gate_stage(k, v)
    y = split_views(k, "ssd_y", W, W + NT * D, TOK)
    about = output_projection(k, "about_ssd", k.io["ab_w_out"][0, 0:D], y, range(NT), 0, W + 2 * NT * D, 3, k.r3)
    norm_stage(k, lambda t: v["y"][:, t, :], range(NT), k.io["ssm_norm_g"][0:1, :], None, None, k.rw[:, 12288:12288 + 8 * D],
               prefetch=about.early, split=y)
    n = {"qT": k.rw[:, 0:6144].rearrange("p (c t) -> p c t", c=KD),
         "kT": k.rw[:, 6144:12288].rearrange("p (c t) -> p c t", c=KD),
         "v": k.rw[:, 12288:18432].rearrange("p (t n) -> p t n", t=NT),
         "ring": rings(k, "naqkv", W + 18432, 3, R3, 3)}
    qkv = na_projection(k, n, x)
    about.run(qkv.early)
    qkv.run()
    oT = split_views(k, "na_o", R2, R3, TOK)
    bias = {"tile": k.rw[:, 18432:18432 + 2 * 14 * GRID].rearrange("p (s r c) -> p s r c", s=2, r=14),
            "mask": k.const[:, C_NAMASK:C_NAMASK + GRID]}
    pt = k.xt_r.rearrange("p (s k t) -> p s k t", s=2, k=NT)
    pt_ctx = k.rw[:, 20224:20224 + 4 * N_CTX].rearrange("p (s k t) -> p s k t", s=2, k=CT)

    def rows_of(ap, h, a, b):
        r = (h % 2) * HD
        return ap[r:r + HD, h // 2, a:b]

    about = output_projection(k, "about_na", k.io["ab_w_out"][0, D:2 * D], oT, range(NT), 0, W, 4, k.xt_r)
    attention_stage(k, "na", lambda h, u: rows_of(n["qT"], h, u * P, (u + 1) * P), lambda h, a, b: rows_of(n["kT"], h, a, b),
                    lambda h, kt: n["v"][:, kt, (h // 2) * P:(h // 2 + 1) * P], oT, CT, bias, pt, pt_ctx,
                    about.early)
    about.run()


def layer_odd(k):
    W = k.work_at
    x = split_views(k, "gqa_x", k.big_at, W, TOK)
    g = {"q": k.r2[:, 0:4096].rearrange("p (t n) -> p t n", t=LT),
         "kv": k.r3[:, 0:3072].rearrange("p (t n) -> p t n", t=NT),
         "ring": rings(k, "gqkv", W + 14336, 4, W + 6144, 4),
         "small": k.misc,
         "kd": k.rw[:, 0:3072].rearrange("p (t h n) -> p t h n", t=NT, h=4),
         "vd": k.rw[:, 3072:6144].rearrange("p (t h n) -> p t h n", t=NT, h=4),
         "qT": k.rw[:, 6144:10240].rearrange("p (c t) -> p c t", c=KD),
         "kT": k.rw[:, 10240:13312].rearrange("p (c t) -> p c t", c=4),
         "tmp": k.rw[:, 13312:21600]}
    qkv = gqa_projection(k, g, x)
    norm_stage(k, lambda t: k.h[:, t, :], range(NT), k.io["norm1_g"][1:2, :], (1, 1, 0), None, k.rw[:, 6144:6144 + 8 * D],
               prefetch=qkv.early, split=x)
    qkv.run()
    gqa_rope_stage(k, g)
    oT = split_views(k, "gqa_o", W + 13312, W + 17408, N_LAT)
    pt = k.xt_r.rearrange("p (s k t) -> p s k t", s=2, k=NT)

    def half(h):
        return slice((h % 2) * HD, (h % 2) * HD + HD)

    out = output_projection(k, "gqaout", k.io["gqa_w_out"][0], oT, range(LT), 1, W, 4, k.xt_r)
    attention_stage(k, "gqa", lambda h, u: g["qT"][half(h), h // 2, u * P:(u + 1) * P],
                    lambda h, a, b: g["kT"][half(h), h // 4, a:b], lambda h, kt: g["vd"][:, kt, h // 4, :],
                    oT, 0, None, pt, None, out.early)
    out.run()


def build(nc, io):
    with ExitStack() as ctx:
        k = Kernel(nc, ctx, io)
        load_stage(k)
        stream_in = nc.alloc_semaphore("stream_in")

        def load_stream(sp):
            sp.dma_start(k.h[:, 0:LT, :], io["x"][0].rearrange("(t p) d -> p t d", p=P)).then_inc(stream_in, 16)
            sp.dma_start(k.h[:, LT:NT, :], io["ctx"][0].rearrange("(t p) d -> p t d", p=P)).then_inc(stream_in, 16)
            sp.wait_ge(stream_in, 32)

        modulation_stage(k, load_stream)
        layer_even(k)
        moe(k, 0, NT)
        layer_odd(k)
        moe(k, 1, LT)
        norm_stage(k, lambda t: k.h[:, t, :], range(LT), io["final_g"].rearrange("(a n) -> a n", a=1), None, None,
                   k.rw[:, 0:8 * D], out=io["out"])


def shape_constants():
    import numpy as np
    c = np.zeros((P, C_END), np.float32)
    i, l = np.arange(P)[:, None], np.arange(P)[None, :]
    c[:, C_IDENT:C_IDENT + P] = i == l
    c[:, C_ONES:C_ONES + P] = 1
    c[:, C_TRIF:C_TRIF + P] = i <= l
    c[:, C_TRIB:C_TRIB + P] = i >= l
    c[:, C_TRIS:C_TRIS + P] = i < l
    c[:, C_NEGF:C_NEGF + P] = np.where(i <= l, 0, NEG)
    c[:, C_NEGB:C_NEGB + P] = np.where(i >= l, 0, NEG)
    q, kc = GRID - 1 - np.arange(P)[:, None] % GRID, np.arange(GRID)[None, :]
    start = np.clip(q - 8, 0, GRID - 16)
    c[:, C_NAMASK:C_NAMASK + GRID] = np.where((kc >= start) & (kc < start + 16), 0, NEG)
    c[:, C_TOKID:C_TOKID + NT] = np.arange(P)[:, None] + P * np.arange(NT)[None, :]
    c[:, C_IOTA:C_IOTA + NE] = np.arange(NE)
    c[:, C_EPS] = EPS
    t = np.arange(N_LAT)
    n_freq = HD // 4
    inv = np.float32(10000.0) ** (-np.arange(n_freq, dtype=np.float32) / n_freq)
    ang = np.concatenate([(t // GRID).astype(np.float32)[:, None] * inv, (t % GRID).astype(np.float32)[:, None] * inv], -1)
    for col, f in ((C_COS, np.cos), (C_SIN, np.sin)):
        tab = f(ang).astype(np.float32).reshape(LT, P, HD // 2).transpose(1, 0, 2)
        c[:, col:col + LT * HD // 2] = tab.reshape(P, -1)
    sel = np.zeros((SEL_ROWS, 16 * P), np.float32)
    for h in range(16):
        sel[[h, 32 + h], h * P:(h + 1) * P] = 1
    return c, sel


_INS = ["x", "c", "ctx", "c_ctx", "w_mod", "b_mod", "norm1_g", "norm2_g", "final_g", "ab_w_in", "ab_w_out",
        "ssm_conv_w", "ssm_conv_b", "ssm_A_log", "ssm_dt_bias", "ssm_D", "ssm_norm_g", "na_rpb", "gqa_w_in",
        "gqa_w_out", "gqa_q_norm", "gqa_k_norm", "router_w", "router_bias", "moe_w_gate", "moe_w_up", "moe_w_down"]


def kernel(**inputs):
    import numpy as _np
    import concourse.bacc as _bacc
    from concourse import mybir as _mybir
    from concourse.bass_utils import run_bass_kernel_spmd as _run

    nc = _bacc.Bacc("TRN2", target_bir_lowering=False, num_devices=1)
    arrays, io = {}, {}
    const, sel = shape_constants()
    for name, a in [(n, inputs[n]) for n in _INS] + [("const", const), ("sel", sel)]:
        a = _np.ascontiguousarray(a)
        arrays[f"in_{name}_dram"] = a
        io[name] = nc.dram_tensor(f"in_{name}_dram", a.shape, _mybir.dt.from_np(a.dtype), kind="ExternalInput").ap()
    out = nc.dram_tensor("out_dram", (N_LAT, D), _mybir.dt.float32, kind="ExternalOutput").ap()
    io["out"] = out
    build(nc, io)
    r = _run(nc, [arrays], core_ids=[0])
    return r.results[0]["out_dram"].reshape(1, N_LAT, D)
```
